# Optimizing a Trainium2 kernel written in Bass

```python
import jax, jax.numpy as jnp
from jax import lax
import numpy as np

D_MODEL = 1024
BATCH = 1
SEQ = 1024
DEPTH = 1

N_META = 16
BLOCK = 128
META_PAD = BLOCK - N_META
CONV_CH = 256
CONV_K = 31
POOL_CH = 256
POOL_WINDOWS = (2, 4, 8, 16)
POOL_GROUPS = 4
POOL_GC = POOL_CH // POOL_GROUPS
POOL_OUT = D_MODEL // POOL_GROUPS
ATT_HEADS = 4
HEAD_DIM = 128
ATT_W = ATT_HEADS * HEAD_DIM
N_BRANCH = 3
D_IN = 2 * CONV_CH + POOL_CH + 3 * ATT_W + N_BRANCH * D_MODEL
D_FF = 3 * D_MODEL
FFN_K = 3
EPS = 1e-6

kernel_name = "hybrid_conv_pool_stickbreak_gated"

def rms_norm(x, g):
    x32 = x.astype(jnp.float32)
    y = x32 * lax.rsqrt(jnp.mean(x32 * x32, axis=-1, keepdims=True) + EPS)
    return y.astype(x.dtype) * g

def layer_norm(x, g, b):
    x32 = x.astype(jnp.float32)
    mu = jnp.mean(x32, axis=-1, keepdims=True)
    xc = x32 - mu
    y = xc * lax.rsqrt(jnp.mean(xc * xc, axis=-1, keepdims=True) + EPS)
    return y.astype(x.dtype) * g + b

def causal_dwconv(x, w, b):
    k, c = w.shape
    y = lax.conv_general_dilated(
        x, w[:, None, :].astype(x.dtype), window_strides=(1,), padding=[(k - 1, 0)],
        dimension_numbers=("NWC", "WIO", "NWC"), feature_group_count=c)
    return y + b

def conv_module(u, dw_w, dw_b, ln_g, ln_b, w_out, b_out):
    a, gate = jnp.split(u, 2, axis=-1)
    h = a * jax.nn.sigmoid(gate)
    h = causal_dwconv(h, dw_w, dw_b)
    h = layer_norm(h, ln_g, ln_b)
    h = jax.nn.silu(h)
    return h @ w_out + b_out

def pool_mixer(p, w_grp, scale):
    b, l, _ = p.shape
    p32 = p.astype(jnp.float32)
    csum = jnp.cumsum(p32, axis=1)
    pos = jnp.arange(l, dtype=jnp.float32)[:, None]
    groups = []
    for g, w in enumerate(POOL_WINDOWS):
        sl = slice(g * POOL_GC, (g + 1) * POOL_GC)
        cg = csum[..., sl]
        lag = jnp.pad(cg, ((0, 0), (w, 0), (0, 0)))[:, :l]
        mean = (cg - lag) / jnp.minimum(pos + 1.0, float(w))
        groups.append(mean - p32[..., sl])
    pooled = jnp.stack(groups, axis=2).astype(p.dtype)
    y = jnp.einsum("blgc,gcd->blgd", pooled, w_grp).reshape(b, l, D_MODEL)
    return y * scale

def stick_breaking_attention(q, k, v):
    b, l, h, dh = q.shape
    pad = ((0, 0), (META_PAD, 0), (0, 0), (0, 0))
    qp = jnp.pad(q.astype(jnp.float32) * (HEAD_DIM ** -0.5), pad).transpose(0, 2, 1, 3)
    kp = jnp.pad(k.astype(jnp.float32), pad).transpose(0, 2, 1, 3)
    vp = jnp.pad(v.astype(jnp.float32), pad).transpose(0, 2, 1, 3)
    lp = l + META_PAD
    n_blocks = lp // BLOCK
    tri = jnp.asarray(np.tril(np.ones((BLOCK, BLOCK), np.float32), -1))
    outs = []
    for i in range(n_blocks):
        nk = i + 1
        kl = nk * BLOCK
        qb = qp[:, :, i * BLOCK:(i + 1) * BLOCK]
        z = jnp.einsum("bhqd,bhkd->bhqk", qb, kp[:, :, :kl])
        qpos = i * BLOCK + jnp.arange(BLOCK)
        kpos = jnp.arange(kl)
        valid = (kpos[None, :] < qpos[:, None]) & (kpos[None, :] >= META_PAD)
        log_keep = jnp.where(valid, jax.nn.log_sigmoid(-z), 0.0)
        lk = log_keep.reshape(b, h, BLOCK, nk, BLOCK)
        within = jnp.einsum("bhqnj,js->bhqns", lk, tri)
        blk_sum = jnp.sum(lk, axis=-1)
        blk_tri = jnp.asarray(np.tril(np.ones((nk, nk), np.float32), -1))
        later = jnp.einsum("bhqm,mn->bhqn", blk_sum, blk_tri)
        log_keep_after = (within + later[..., None]).reshape(b, h, BLOCK, kl)
        a = jnp.where(valid, jnp.exp(z + log_keep + log_keep_after), 0.0)
        outs.append(jnp.einsum("bhqk,bhkd->bhqd", a, vp[:, :, :kl]))
    out = jnp.concatenate(outs, axis=2)
    out = out.transpose(0, 2, 1, 3).reshape(b, lp, h * dh)[:, META_PAD:]
    return out.astype(q.dtype)

def gated_conv_mlp(x, w_up, dw_w, dw_b, w_down):
    u = x @ w_up
    u = causal_dwconv(u, dw_w, dw_b)
    gate, val = jnp.split(u, 2, axis=-1)
    return (jax.nn.gelu(gate) * val) @ w_down

def _w(key, shape, fan_in):
    return jax.random.normal(key, shape, jnp.float32) * (fan_in ** -0.5)

def setup_inputs(seed: int = 0) -> dict:
    key = jax.random.key(seed)
    ks = jax.random.split(key, 24)
    L = DEPTH
    return {
        "x": jax.random.normal(ks[0], (BATCH, SEQ, D_MODEL), jnp.float32),
        "meta": jax.random.normal(ks[1], (N_META, D_MODEL), jnp.float32),
        "norm1": 1.0 + 0.02 * jax.random.normal(ks[2], (L, D_MODEL), jnp.float32),
        "w_in": _w(ks[3], (L, D_MODEL, D_IN), D_MODEL),
        "conv_dw_w": _w(ks[4], (L, CONV_K, CONV_CH), CONV_K),
        "conv_dw_b": 0.02 * jax.random.normal(ks[5], (L, CONV_CH), jnp.float32),
        "conv_ln_g": 1.0 + 0.02 * jax.random.normal(ks[6], (L, CONV_CH), jnp.float32),
        "conv_ln_b": 0.02 * jax.random.normal(ks[7], (L, CONV_CH), jnp.float32),
        "w_conv_out": _w(ks[8], (L, CONV_CH, D_MODEL), CONV_CH),
        "b_conv_out": 0.02 * jax.random.normal(ks[9], (L, D_MODEL), jnp.float32),
        "w_pool_grp": _w(ks[10], (L, POOL_GROUPS, POOL_GC, POOL_OUT), POOL_GC),
        "pool_scale": 1.0 + 0.02 * jax.random.normal(ks[11], (L, D_MODEL), jnp.float32),
        "w_attn_out": _w(ks[12], (L, ATT_W, D_MODEL), ATT_W),
        "w_o": _w(ks[13], (L, D_MODEL, D_MODEL), D_MODEL),
        "norm2": 1.0 + 0.02 * jax.random.normal(ks[14], (L, D_MODEL), jnp.float32),
        "w_up": _w(ks[15], (L, D_MODEL, 2 * D_FF), D_MODEL),
        "ffn_dw_w": _w(ks[16], (L, FFN_K, 2 * D_FF), FFN_K),
        "ffn_dw_b": 0.02 * jax.random.normal(ks[17], (L, 2 * D_FF), jnp.float32),
        "w_down": _w(ks[18], (L, D_FF, D_MODEL), D_FF),
        "final_norm": 1.0 + 0.02 * jax.random.normal(ks[19], (D_MODEL,), jnp.float32),
    }

def reference(x, meta, norm1, w_in, conv_dw_w, conv_dw_b, conv_ln_g, conv_ln_b, w_conv_out, b_conv_out,
              w_pool_grp, pool_scale, w_attn_out, w_o, norm2, w_up, ffn_dw_w, ffn_dw_b, w_down, final_norm):
    b = x.shape[0]
    h = jnp.concatenate([jnp.broadcast_to(meta[None].astype(x.dtype), (b, N_META, D_MODEL)), x], axis=1)
    l = h.shape[1]
    splits = [2 * CONV_CH, 2 * CONV_CH + POOL_CH, 2 * CONV_CH + POOL_CH + ATT_W,
              2 * CONV_CH + POOL_CH + 2 * ATT_W, 2 * CONV_CH + POOL_CH + 3 * ATT_W]
    for i in range(DEPTH):
        hn = rms_norm(h, norm1[i])
        proj = hn @ w_in[i]
        u_conv, u_pool, q, k, v, gates = jnp.split(proj, splits, axis=-1)
        y_a = conv_module(u_conv, conv_dw_w[i], conv_dw_b[i], conv_ln_g[i], conv_ln_b[i],
                          w_conv_out[i], b_conv_out[i])
        y_b = pool_mixer(u_pool, w_pool_grp[i], pool_scale[i])
        att = stick_breaking_attention(q.reshape(b, l, ATT_HEADS, HEAD_DIM),
                                       k.reshape(b, l, ATT_HEADS, HEAD_DIM),
                                       v.reshape(b, l, ATT_HEADS, HEAD_DIM))
        y_c = att @ w_attn_out[i]
        g = jax.nn.sigmoid(gates).reshape(b, l, N_BRANCH, D_MODEL)
        mixed = g[:, :, 0] * y_a + g[:, :, 1] * y_b + g[:, :, 2] * y_c
        h = h + mixed @ w_o[i]
        h = h + gated_conv_mlp(rms_norm(h, norm2[i]), w_up[i], ffn_dw_w[i], ffn_dw_b[i], w_down[i])
    return rms_norm(h, final_norm)[:, N_META:]


_drawn_inputs = setup_inputs


def setup_inputs(seed=0):
    import zlib

    import numpy as np

    out = dict(_drawn_inputs(seed))
    spreads = {}
    factors = {'norm1': 3.889,
     'conv_dw_b': 23.767,
     'conv_ln_g': 60.136,
     'conv_ln_b': 64.0,
     'b_conv_out': 46.184,
     'pool_scale': 6.392,
     'norm2': 13.122,
     'ffn_dw_b': 12.816,
     'final_norm': 8.053}
    for name, (base, spread) in spreads.items():
        noise = np.random.default_rng([zlib.crc32(name.encode()), seed]).standard_normal(out[name].shape)
        drawn = base * np.exp(spread * noise) if base else spread * noise
        out[name] = __import__('jax').numpy.asarray(drawn.astype(out[name].dtype))
    for name, factor in factors.items():
        out[name] = (out[name] * factor).astype(out[name].dtype)
    return out
```

```python
import concourse.bass as bass
from concourse import mybir
from contextlib import ExitStack


def hybrid_trunk_kernel(nc, x, meta, norm1, w_in, conv_dw_w, conv_dw_b, conv_ln_g, conv_ln_b, w_conv_out,
                        b_conv_out, w_pool_grp, pool_scale, w_attn_out, w_o, norm2, w_up, ffn_dw_w,
                        ffn_dw_b, w_down, final_norm, out):
    f32, f32r = mybir.dt.float32, mybir.dt.float32r
    ALU, ACT = mybir.AluOpType, mybir.ActivationFunctionType
    COPY = ACT.Copy

    P = 128
    SEQ, DM = x.shape[1], x.shape[2]
    NMETA = meta.shape[0]
    T = NMETA + SEQ
    KC = DM // P
    NT = -(-T // P)
    TP = NT * P
    REST = T - (NT - 1) * P
    TAPS, CONV = conv_dw_w.shape[1], conv_dw_w.shape[2]
    CC = CONV // P
    GRPS, GC, GOUT = w_pool_grp.shape[1:]
    POOLC = GRPS * GC
    WINDOWS = (2, 4, 8, 16)
    ATTW = w_attn_out.shape[1]
    DH = P
    HEADS = ATTW // DH
    FF = w_down.shape[1]
    FC = FF // P
    FTAPS = ffn_dw_w.shape[1]
    EPS = 1e-6
    SCALE = float(DH) ** -0.5
    COL_POOL = 2 * CONV
    COL_Q = COL_POOL + POOLC
    COL_K, COL_V, COL_GATE = COL_Q + ATTW, COL_Q + 2 * ATTW, COL_Q + 3 * ATTW

    THIRD = [(0, 352), (352, 344), (696, 344)]
    NU = len(THIRD)
    TW = THIRD[0][1]
    QW = T // 4
    TILES = [(i, n) for i in range(T // QW) for n in reversed(range((QW * (i + 1) - 2) // P + 1))]
    LAST = [n == 0 for _, n in TILES]
    FIRST = [k == 0 or TILES[k - 1][0] != TILES[k][0] for k in range(len(TILES))]
    MASKED = [P * n + P - 1 >= QW * i for i, n in TILES]
    NS = len(TILES)
    STEPS = NS * HEADS
    FILL0 = 3
    GROUPS = [(0, 4), (4, 4), (8, 1)]
    SPAN = [(0, 512), (512, 512), (1024, T - 1024)]

    C_N1, C_N2, C_BC, C_PS = 0, KC, 2 * KC, 3 * KC
    C_CB = 4 * KC
    C_LG, C_LB = C_CB + CC, C_CB + 2 * CC
    C_CW = C_CB + 3 * CC
    C_FW = C_CW + TAPS * CC
    C_FB = C_FW + FTAPS * 2 * FC
    NCOL = C_FB + 2 * FC

    SLOT_Q0 = 2 * CC
    SLOT_ATT = SLOT_Q0 + 3
    SLOT_MIX = SLOT_ATT + 3 * (HEADS - 1) + POOLC // P
    SLOT_OUT = SLOT_MIX + 4 * KC
    SLOT_FFN = SLOT_OUT + KC
    HALF_SLOTS = 6 + KC // 2
    SLOT_END = SLOT_FFN + 2 * FC + FC // 3 * (KC // 2)
    UNIT_Q0 = NU * SLOT_Q0
    UNIT_ATT = UNIT_Q0 + 3 * NU
    UNIT_MIX = UNIT_ATT + NU * HEADS + NU * (SLOT_MIX - SLOT_ATT)
    UNIT_OUT = UNIT_MIX + 2 * NU * 3 * KC
    UNIT_FFN = UNIT_OUT + NU * KC
    HALF_UP, HALF_DOWN = 6 * NU, NU * KC
    HALF_UNITS = HALF_UP + HALF_DOWN
    DVE_MIX = UNIT_MIX
    DVE_FFN = DVE_MIX + 3 * NU * KC
    ACT_OUT = 3 * NU * KC
    ACT_FFN = ACT_OUT + NU * KC

    def slot_att(h, j):
        return SLOT_ATT + 3 * h + j

    def unit_att(h):
        return UNIT_ATT + (4 * NU) * h

    def slot_left(n):
        if n < SLOT_Q0:
            return 2 * NU * (n // 2 + 1) - 1 + n % 2
        if n < SLOT_ATT:
            return UNIT_Q0 + NU * (n - SLOT_Q0 + 1)
        if n < SLOT_MIX:
            h = min((n - SLOT_ATT) // 3, HEADS - 1)
            return unit_att(h) + NU + NU * (n - slot_att(h, 0) + 1)
        if n < SLOT_OUT:
            c, j = divmod(n - SLOT_MIX, 4)
            return UNIT_MIX + 6 * NU * c + (NU * (j + 1) if j < 3 else 6 * NU)
        if n < SLOT_FFN:
            return UNIT_OUT + (2 * NU - 1 + n - SLOT_OUT if n < SLOT_OUT + 2 else NU * (n - SLOT_OUT + 1))
        assert n < SLOT_FFN + 2
        return UNIT_FFN + NU * (n - SLOT_FFN + 1)

    def fillers(h):
        return 3 * NU if h < HEADS - 1 else NU * (POOLC // P)

    B = 4
    ctx = ExitStack()
    with ctx:
        base = [-(-nc.sbuf_base // 32) * 32]

        def place(name, shape, dtype, at):
            return nc.alloc_sbuf_tensor_at(name, shape, dtype, offset=at)

        def take(name, shape, dtype=f32):
            n = B
            for s in shape[1:]:
                n *= s
            at = base[0]
            base[0] += -(-n // 32) * 32
            return place(name, shape, dtype, at)

        ident = take("ident", [P, P])
        ones = take("ones", [P, P])
        neg_tri = take("neg_tri", [P, P], f32r)
        neg_rest = take("neg_rest", [P, P], f32r)
        cols = take("cols", [P, NCOL])
        eps = take("eps", [P, 1])
        stat = take("stat", [P, 4 * NT])
        inv_cnt = take("inv_cnt", [P, CC, WINDOWS[-1]])
        raw = [take(f"raw{s}", [P, KC, P]) for s in range(2)]
        wh = [take(f"wh{s}", [P, KC, P], f32r) for s in range(2)]
        wl = [take(f"wl{s}", [P, KC, P], f32r) for s in range(2)]
        HN = base[0]
        hn_hi = take("hn_hi", [P, KC, T], f32r)
        hn_lo = take("hn_lo", [P, KC, T], f32r)
        ATT = base[0]
        att_hi = take("att_hi", [P, HEADS, T], f32r)
        att_lo = take("att_lo", [P, HEADS, T], f32r)
        R = base[0]
        U, UP = T * B, TP * B

        assert R + 20 * T * B <= nc.sbuf_usable_end, (R, nc.sbuf_usable_end)
        xn = place("xn", [P, NT, DM], f32, R)
        QK = 2 * U + 2 * UP
        q_hi = [place(f"q_hi{s}", [P, T], f32r, R + s * QK) for s in range(2)]
        q_lo = [place(f"q_lo{s}", [P, T], f32r, R + s * QK + U) for s in range(2)]
        k_hi = [place(f"k_hi{s}", [P, TP], f32r, R + s * QK + 2 * U) for s in range(2)]
        k_lo = [place(f"k_lo{s}", [P, TP], f32r, R + s * QK + 2 * U + UP) for s in range(2)]
        R_VT = R + 2 * QK
        vt = place("vt", [P, TP], f32, R_VT)
        R_V = R_VT + UP
        v_hi = place("v_hi", [P, NT, DH], f32r, R_V)
        v_lo = place("v_lo", [P, NT, DH], f32r, R_V + UP)
        R_TMP = R_V + 2 * UP
        W = -(-QW * B // 32) * 32
        zs = [place(f"zs{s}", [P, QW], f32, R_TMP + s * W) for s in range(3)]
        soft = [place(f"soft{s}", [P, QW], f32, R_TMP + (3 + s) * W) for s in range(2)]
        sp = place("sp", [P, QW], f32, R_TMP + 5 * W)
        sp_hi = [place(f"sp_hi{s}", [P, QW], f32r, R_TMP + (6 + s) * W) for s in range(2)]
        sp_lo = [place(f"sp_lo{s}", [P, QW], f32r, R_TMP + (8 + s) * W) for s in range(2)]
        att_w = [place(f"att_w{s}", [P, QW], f32, R_TMP + (10 + s) * W) for s in range(2)]
        a_hi = [place(f"a_hi{s}", [P, QW], f32r, R_TMP + (12 + s) * W) for s in range(2)]
        a_lo = [place(f"a_lo{s}", [P, QW], f32r, R_TMP + (14 + s) * W) for s in range(2)]
        sig = [place(f"sig{s}", [P, TW], f32, R_TMP + s * TW * B) for s in range(2)]
        rows = place("rows", [P, 3, P], f32, R_TMP + 3072)
        junk = [place(f"junk{s}", [P, DM], f32, R_TMP + 4608 + s * DM * B) for s in range(2)]
        mask32 = place("mask32", [P, 2, P], f32, R_TMP + 4608 + 2 * DM * B)
        R_CV = R_TMP + 16 * W
        cv = place("cv", [P, CC, T], f32, R_CV)
        R_PB = R_CV + CC * U
        LEFT = WINDOWS[-1]
        glu = place("glu", [P, CC, TAPS - 1 + T], f32, R_PB)
        assert R_PB + CC * (TAPS - 1 + T) * B <= nc.sbuf_usable_end
        pool_in = place("pool_in", [P, CC, LEFT + T], f32, R_PB)
        s_hi = place("s_hi", [P, CC, T], f32r, R)
        s_lo = place("s_lo", [P, CC, T], f32r, R + 2 * U)
        pooled_hi = place("pooled_hi", [P, CC, T], f32r, R + 4 * U)
        pooled_lo = place("pooled_lo", [P, CC, T], f32r, R + 6 * U)
        gate = place("gate", [P, 3, T], f32, R + 8 * U)
        pool_w = place("pool_w", [P, KC, P], f32, R + 11 * U)
        R_MIX = R + 11 * U + KC * P * B
        mixed = place("mixed", [P, KC, T], f32, R_MIX)
        win = [place(f"win{s}", [P, LEFT + T], f32, R_MIX + s * (LEFT + T) * B) for s in range(2)]
        sq_cv = place("sq_cv", [P, CC, TW], f32, R_MIX + 2 * (LEFT + T) * B)
        std_cv = place("std_cv", [P, T], f32, R_MIX + 2 * (LEFT + T) * B + CC * TW * B)
        assert R_MIX + 2 * (LEFT + T) * B + CC * TW * B + U <= R_CV
        mix_hi = place("mix_hi", [P, KC, T], f32r, HN)
        mix_lo = place("mix_lo", [P, KC, T], f32r, HN + KC * U)
        x_again = place("x_again", [P, NT - 1, DM], f32, ATT)
        h2 = place("h2", [P, KC, T], f32, R)
        x_last = place("x_last", [P, DM], f32, R + 8 * U)
        sq_h = place("sq_h", [P, T], f32, R + 9 * U)
        sq_sum = place("sq_sum", [P, T], f32, R + 10 * U)
        R_T4 = R_MIX
        rstd2 = place("rstd2", [P, T], f32, R_T4)
        scaled = [place(f"scaled{s}", [P, 512], f32, R_T4 + U + s * 2048) for s in range(2)]
        UW = -(-(FTAPS - 1 + T) // 8) * 8
        up = [place(f"up{s}", [P, UW], f32, ATT + s * UW * B) for s in range(2)]
        acc = [place(f"acc{s}", [P, T], f32, ATT + 2 * UW * B + s * U) for s in range(4)]
        final_g = place("final_g", [P, DM], f32, ATT + 2 * UW * B + 4 * U)
        assert 2 * UW * B + 4 * U + DM * B <= 8 * U
        RING = 6
        g_hi = place("g_hi", [P, RING, T], f32r, R + 8 * U)
        g_lo = place("g_lo", [P, RING, T], f32r, R + 14 * U)
        sq_out = [place(f"sq_out{s}", [P, DM], f32, HN + s * DM * B) for s in range(2)]
        y_out = [place(f"y_out{s}", [P, DM], f32, HN + (2 + s) * DM * B) for s in range(3)]

        psum = ctx.enter_context(nc.psum_tensor("psum", [P, 8, 512], f32))
        PZ, PU, PO = [3, 4], [5, 6], 7

        def sem(name):
            return ctx.enter_context(nc.semaphore(name))

        x_in = [sem(f"x_in{g}") for g in range(3)]
        params_in = sem("params_in")
        raw_in = [sem("raw_in0"), sem("raw_in1")]
        pool_w_in = sem("pool_w_in")
        x_again_in = sem("x_again_in")
        final_g_in = sem("final_g_in")
        stored = [sem(f"stored{s}") for s in range(3)]
        ident_set = sem("ident_set")
        masks32_set = sem("masks32_set")
        masks_set = sem("masks_set")
        cols_t = sem("cols_t")
        cols_set = sem("cols_set")
        glu_pad_set = sem("glu_pad_set")
        kv_pads_set = sem("kv_pads_set")
        pool_pad_set = sem("pool_pad_set")
        up_pads_set = sem("up_pads_set")
        pool_w_zeroed = sem("pool_w_zeroed")
        cnt_set = sem("cnt_set")
        x_ss = sem("x_ss")
        x_ms = sem("x_ms")
        x_std = sem("x_std")
        x_rstd = sem("x_rstd")
        xn_done = sem("xn_done")
        xt_done = sem("xt_done")
        hn_hi_done = sem("hn_hi_done")
        hn_done = sem("hn_done")
        w_hi_done = sem("w_hi_done")
        w_lo_done = sem("w_lo_done")
        unit_done = sem("unit_done")
        act_freed = sem("act_freed")
        dve_freed = sem("dve_freed")
        evac_hi = sem("evac_hi")
        sig_done = sem("sig_done")
        conv_chain = sem("conv_chain")
        z_done = sem("z_done")
        z_copied = sem("z_copied")
        nabs_done = sem("nabs_done")
        exp_done = sem("exp_done")
        log_done = sem("log_done")
        sp_done = sem("sp_done")
        sp_masked = sem("sp_masked")
        sp_hi_done = sem("sp_hi_done")
        sp_split = sem("sp_split")
        u_done = sem("u_done")
        logit_done = sem("logit_done")
        a_done = sem("a_done")
        a_masked = sem("a_masked")
        a_hi_done = sem("a_hi_done")
        a_split = sem("a_split")
        o_mm = sem("o_mm")
        o_hi_done = sem("o_hi_done")
        o_evac = sem("o_evac")
        mu_done = sem("mu_done")
        xc_done = sem("xc_done")
        sqc_done = sem("sqc_done")
        var_done = sem("var_done")
        stdc_done = sem("stdc_done")
        rstdc_done = sem("rstdc_done")
        yc_done = sem("yc_done")
        silu_done = sem("silu_done")
        s_hi_done = sem("s_hi_done")
        s_ready = sem("s_ready")
        win_chain = sem("win_chain")
        pooled_ready = sem("pooled_ready")
        mix_chain = sem("mix_chain")
        mix_done = sem("mix_done")
        mix_hi_done = sem("mix_hi_done")
        mix_split = sem("mix_split")
        h2_copied = sem("h2_copied")
        xt2_done = sem("xt2_done")
        res_done = sem("res_done")
        sqh_done = sem("sqh_done")
        ssum_done = sem("ssum_done")
        ss2_done = sem("ss2_done")
        std2_done = sem("std2_done")
        rstd2_done = sem("rstd2_done")
        scaled_done = sem("scaled_done")
        hn2_hi_done = sem("hn2_hi_done")
        hn2_done = sem("hn2_done")
        up_evac = sem("up_evac")
        tap_chain = sem("tap_chain")
        conv_done = sem("conv_done")
        gelu_done = sem("gelu_done")
        prod_done = sem("prod_done")
        g_hi_done = sem("g_hi_done")
        g_done = sem("g_done")
        ht_done = sem("ht_done")
        sso_done = sem("sso_done")
        mso_done = sem("mso_done")
        stdo_done = sem("stdo_done")
        rstdo_done = sem("rstdo_done")
        y_done = sem("y_done")

        block = ctx.enter_context(nc.Block())

        def unit_bank(j):
            return j % NU

        @block.sync
        def _(sp_eng):
            e = sp_eng

            def load(n, src, dst, again=0):
                if not (isinstance(n, int) and n < 2):
                    e.wait_ge(w_lo_done, n - 1)
                e.dma_start(dst, src).then_inc(raw_in[again], 16)

            def at_col(value):
                if isinstance(value, int):
                    return value
                return e.snap(value)

            def w_tile(w, col, width=P):
                return w[0].rearrange("(k p) n -> p k n", p=P)[:, :, bass.ds(col, width)]

            def full(s):
                return raw[s][:, :, :]

            first = NMETA
            e.dma_start(xn[0:first, 0, :], meta).then_inc(x_in[0], 16)
            e.dma_start(xn[first:P, 0, :], x[0, 0:P - first, :]).then_inc(x_in[0], 16)
            a = P - first
            e.dma_start(xn[:, 1:4, :], x[0, a:a + 3 * P, :].rearrange("(i p) d -> p i d", p=P)).then_inc(x_in[0], 16)
            load(0, w_tile(w_in, 0), full(0), 0)
            load(1, w_tile(w_in, CONV), full(1), 1)
            b = a + 3 * P
            e.dma_start(xn[:, 4:8, :], x[0, b:b + 4 * P, :].rearrange("(i p) d -> p i d", p=P)).then_inc(x_in[1], 16)
            e.dma_start(xn[0:REST, NT - 1, :], x[0, SEQ - REST:SEQ, :]).then_inc(x_in[2], 16)
            for c in range(1, CC):
                load(2 * c, w_tile(w_in, c * P), full(0), 0)
                load(2 * c + 1, w_tile(w_in, CONV + c * P), full(1), 1)
            for j, col in enumerate((COL_Q, COL_K, COL_V)):
                n = SLOT_Q0 + j
                load(n, w_tile(w_in, col), full(n % 2), n % 2)
            for h in range(HEADS):
                cs = [c + (h + 1) * DH for c in (COL_Q, COL_K, COL_V)] if h < HEADS - 1 else \
                     [COL_POOL + c * P for c in range(POOLC // P)]
                for j, col in enumerate(cs):
                    n = slot_att(h, j)
                    load(n, w_tile(w_in, col), full(n % 2), n % 2)
            def load_gate(c, br):
                col = at_col(c * P + (COL_GATE + br * DM))
                e.wait_ge(w_lo_done, c * 4 + (SLOT_MIX + br - 1))
                e.dma_start(full(br % 2), w_tile(w_in, col)).then_inc(raw_in[br % 2], 16)

            load_gate(0, 0)
            load_gate(0, 1)
            e.wait_ge(pool_w_zeroed, 1)
            for g in range(GRPS):
                half = GC * (g % 2)
                per = GOUT // P
                e.dma_start(pool_w[half:half + GC, per * g:per * (g + 1), :],
                            w_pool_grp[0, g, :, :].rearrange("k (c n) -> k c n", n=P)).then_inc(pool_w_in, 16)
            load_gate(0, 2)
            with e.Fori(1, KC) as c:
                for br in range(3):
                    load_gate(c, br)
            for m in range(2):
                load(SLOT_OUT + m, w_tile(w_o, m * P), full(m % 2), m % 2)
            e.wait_ge(unit_done, UNIT_OUT)
            e.wait_ge(mix_done, NU * KC)
            e.dma_start(x_again[0:first, 0, :], meta).then_inc(x_again_in, 16)
            e.dma_start(x_again[first:P, 0, :], x[0, 0:P - first, :]).then_inc(x_again_in, 16)
            e.dma_start(x_again[:, 1:NT - 1, :],
                        x[0, a:a + (NT - 2) * P, :].rearrange("(i p) d -> p i d", p=P)).then_inc(x_again_in, 16)
            e.dma_start(x_last[0:REST, :], x[0, SEQ - REST:SEQ, :]).then_inc(x_again_in, 16)
            for m in range(2, KC):
                load(SLOT_OUT + m, w_tile(w_o, m * P), full(m % 2), m % 2)

            def load_up(n, j):
                for s in range(2):
                    col = at_col(j * P + s * FF)
                    load(n + s, w_tile(w_up, col), full(s), s)

            def load_half(n, j0, chunks):
                for i in range(chunks):
                    load_up(n + 2 * i, j0 + (1 + i))
                row = at_col(j0 * P)
                for m in range(KC // 2):
                    load(n + (2 * chunks + m),
                         w_down[0, bass.ds(row, 3 * P), m * 2 * P:(m + 1) * 2 * P].rearrange("(k p) n -> p k n", p=P),
                         raw[m % 2][:, 0:6, :].rearrange("p (k m) n -> p k (m n)", k=3), m % 2)

            load_up(SLOT_FFN, 0)
            e.wait_ge(xt2_done, NU * KC)
            e.dma_start(final_g[:, :], final_norm.partition_broadcast(P)).then_inc(final_g_in, 16)
            with e.Fori(0, FC // 6 - 1) as it:
                for half in range(2):
                    load_half(it * (2 * HALF_SLOTS) + (SLOT_FFN + 2 + half * HALF_SLOTS), it * 6 + 3 * half, 3)
            it = FC // 6 - 1
            for half in range(2):
                load_half(it * (2 * HALF_SLOTS) + (SLOT_FFN + 2 + half * HALF_SLOTS), it * 6 + 3 * half, 3 - half)
            for i in range(SEQ // P):
                e.wait_ge(y_done, i + 1)
                e.dma_start(out[0, i * P:(i + 1) * P, :], y_out[i % 3][:, :]).then_inc(stored[i % 3], 16)
            for s in range(3):
                e.wait_ge(stored[s], 16 * len(range(s, SEQ // P, 3)))

        @block.gpsimd
        def _(e):
            def split_lo(n):
                s = n % 2
                e.wait_ge(w_hi_done, n + 1)
                e.tensor_tensor(wl[s][:, :, :], raw[s][:, :, :], wh[s][:, :, :].bitcast(f32), ALU.subtract)\
                    .then_inc(w_lo_done, 1)

            def split_lo_at(s, n, tiles=KC):
                e.wait_ge(w_hi_done, n + 1)
                e.tensor_tensor(wl[s][:, 0:tiles, :], raw[s][:, 0:tiles, :], wh[s][:, 0:tiles, :].bitcast(f32),
                                ALU.subtract).then_inc(w_lo_done, 1)

            e.memset(ident[:, :], 0.0).then_inc(ident_set, 1)
            e.memset(ones[:, :], 1.0).then_inc(ident_set, 1)
            e.memset(eps[:, :], EPS).then_inc(ident_set, 1)
            e.wait_ge(ident_set, 3)
            e.affine_select(out=ident[:, :], in_=ident[:, :], compare_op=ALU.not_equal, fill=1.0, base=0,
                            pattern=[[-1, P]], channel_multiplier=1).then_inc(ident_set, 1)
            e.memset(mask32[:, :, :], -1.0).then_inc(masks32_set, 1)
            e.wait_ge(masks32_set, 1)
            e.affine_select(out=mask32[:, 0, :], in_=mask32[:, 0, :], compare_op=ALU.is_ge, fill=0.0, base=0,
                            pattern=[[-1, P]], channel_multiplier=1).then_inc(masks32_set, 1)
            e.affine_select(out=mask32[:, 1, :], in_=mask32[:, 1, :], compare_op=ALU.is_gt, fill=0.0, base=0,
                            pattern=[[1, P]], channel_multiplier=-1).then_inc(masks32_set, 1)
            e.memset(glu[:, :, 0:TAPS - 1], 0.0).then_inc(glu_pad_set, 1)
            e.iota(inv_cnt[:, :, :], pattern=[[0, CC], [1, LEFT]], base=1, channel_multiplier=0,
                   allow_small_or_imprecise_dtypes=True).then_inc(cnt_set, 1)
            split_lo(0)
            split_lo(1)
            e.wait_ge(xt_done, KC * len(GROUPS))
            for s in range(2):
                e.memset(k_hi[s][:, T:TP].bitcast(f32), 0.0).then_inc(kv_pads_set, 1)
                e.memset(k_lo[s][:, T:TP].bitcast(f32), 0.0).then_inc(kv_pads_set, 1)
            e.memset(vt[:, T:TP], 0.0).then_inc(kv_pads_set, 1)
            for n in range(2, SLOT_ATT + 2):
                split_lo(n)

            masked_sp = [0]
            masked_a = [0]

            def causal(buf, t):
                i, n = TILES[t % NS]
                return e.affine_select(out=buf[:, :], in_=buf[:, :], compare_op=ALU.is_gt, fill=0.0,
                                       base=QW * i - P * n, pattern=[[1, QW]], channel_multiplier=-1)

            def mask_sp(t):
                if MASKED[t % NS]:
                    e.wait_ge(sp_done, t + 1)
                    causal(sp, t).then_inc(sp_masked, 1)

            mask_sp(0)
            for h in range(HEADS):
                nfill = fillers(h)
                if h == HEADS - 1:
                    e.wait_ge(conv_chain, TAPS * CC)
                    e.memset(pool_in[:, :, 0:LEFT], 0.0).then_inc(pool_pad_set, 1)
                for idx in range(NS):
                    t = h * NS + idx
                    if t + 1 < STEPS:
                        mask_sp(t + 1)
                    if MASKED[idx]:
                        e.wait_ge(a_done, t + 1)
                        causal(att_w[t % 2], t).then_inc(a_masked, 1)
                    e.wait_ge(a_hi_done, t + 1)
                    if t >= 2:
                        e.wait_ge(o_mm, t - 1)
                    e.tensor_tensor(a_lo[t % 2][:, :], att_w[t % 2][:, :], a_hi[t % 2][:, :].bitcast(f32),
                                    ALU.subtract).then_inc(a_split, 1)
                    j = (idx - FILL0) // 6 - 1
                    if (idx - FILL0) % 6 == 0 and 0 <= j < nfill // NU:
                        split_lo(slot_att(h, j) + 2)
            e.wait_ge(o_evac, HEADS * (T // QW))
            e.memset(pool_w[:, :, :], 0.0).then_inc(pool_w_zeroed, 1)

            with e.Fori(0, KC) as c:
                n = SLOT_MIX + c * 4
                split_lo_at(0, n + 2)
                split_lo_at(1, n + 3, HEADS + CC + 1)
                split_lo_at(0, n + 4)
                split_lo_at(1, n + 5)
            for m in range(KC):
                split_lo(SLOT_OUT + 2 + m)

            split_lo(SLOT_FFN + 2)
            split_lo(SLOT_FFN + 3)

            def split_half(n, chunks, tail=0):
                for i in range(2 * chunks - 2):
                    split_lo_at(i % 2, n + i)
                for m in range(KC // 2):
                    split_lo_at(m % 2, n + (2 * chunks - 2 + m), 6)
                for i in range(2 - tail):
                    split_lo_at(i % 2, n + (2 * chunks - 2 + KC // 2 + i))

            with e.Fori(0, FC // 6 - 1) as it:
                for half in range(2):
                    split_half(it * (2 * HALF_SLOTS) + (SLOT_FFN + 4 + half * HALF_SLOTS), 3)
            n = SLOT_FFN + 4 + (FC // 6 - 1) * 2 * HALF_SLOTS
            split_half(n, 3)
            split_half(n + HALF_SLOTS, 2, tail=2)

        @block.scalar
        def _(e):
            raw_count = [0, 0]

            def split_hi(n, tiles=KC, dmas=1):
                s = n % 2
                raw_count[s] += 16 * dmas
                e.wait_ge(raw_in[s], raw_count[s])
                if n >= 2:
                    e.wait_ge(unit_done, slot_left(n - 2))
                e.activation(wh[s][:, 0:tiles, :], raw[s][:, 0:tiles, :], COPY).then_inc(w_hi_done, 1)

            def split_hi_at(s, left, raw_value, tiles=KC):
                e.wait_ge(raw_in[s], raw_value)
                e.wait_ge(unit_done, left)
                e.activation(wh[s][:, 0:tiles, :], raw[s][:, 0:tiles, :], COPY).then_inc(w_hi_done, 1)

            def rows_in(slot, at, count, src):
                e.dma_start(rows[at:at + count, slot, :], src).then_inc(params_in, 16)

            n_params = 0
            for at, p in ((C_N1, norm1), (C_N2, norm2), (C_BC, b_conv_out), (C_PS, pool_scale)):
                rows_in(0, at, KC, p[0].rearrange("(k p) -> k p", p=P))
                n_params += 1
            for at, p in ((C_CB, conv_dw_b), (C_LG, conv_ln_g), (C_LB, conv_ln_b)):
                rows_in(0, at, CC, p[0].rearrange("(k p) -> k p", p=P))
                n_params += 1
            rows_in(0, C_CW, TAPS * CC, conv_dw_w[0].rearrange("t (k p) -> (t k) p", p=P))
            fw = ffn_dw_w[0].rearrange("t (k p) -> (t k) p", p=P)
            rows_in(1, 0, P, fw[0:P, :])
            rows_in(2, 0, FTAPS * 2 * FC - P, fw[P:FTAPS * 2 * FC, :])
            rows_in(2, FTAPS * 2 * FC - P, 2 * FC, ffn_dw_b[0].rearrange("(k p) -> k p", p=P))

            def hn_hi_group(g):
                c0, cn = SPAN[g]
                for k in range(KC):
                    n = g * KC + k
                    if n == 0:
                        e.wait_ge(cols_set, 1)
                    e.wait_ge(xt_done, n + 1)
                    e.activation(hn_hi[:, k, c0:c0 + cn], psum[:, 3 + n % 4, 0:cn], COPY,
                                 scale=cols[:, C_N1 + k:C_N1 + k + 1]).then_inc(hn_hi_done, 1)

            def token_stats(g):
                i0, ni = GROUPS[g]
                e.wait_ge(x_in[g], (48, 16, 16)[g])
                for i in range(i0, i0 + ni):
                    r = P if i < NT - 1 else REST
                    if i >= 2:
                        e.wait_ge(x_ss, i - 1)
                    e.activation(junk[i % 2][0:r, :], xn[0:r, i, :], ACT.Square, accum_out=stat[0:r, i:i + 1])\
                        .then_inc(x_ss, 1)
                r = P if i0 < NT - 1 else REST
                e.wait_ge(x_ms, g + 1)
                e.activation(stat[0:r, NT + i0:NT + i0 + ni], stat[0:r, NT + i0:NT + i0 + ni], ACT.Sqrt)\
                    .then_inc(x_std, 1)

            token_stats(0)
            split_hi(0)
            split_hi(1)
            for g in range(3):
                if g < 2:
                    token_stats(g + 1)
                hn_hi_group(g)

            for c in range(CC):
                for tt, (t0, tw) in enumerate(THIRD):
                    n = NU * c + tt
                    e.wait_ge(unit_done, 2 * n + 2)
                    if n >= 2:
                        e.wait_ge(dve_freed, 2 * (n - 1))
                    e.activation(sig[n % 2][:, 0:tw], psum[:, unit_bank(2 * n + 1), 0:tw], ACT.Sigmoid)\
                        .then_inc(sig_done, 1)
                split_hi(2 * c + 2)
                split_hi(2 * c + 3)
            def qk_hi(u, dst, tt, scale):
                t0, tw = THIRD[tt]
                e.wait_ge(unit_done, u + 1)
                e.activation(dst[:, t0:t0 + tw], psum[:, unit_bank(u), 0:tw], COPY, scale=scale)\
                    .then_inc(evac_hi, 1)

            for j in range(3):
                for tt in range(NU):
                    if j < 2:
                        qk_hi(UNIT_Q0 + NU * j + tt, (q_hi, k_hi)[j][0], tt, (SCALE, 1.0)[j])
                split_hi(SLOT_Q0 + j + 2)

            def copy_z(t):
                e.wait_ge(z_done, t + 1)
                if t >= 3:
                    e.wait_ge(logit_done, t - 2)
                e.activation(zs[t % 3][:, :], psum[:, PZ[t % 2], 0:QW], COPY).then_inc(z_copied, 1)

            def exp_log(t):
                b_ = soft[t % 2]
                e.wait_ge(nabs_done, t + 1)
                e.activation(b_[:, :], b_[:, :], ACT.Exp).then_inc(exp_done, 1)
                e.wait_ge(exp_done, t + 1)
                e.activation(b_[:, :], b_[:, :], ACT.Ln, bias=1.0).then_inc(log_done, 1)

            e.preload_act_table_set("natural_log_exp_and_others")
            copy_z(0)
            copy_z(1)
            exp_log(0)
            for h in range(HEADS):
                nfill = fillers(h)
                for g, (i0, ni) in enumerate(GROUPS):
                    u = unit_att(h) + g
                    e.wait_ge(unit_done, u + 1)
                    e.activation(v_hi[:, i0:i0 + ni, :],
                                 psum[:, unit_bank(u), 0:ni * P].rearrange("p (n d) -> p n d", d=DH), COPY)\
                        .then_inc(evac_hi, 1)
                for idx in range(NS):
                    t = h * NS + idx
                    if t + 1 < STEPS:
                        exp_log(t + 1)
                    if t + 2 < STEPS:
                        copy_z(t + 2)
                    e.wait_ge(logit_done, t + 1)
                    e.activation(att_w[t % 2][:, :], att_w[t % 2][:, :], ACT.Exp).then_inc(a_done, 1)
                    if t >= 1 and LAST[(t - 1) % NS]:
                        hh, i = (t - 1) // NS, TILES[(t - 1) % NS][0]
                        e.wait_ge(o_mm, t)
                        e.activation(att_hi[:, hh, QW * i:QW * (i + 1)], psum[:, PO, 0:QW], COPY)\
                            .then_inc(o_hi_done, 1)
                    f = (idx - FILL0 - 2) // 2
                    if (idx - FILL0) % 2 == 0 and 0 <= f < nfill and h < HEADS - 1 and f < 2 * NU:
                        qk_hi(unit_att(h) + NU + f, (q_hi, k_hi)[f // NU][(h + 1) % 2], f % NU,
                              (SCALE, 1.0)[f // NU])
                    j = (idx - FILL0) // 6 - 1
                    if (idx - FILL0) % 6 == 0 and 0 <= j < nfill // NU:
                        split_hi(slot_att(h, j) + 2)
            e.wait_ge(o_mm, STEPS)
            e.activation(att_hi[:, HEADS - 1, T - QW:T], psum[:, PO, 0:QW], COPY).then_inc(o_hi_done, 1)

            RAW_MIX = list(raw_count)

            def gate_evac(c, j):
                t0, tw = THIRD[j % NU]
                u = c * (6 * NU) + (UNIT_MIX + j)
                e.wait_ge(unit_done, u + 1)
                e.activation(gate[:, j // NU, t0:t0 + tw], psum[:, unit_bank(j), 0:tw], ACT.Sigmoid)\
                    .then_inc(act_freed, 1)

            def splits_mix(c, which):
                left = c * (6 * NU) + (UNIT_MIX + (NU * (which + 1) if which < 3 else 6 * NU))
                if which == 0:
                    split_hi_at(0, left, c * 32 + (RAW_MIX[0] + 16))
                if which == 1:
                    e.wait_ge(raw_in[1], c * 48 + (RAW_MIX[1] + 32))
                    e.wait_ge(unit_done, left)
                    e.activation(wh[1][:, 0:HEADS + CC, :], raw[1][:, 0:HEADS + CC, :], COPY)
                    e.activation(raw[1][:, HEADS + CC, :], pool_w[:, bass.ds(c, 1), :].rearrange("p a n -> p (a n)"),
                                 COPY)
                    e.activation(wh[1][:, HEADS + CC, :], pool_w[:, bass.ds(c, 1), :].rearrange("p a n -> p (a n)"),
                                 COPY).then_inc(w_hi_done, 1)
                if which == 2:
                    split_hi_at(0, left, c * 32 + (RAW_MIX[0] + 32))
                if which == 3:
                    split_hi_at(1, left, c * 48 + (RAW_MIX[1] + 48))

            def load_branch_tiles(c):
                e.wait_ge(w_lo_done, c * 4 + (SLOT_MIX + 2))
                for k, kn, w in ((0, HEADS, w_attn_out), (HEADS, CC, w_conv_out)):
                    e.dma_start(raw[1][:, k:k + kn, :],
                                w[0].rearrange("(k p) n -> p k n", p=P)[:, :, bass.ds(c * P, P)])\
                        .then_inc(raw_in[1], 16)

            load_branch_tiles(0)
            for tt, (t0, tw) in enumerate(THIRD):
                e.wait_ge(xc_done, CC * (tt + 1))
                if tt >= 1:
                    e.wait_ge(var_done, tt)
                e.activation(sq_cv[:, :, 0:tw], cv[:, :, t0:t0 + tw], ACT.Square).then_inc(sqc_done, 1)
                gate_evac(0, tt)
            for tt, (t0, tw) in enumerate(THIRD):
                e.wait_ge(var_done, tt + 1)
                e.activation(std_cv[:, t0:t0 + tw], psum[:, (PU[1], PO, PZ[0])[tt], 0:tw], ACT.Sqrt,
                             scale=1.0 / CONV, bias=eps[:, :]).then_inc(stdc_done, 1)
            e.wait_ge(pool_w_in, 16 * GRPS)
            splits_mix(0, 0)
            for j in range(NU, 2 * NU):
                gate_evac(0, j)
            splits_mix(0, 1)
            for j in range(2 * NU, 3 * NU):
                gate_evac(0, j)
            splits_mix(0, 2)
            e.wait_ge(yc_done, CC)
            for cc in range(CC):
                e.activation(cv[:, cc, :], cv[:, cc, :], ACT.Silu, scale=cols[:, C_LG + cc:C_LG + cc + 1],
                             bias=cols[:, C_LB + cc:C_LB + cc + 1]).then_inc(silu_done, 1)
            for cc in range(CC):
                e.wait_ge(silu_done, cc + 1)
                e.activation(s_hi[:, cc, :], cv[:, cc, :], COPY).then_inc(s_hi_done, 1)
            splits_mix(0, 3)
            with e.Fori(1, KC) as c:
                load_branch_tiles(c)
                e.wait_ge(mix_done, c * NU)
                for j in range(3 * NU):
                    gate_evac(c, j)
                    if j % NU == NU - 1:
                        splits_mix(c, j // NU)
                splits_mix(c, 3)

            e.wait_ge(unit_done, UNIT_OUT)
            for tt, (t0, tw) in enumerate(THIRD):
                e.wait_ge(mix_done, NU * (KC - 1) + tt + 1)
                for k in range(0, KC, KC // 2):
                    e.activation(mix_hi[:, k:k + KC // 2, t0:t0 + tw], mixed[:, k:k + KC // 2, t0:t0 + tw], COPY)\
                        .then_inc(mix_hi_done, 1)
            raw_count[0] = RAW_MIX[0] + 32 * KC
            raw_count[1] = RAW_MIX[1] + 48 * KC
            order = [(m, tt) for tt in range(NU) for m in range(2)]

            def h2_copy(i, m, tt):
                t0, tw = THIRD[tt]
                e.wait_ge(unit_done, UNIT_OUT + i + 1)
                if i == 0:
                    e.wait_ge(mix_split, 2 * NU)
                e.activation(h2[:, m, t0:t0 + tw], psum[:, unit_bank(i), 0:tw], COPY).then_inc(act_freed, 1)

            def square_h(m):
                spans = [(0, T)] if m < KC - 1 else SPAN
                for q, (c0, cn) in enumerate(spans):
                    e.wait_ge(res_done, NU * m + (NU if m < KC - 1 else q + 1))
                    if m >= 2 and q == 0:
                        e.wait_ge(ssum_done, m - 1)
                    dst = sq_sum if m == 0 else sq_h
                    e.activation(dst[:, c0:c0 + cn], h2[:, m, c0:c0 + cn], ACT.Square).then_inc(sqh_done, 1)

            for i, (m, tt) in enumerate(order):
                h2_copy(i, m, tt)
            split_hi(SLOT_OUT + 2)
            split_hi(SLOT_OUT + 3)
            for m in range(2, KC):
                for tt in range(NU):
                    h2_copy(NU * m + tt, m, tt)
                split_hi(SLOT_OUT + m + 2)
                if m == 2:
                    square_h(0)
                square_h(m - 1)
            square_h(KC - 1)
            for q, (c0, cn) in enumerate(SPAN):
                e.wait_ge(ss2_done, q + 1)
                e.activation(rstd2[:, c0:c0 + cn], psum[:, PZ[0] + q, 0:cn], ACT.Sqrt, scale=1.0 / DM,
                             bias=eps[:, :]).then_inc(std2_done, 1)
                for k in range(KC):
                    n = q * KC + k
                    e.wait_ge(scaled_done, n + 1)
                    e.activation(hn_hi[:, k, c0:c0 + cn], scaled[n % 2][:, 0:cn], COPY,
                                 scale=cols[:, C_N2 + k:C_N2 + k + 1]).then_inc(hn2_hi_done, 1)

            RAW_FFN = list(raw_count)

            def up_tile(ch, e6, which, u):
                j = ch + which * FC
                tile_n = 2 * ch + which
                if not isinstance(ch, int) or tile_n >= 2:
                    e.wait_ge(conv_done, tile_n - 1)
                if (not isinstance(ch, int) or ch >= 2) and which == 0:
                    e.wait_ge(g_done, ch - 1)
                w2 = cols[:, bass.ds(j + (C_FW + (FTAPS - 1) * 2 * FC), 1)]
                bb = cols[:, bass.ds(j + C_FB, 1)]
                dst = acc[2 * (e6 % 2) + which]
                for tt, (t0, tw) in enumerate(THIRD):
                    e.wait_ge(unit_done, u + (tt + 1))
                    e.activation(up[which][:, FTAPS - 1 + t0:FTAPS - 1 + t0 + tw], psum[:, tt, 0:tw], COPY)
                    last = e.activation(dst[:, t0:t0 + tw], psum[:, tt, 0:tw], ACT.Identity, scale=w2, bias=bb)
                    last.then_inc(act_freed, 1)

            def gelu_and_hi(ch, e6):
                g = acc[2 * (e6 % 2)]
                e.wait_ge(conv_done, 2 * ch + 1)
                e.activation(g[:, :], g[:, :], ACT.Gelu_apprx_tanh).then_inc(gelu_done, 1)
                e.wait_ge(prod_done, ch + 1)
                e.activation(g_hi[:, e6 % RING, :], acc[2 * (e6 % 2) + 1][:, :], COPY).then_inc(g_hi_done, 1)

            def half_body(it6, half, chunks, total_it, last=False):
                u0 = total_it * (2 * HALF_UNITS) + (UNIT_FFN + 2 * NU + half * HALF_UNITS)
                r0 = [total_it * (16 * HALF_SLOTS) + (RAW_FFN[s] + 16 + half * 8 * HALF_SLOTS) for s in range(2)]
                count = 2 * chunks + KC // 2
                for i in range(chunks):
                    e6 = 3 * half + 1 + i
                    for which in range(2):
                        up_tile(it6 + e6, e6, which, u0 + NU * (2 * i + which))
                        s = 2 * i + which
                        split_hi_at(which, u0 + NU * (s + 1), r0[which] + 16 * (s // 2 + 1), 
                                    KC if s + 2 < 2 * chunks else 6)
                    gelu_and_hi(it6 + e6, e6)
                for m in range(KC // 2):
                    s = 2 * chunks + m
                    if last and m >= KC // 2 - 2:
                        break
                    tiles = 6 if s + 2 < count else KC
                    split_hi_at(s % 2, u0 + (2 * NU * chunks + 2 * NU * (m + 1)), r0[s % 2] + 16 * (s // 2 + 1), tiles)

            for which in range(2):
                up_tile(0, 0, which, UNIT_FFN + NU * which)
                split_hi_at(which, slot_left(SLOT_FFN + which), RAW_FFN[which] + 16)
            gelu_and_hi(0, 0)
            with e.Fori(0, FC // 6 - 1) as it:
                for half in range(2):
                    half_body(it * 6, half, 3, it)
            it = FC // 6 - 1
            half_body(it * 6, 0, 3, it)
            half_body(it * 6, 1, 2, it, last=True)

            def std_out(i):
                e.wait_ge(mso_done, i + 1)
                e.activation(stat[:, NT + i:NT + i + 1], stat[:, NT + i:NT + i + 1], ACT.Sqrt).then_inc(stdo_done, 1)

            for i in range(SEQ // P):
                e.wait_ge(ht_done, i + 1)
                if i >= 2:
                    e.wait_ge(sso_done, i - 1)
                e.activation(sq_out[i % 2][:, :].rearrange("p (a n) -> p a n", a=2), psum[:, 2 * (i % 4):2 * (i % 4) + 2, :],
                             ACT.Square, accum_out=stat[:, i:i + 1]).then_inc(sso_done, 1)
                if i >= 1:
                    std_out(i - 1)
            std_out(SEQ // P - 1)

        @block.vector
        def _(e):
            e.wait_ge(masks32_set, 3)
            e.tensor_copy(neg_tri[:, :], mask32[:, 0, :]).then_inc(masks_set, 1)
            e.tensor_copy(neg_rest[:, :], mask32[:, 1, :]).then_inc(masks_set, 1)
            e.wait_ge(cols_t, 3)
            e.tensor_copy(cols[:, :], psum[:, PO, 0:NCOL]).then_inc(cols_set, 1)

            def norm_group(g):
                i0, ni = GROUPS[g]
                r = P if i0 < NT - 1 else REST
                s_in, s_out = stat[0:r, i0:i0 + ni], stat[0:r, NT + i0:NT + i0 + ni]
                e.wait_ge(x_ss, i0 + ni)
                e.tensor_scalar(s_out, s_in, 1.0 / DM, EPS, ALU.mult, ALU.add).then_inc(x_ms, 1)
                e.wait_ge(x_std, g + 1)
                e.reciprocal(s_out, s_out).then_inc(x_rstd, 1)
                e.wait_ge(x_rstd, g + 1)
                for i in range(i0, i0 + ni):
                    e.tensor_scalar(xn[0:r, i, :], xn[0:r, i, :], stat[0:r, NT + i:NT + i + 1], None, ALU.mult)\
                        .then_inc(xn_done, 1)

            def hn_lo_group(g):
                c0, cn = SPAN[g]
                for k in range(KC):
                    n = g * KC + k
                    e.wait_ge(hn_hi_done, n + 1)
                    e.scalar_tensor_tensor(out=hn_lo[:, k, c0:c0 + cn], in0=psum[:, 3 + n % 4, 0:cn],
                                           scalar=cols[:, C_N1 + k:C_N1 + k + 1],
                                           in1=hn_hi[:, k, c0:c0 + cn].bitcast(f32),
                                           op0=ALU.mult, op1=ALU.subtract).then_inc(hn_done, 1)

            norm_group(0)
            for g in range(3):
                if g < 2:
                    norm_group(g + 1)
                hn_lo_group(g)

            def glu_third(c, tt):
                t0, tw = THIRD[tt]
                n = NU * c + tt
                e.wait_ge(sig_done, n + 1)
                e.tensor_tensor(glu[:, c, TAPS - 1 + t0:TAPS - 1 + t0 + tw], psum[:, unit_bank(2 * n), 0:tw],
                                sig[n % 2][:, 0:tw], ALU.mult).then_inc(dve_freed, 2)

            def conv_tap(i):
                c, tap = i // TAPS, i % TAPS
                w = cols[:, C_CW + tap * CC + c:C_CW + tap * CC + c + 1]
                src = glu[:, c, tap:tap + T]
                if tap == 0:
                    e.wait_ge(dve_freed, 2 * NU * (c + 1))
                    if c == 0:
                        e.wait_ge(glu_pad_set, 1)
                    e.tensor_scalar(cv[:, c, :], src, w, cols[:, C_CB + c:C_CB + c + 1], ALU.mult, ALU.add)\
                        .then_inc(conv_chain, 1)
                else:
                    e.wait_ge(conv_chain, i)
                    e.scalar_tensor_tensor(out=cv[:, c, :], in0=src, scalar=w, in1=cv[:, c, :],
                                           op0=ALU.mult, op1=ALU.add).then_inc(conv_chain, 1)

            taps = [0]

            def conv_taps(n):
                for i in range(taps[0], min(taps[0] + n, TAPS * CC)):
                    conv_tap(i)
                taps[0] = min(taps[0] + n, TAPS * CC)

            for tt in range(NU):
                glu_third(0, tt)
            for c in range(1, CC):
                for tt in range(NU):
                    conv_taps(5)
                    glu_third(c, tt)
            hi_seen = [0]

            def qk_lo(u, dst, hi, tt, scale):
                t0, tw = THIRD[tt]
                hi_seen[0] += 1
                e.wait_ge(evac_hi, hi_seen[0])
                e.scalar_tensor_tensor(out=dst[:, t0:t0 + tw], in0=psum[:, unit_bank(u), 0:tw], scalar=scale,
                                       in1=hi[:, t0:t0 + tw].bitcast(f32), op0=ALU.mult, op1=ALU.subtract)\
                    .then_inc(dve_freed, 1)

            def copy_unit(u, dst):
                e.wait_ge(unit_done, u + 1)
                e.tensor_copy(dst, psum[:, unit_bank(u), 0:dst.shape[-1]]).then_inc(dve_freed, 1)

            for j in range(3):
                for tt, (t0, tw) in enumerate(THIRD):
                    u = UNIT_Q0 + NU * j + tt
                    if j < 2:
                        qk_lo(u, (q_lo, k_lo)[j][0], (q_hi, k_hi)[j][0], tt, (SCALE, 1.0)[j])
                    else:
                        copy_unit(u, vt[:, t0:t0 + tw])
                    conv_taps(3)

            def neg_abs(t):
                e.wait_ge(z_copied, t + 1)
                e.scalar_tensor_tensor(out=soft[t % 2][:, :], in0=zs[t % 3][:, :], scalar=-1.0, in1=zs[t % 3][:, :],
                                       op0=ALU.mult, op1=ALU.min).then_inc(nabs_done, 1)

            seen_masks = [0, 0]

            def softplus_split(t):
                e.wait_ge(log_done, t + 1)
                if t >= 1:
                    e.wait_ge(sp_split, t)
                e.scalar_tensor_tensor(out=sp[:, :], in0=zs[t % 3][:, :], scalar=0.0, in1=soft[t % 2][:, :],
                                       op0=ALU.max, op1=ALU.add).then_inc(sp_done, 1)
                e.wait_ge(sp_done, t + 1)
                if MASKED[t % NS]:
                    seen_masks[0] += 1
                    e.wait_ge(sp_masked, seen_masks[0])
                e.tensor_copy(sp_hi[t % 2][:, :], sp[:, :]).then_inc(sp_hi_done, 1)
                e.wait_ge(sp_hi_done, t + 1)
                e.tensor_tensor(sp_lo[t % 2][:, :], sp[:, :], sp_hi[t % 2][:, :].bitcast(f32), ALU.subtract)\
                    .then_inc(sp_split, 1)

            neg_abs(0)
            neg_abs(1)
            softplus_split(0)
            for h in range(HEADS):
                nfill = fillers(h)
                for g, (i0, ni) in enumerate(GROUPS):
                    u = unit_att(h) + g
                    hi_seen[0] += 1
                    e.wait_ge(evac_hi, hi_seen[0])
                    e.tensor_tensor(v_lo[:, i0:i0 + ni, :],
                                    psum[:, unit_bank(u), 0:ni * P].rearrange("p (n d) -> p n d", d=DH),
                                    v_hi[:, i0:i0 + ni, :].bitcast(f32), ALU.subtract).then_inc(dve_freed, 1)
                for idx in range(NS):
                    t = h * NS + idx
                    e.wait_ge(u_done, t + 1)
                    if t >= 2:
                        e.wait_ge(a_split, t - 1)
                    e.tensor_tensor(att_w[t % 2][:, :], psum[:, PU[(HEADS * h + TILES[idx][0]) % 2], 0:QW],
                                    zs[t % 3][:, :], ALU.add).then_inc(logit_done, 1)
                    if t + 1 < STEPS:
                        softplus_split(t + 1)
                    if t + 2 < STEPS:
                        neg_abs(t + 2)
                    conv_taps(1)
                    e.wait_ge(a_done, t + 1)
                    if MASKED[idx]:
                        seen_masks[1] += 1
                        e.wait_ge(a_masked, seen_masks[1])
                    if t >= 2:
                        e.wait_ge(o_mm, t - 1)
                    e.tensor_copy(a_hi[t % 2][:, :], att_w[t % 2][:, :]).then_inc(a_hi_done, 1)
                    if t >= 1 and LAST[(t - 1) % NS]:
                        hh, i = (t - 1) // NS, TILES[(t - 1) % NS][0]
                        n_o = hh * (T // QW) + i
                        e.wait_ge(o_hi_done, n_o + 1)
                        e.tensor_tensor(att_lo[:, hh, QW * i:QW * (i + 1)], psum[:, PO, 0:QW],
                                        att_hi[:, hh, QW * i:QW * (i + 1)].bitcast(f32), ALU.subtract)\
                            .then_inc(o_evac, 1)
                    f = (idx - FILL0 - 2) // 2
                    if (idx - FILL0) % 2 == 0 and 0 <= f < nfill:
                        u = unit_att(h) + NU + f
                        t0, tw = THIRD[f % NU]
                        if h == HEADS - 1:
                            copy_unit(u, pool_in[:, f // NU, LEFT + t0:LEFT + t0 + tw])
                        elif f < 2 * NU:
                            p_ = (h + 1) % 2
                            qk_lo(u, (q_lo, k_lo)[f // NU][p_], (q_hi, k_hi)[f // NU][p_], f % NU,
                                  (SCALE, 1.0)[f // NU])
                        else:
                            copy_unit(u, vt[:, t0:t0 + tw])
            n_o = HEADS * (T // QW)
            e.wait_ge(o_hi_done, n_o)
            e.tensor_tensor(att_lo[:, HEADS - 1, T - QW:T], psum[:, PO, 0:QW],
                            att_hi[:, HEADS - 1, T - QW:T].bitcast(f32), ALU.subtract).then_inc(o_evac, 1)

            for tt, (t0, tw) in enumerate(THIRD):
                e.wait_ge(mu_done, tt + 1)
                for cc in range(CC):
                    e.scalar_tensor_tensor(out=cv[:, cc, t0:t0 + tw], in0=psum[:, (PZ[0], PZ[1], PU[0])[tt], 0:tw],
                                           scalar=-1.0 / CONV, in1=cv[:, cc, t0:t0 + tw],
                                           op0=ALU.mult, op1=ALU.add).then_inc(xc_done, 1)
            chained = [0]

            def link(ins):
                ins.then_inc(win_chain, 1)
                chained[0] += 1
                e.wait_ge(win_chain, chained[0])

            link(e.memset(win[0][:, 0:LEFT], 0.0))
            link(e.memset(win[1][:, 0:LEFT], 0.0))
            e.wait_ge(cnt_set, 1)
            for g in range(GRPS):
                part = inv_cnt[GC * (g % 2):GC * (g % 2) + GC, g // 2, :]
                link(e.tensor_scalar(part, part, float(WINDOWS[g]), None, ALU.min))
            link(e.reciprocal(inv_cnt[:, :, :], inv_cnt[:, :, :]))
            e.wait_ge(pool_pad_set, 1)
            for c in range(CC):
                lo_w, hi_w = WINDOWS[2 * c], WINDOWS[2 * c + 1]
                cur, w_ = pool_in[:, c, :], 1
                flip = 0
                while w_ < lo_w:
                    dst = win[flip]
                    link(e.tensor_tensor(dst[:, LEFT:LEFT + T], cur[:, LEFT:LEFT + T], cur[:, LEFT - w_:LEFT - w_ + T],
                                         ALU.add))
                    cur, flip, w_ = dst, 1 - flip, 2 * w_
                dst = win[flip]
                link(e.tensor_tensor(dst[GC:P, LEFT:LEFT + T], cur[GC:P, LEFT:LEFT + T],
                                     cur[GC:P, LEFT - w_:LEFT - w_ + T], ALU.add))
                link(e.tensor_copy(dst[0:GC, LEFT:LEFT + T], cur[0:GC, LEFT:LEFT + T]))
                link(e.tensor_tensor(dst[:, LEFT:2 * LEFT], dst[:, LEFT:2 * LEFT], inv_cnt[:, c, :], ALU.mult))
                link(e.tensor_tensor(dst[:, LEFT:2 * LEFT], dst[:, LEFT:2 * LEFT], pool_in[:, c, LEFT:2 * LEFT],
                                     ALU.subtract))
                link(e.scalar_tensor_tensor(out=dst[:, 2 * LEFT:LEFT + T], in0=dst[:, 2 * LEFT:LEFT + T],
                                            scalar=inv_cnt[:, c, LEFT - 1:LEFT], in1=pool_in[:, c, 2 * LEFT:LEFT + T],
                                            op0=ALU.mult, op1=ALU.subtract))
                link(e.tensor_copy(pooled_hi[:, c, :], dst[:, LEFT:LEFT + T]))
                ins = e.tensor_tensor(pooled_lo[:, c, :], dst[:, LEFT:LEFT + T], pooled_hi[:, c, :].bitcast(f32),
                                      ALU.subtract)
                link(ins)
            for tt, (t0, tw) in enumerate(THIRD):
                e.wait_ge(stdc_done, tt + 1)
                e.reciprocal(std_cv[:, t0:t0 + tw], std_cv[:, t0:t0 + tw]).then_inc(rstdc_done, 1)
            e.wait_ge(rstdc_done, NU)
            for cc in range(CC):
                e.tensor_tensor(cv[:, cc, :], cv[:, cc, :], std_cv[:, :], ALU.mult).then_inc(yc_done, 1)
            for cc in range(CC):
                e.wait_ge(s_hi_done, cc + 1)
                e.tensor_tensor(s_lo[:, cc, :], cv[:, cc, :], s_hi[:, cc, :].bitcast(f32), ALU.subtract)\
                    .then_inc(s_ready, 1)

            def mix_chunk(c):
                bc = cols[:, bass.ds(c + C_BC, 1)]
                ps = cols[:, bass.ds(c + C_PS, 1)]
                for tt, (t0, tw) in enumerate(THIRD):
                    g0, g1, g2 = (gate[:, br, t0:t0 + tw] for br in range(3))
                    u = c * (6 * NU) + (UNIT_MIX + 3 * NU + 3 * tt)
                    if tt == 0:
                        e.wait_ge(act_freed, c * (3 * NU) + 3 * NU)
                    e.wait_ge(unit_done, u + 1)
                    e.tensor_tensor(g2, psum[:, 0, 0:tw], g2, ALU.mult).then_inc(dve_freed, 1)
                    e.wait_ge(unit_done, u + 2)
                    e.scalar_tensor_tensor(out=g1, in0=psum[:, 1, 0:tw], scalar=ps, in1=g1,
                                           op0=ALU.mult, op1=ALU.mult).then_inc(dve_freed, 1)
                    e.wait_ge(dve_freed, c * (3 * NU) + (DVE_MIX + 3 * tt + 2))
                    e.tensor_tensor(g1, g1, g2, ALU.add).then_inc(mix_chain, 1)
                    e.wait_ge(unit_done, u + 3)
                    e.scalar_tensor_tensor(out=g0, in0=psum[:, 2, 0:tw], scalar=bc, in1=g0,
                                           op0=ALU.add, op1=ALU.mult).then_inc(dve_freed, 1)
                    e.wait_ge(dve_freed, c * (3 * NU) + (DVE_MIX + 3 * tt + 3))
                    e.wait_ge(mix_chain, c * NU + (tt + 1))
                    e.tensor_tensor(mixed[:, bass.ds(c, 1), t0:t0 + tw].rearrange("p a n -> p (a n)"), g0, g1, ALU.add)\
                        .then_inc(mix_done, 1)

            with e.Fori(0, KC) as c:
                mix_chunk(c)

            for tt, (t0, tw) in enumerate(THIRD):
                for b_, k in enumerate(range(0, KC, KC // 2)):
                    e.wait_ge(mix_hi_done, 2 * tt + b_ + 1)
                    e.tensor_tensor(mix_lo[:, k:k + KC // 2, t0:t0 + tw], mixed[:, k:k + KC // 2, t0:t0 + tw],
                                    mix_hi[:, k:k + KC // 2, t0:t0 + tw].bitcast(f32), ALU.subtract)\
                        .then_inc(mix_split, 1)

            for m in range(KC):
                for g, (c0, cn) in enumerate(SPAN):
                    n = NU * m + g
                    e.wait_ge(xt2_done, n + 1)
                    e.wait_ge(act_freed, ACT_OUT + (2 * NU if m < 2 else NU * (m + 1)))
                    e.tensor_tensor(h2[:, m, c0:c0 + cn], h2[:, m, c0:c0 + cn], psum[:, PZ[0] + n % 5, 0:cn], ALU.add)\
                        .then_inc(res_done, 1)
                if m >= 2:
                    mm = m - 1
                    e.wait_ge(sqh_done, mm + 1)
                    if mm >= 2:
                        e.wait_ge(ssum_done, mm - 1)
                    e.tensor_tensor(sq_sum[:, :], sq_sum[:, :], sq_h[:, :], ALU.add).then_inc(ssum_done, 1)
            for q, (c0, cn) in enumerate(SPAN):
                e.wait_ge(sqh_done, KC - 1 + q + 1)
                if q == 0:
                    e.wait_ge(ssum_done, KC - 2)
                e.tensor_tensor(sq_sum[:, c0:c0 + cn], sq_sum[:, c0:c0 + cn], sq_h[:, c0:c0 + cn], ALU.add)\
                    .then_inc(ssum_done, 1)
            for q, (c0, cn) in enumerate(SPAN):
                e.wait_ge(std2_done, q + 1)
                e.reciprocal(rstd2[:, c0:c0 + cn], rstd2[:, c0:c0 + cn]).then_inc(rstd2_done, 1)
                e.wait_ge(rstd2_done, q + 1)

                def lo_of(n):
                    k = n % KC
                    e.wait_ge(hn2_hi_done, n + 1)
                    e.scalar_tensor_tensor(out=hn_lo[:, k, c0:c0 + cn], in0=scaled[n % 2][:, 0:cn],
                                           scalar=cols[:, C_N2 + k:C_N2 + k + 1],
                                           in1=hn_hi[:, k, c0:c0 + cn].bitcast(f32),
                                           op0=ALU.mult, op1=ALU.subtract).then_inc(hn2_done, 1)

                for k in range(KC):
                    n = q * KC + k
                    if n >= 2:
                        e.wait_ge(hn2_done, n - 1)
                    e.tensor_tensor(scaled[n % 2][:, 0:cn], h2[:, k, c0:c0 + cn], rstd2[:, c0:c0 + cn], ALU.mult)\
                        .then_inc(scaled_done, 1)
                    if k >= 1:
                        lo_of(n - 1)
                lo_of(q * KC + KC - 1)

            for s in range(2):
                e.memset(up[s][:, 0:FTAPS - 1], 0.0).then_inc(up_pads_set, 1)
            e.wait_ge(up_pads_set, 2)

            def conv3(ch, e6, which):
                j = ch + which * FC
                tile_n = 2 * ch + which
                a_ = acc[2 * (e6 % 2) + which]
                e.wait_ge(act_freed, tile_n * NU + (ACT_FFN + NU))
                w1 = cols[:, bass.ds(j + (C_FW + 2 * FC), 1)]
                w0 = cols[:, bass.ds(j + C_FW, 1)]
                e.scalar_tensor_tensor(out=a_[:, :], in0=up[which][:, 1:1 + T], scalar=w1, in1=a_[:, :],
                                       op0=ALU.mult, op1=ALU.add).then_inc(tap_chain, 1)
                e.wait_ge(tap_chain, tile_n + 1)
                e.scalar_tensor_tensor(out=a_[:, :], in0=up[which][:, 0:T], scalar=w0, in1=a_[:, :],
                                       op0=ALU.mult, op1=ALU.add).then_inc(conv_done, 1)

            def chunk(ch, e6):
                conv3(ch, e6, 0)
                conv3(ch, e6, 1)
                g, v = acc[2 * (e6 % 2)], acc[2 * (e6 % 2) + 1]
                e.wait_ge(gelu_done, ch + 1)
                e.wait_ge(conv_done, 2 * ch + 2)
                e.tensor_tensor(v[:, :], g[:, :], v[:, :], ALU.mult).then_inc(prod_done, 1)
                e.wait_ge(g_hi_done, ch + 1)
                e.tensor_tensor(g_lo[:, e6 % RING, :], v[:, :], g_hi[:, e6 % RING, :].bitcast(f32), ALU.subtract)\
                    .then_inc(g_done, 1)

            def downs(u, first):
                for m in range(KC):
                    for tt, (t0, tw) in enumerate(THIRD):
                        e.wait_ge(unit_done, u + (NU * m + tt + 1))
                        e.tensor_tensor(h2[:, m, t0:t0 + tw], h2[:, m, t0:t0 + tw], psum[:, tt, 0:tw], ALU.add)\
                            .then_inc(dve_freed, 1)

            def half_body(it, half, chunks):
                for i in range(chunks):
                    e6 = 3 * half + 1 + i
                    chunk(it * 6 + e6, e6)
                downs(it * (2 * HALF_UNITS) + (UNIT_FFN + 2 * NU + half * HALF_UNITS + 2 * NU * chunks), it)

            chunk(0, 0)
            with e.Fori(0, FC // 6 - 1) as it:
                half_body(it, 0, 3)
                half_body(it, 1, 3)
            half_body(FC // 6 - 1, 0, 3)
            half_body(FC // 6 - 1, 1, 2)

            def finish(i):
                e.wait_ge(stdo_done, i + 1)
                e.reciprocal(stat[:, NT + i:NT + i + 1], stat[:, NT + i:NT + i + 1]).then_inc(rstdo_done, 1)
                e.wait_ge(rstdo_done, i + 1)
                if i == 0:
                    e.wait_ge(final_g_in, 16)
                if i >= 3:
                    e.wait_ge(stored[i % 3], 16 * (i // 3))
                e.scalar_tensor_tensor(out=y_out[i % 3][:, :].rearrange("p (a n) -> p a n", a=2),
                                       in0=psum[:, 2 * (i % 4):2 * (i % 4) + 2, :], scalar=stat[:, NT + i:NT + i + 1],
                                       in1=final_g[:, :].rearrange("p (a n) -> p a n", a=2),
                                       op0=ALU.mult, op1=ALU.mult).then_inc(y_done, 1)

            for i in range(SEQ // P):
                e.wait_ge(sso_done, i + 1)
                e.tensor_scalar(stat[:, NT + i:NT + i + 1], stat[:, i:i + 1], 1.0 / DM, EPS, ALU.mult, ALU.add)\
                    .then_inc(mso_done, 1)
                if i >= 1:
                    finish(i - 1)
            finish(SEQ // P - 1)

        @block.tensor
        def _(e):
            def passes(dst, w_pair, r_pair, start, stop):
                (a_h, a_l), (r_h, r_l) = w_pair, r_pair
                e.matmul(dst, a_h, r_h, start=start, stop=False)
                e.matmul(dst, a_h, r_l, start=False, stop=False)
                return e.matmul(dst, a_l, r_h, start=False, stop=stop)

            def tiles(s, ks, rhs, tt, bank, j0=0, ks_rhs=None):
                t0, tw = THIRD[tt]
                for k in ks:
                    last = passes(psum[:, bank, 0:tw], (wh[s][:, k, :], wl[s][:, k, :]),
                                  (rhs[0][:, k, t0:t0 + tw], rhs[1][:, k, t0:t0 + tw]),
                                  start=k == 0, stop=k == KC - 1)
                return last

            hn = (hn_hi, hn_lo)

            e.wait_ge(params_in, 16 * 11)
            e.wait_ge(ident_set, 4)
            at = 0
            for slot, count in ((0, C_FW), (1, P), (2, NCOL - C_FW - P)):
                e.transpose(psum[:, PO, at:at + count], rows[0:count, slot, :], ident[0:count, 0:count])\
                    .then_inc(cols_t, 1)
                at += count

            for g, (i0, ni) in enumerate(GROUPS):
                e.wait_ge(xn_done, i0 + ni)
                for k in range(KC):
                    n = g * KC + k
                    if n >= 4:
                        e.wait_ge(hn_done, n - 3)
                    for i in range(i0, i0 + ni):
                        r = P if i < NT - 1 else REST
                        last = e.transpose(psum[:, 3 + n % 4, (i - i0) * P:(i - i0) * P + r],
                                           xn[0:r, i, k * P:(k + 1) * P], ident[0:r, 0:r])
                    last.then_inc(xt_done, 1)

            for c in range(CC):
                for tt in range(NU):
                    if c == 0:
                        e.wait_ge(hn_done, KC * (tt + 1))
                    for s in range(2):
                        u = 2 * NU * c + 2 * tt + s
                        if tt == 0:
                            e.wait_ge(w_lo_done, 2 * c + s + 1)
                        if u >= NU:
                            e.wait_ge(dve_freed, u - NU + 1)
                        last = tiles(s, range(KC), hn, tt, unit_bank(u))
                        last.then_inc(unit_done, 1)

            def half_unit(n, u, tt, part, freed, count, done=False):
                s = n % 2
                if part == 0:
                    if tt == 0:
                        e.wait_ge(w_lo_done, n + 1)
                    e.wait_ge(freed, count)
                half = KC // 2
                last = tiles(s, range(part * half, (part + 1) * half), hn, tt, unit_bank(u))
                if part == 1:
                    last.then_inc(unit_done, 1)

            for j in range(3):
                for tt in range(NU):
                    u = UNIT_Q0 + NU * j + tt
                    for part in range(2):
                        half_unit(SLOT_Q0 + j, u, tt, part, dve_freed, u - NU + 1)

            def scores(t):
                h, (i, n) = t // NS, TILES[t % NS]
                p_ = h % 2
                if t >= 2:
                    e.wait_ge(z_copied, t - 1)
                if t % NS == 0:
                    e.wait_ge(dve_freed, UNIT_Q0 + 2 * NU if h == 0 else unit_att(h - 1) + 3 * NU)
                    e.wait_ge(kv_pads_set, 5)
                ks, qs = slice(n * P, (n + 1) * P), slice(i * QW, (i + 1) * QW)
                passes(psum[:, PZ[t % 2], 0:QW], (k_hi[p_][:, ks], k_lo[p_][:, ks]), (q_hi[p_][:, qs], q_lo[p_][:, qs]),
                       True, True).then_inc(z_done, 1)

            def weigh(t):
                i, n = TILES[t % NS]
                e.wait_ge(a_split, t + 1)
                if FIRST[t % NS]:
                    n_o = (t // NS) * (T // QW) + i
                    if n_o >= 1:
                        e.wait_ge(o_evac, n_o)
                if t % NS == 0:
                    e.wait_ge(dve_freed, unit_att(t // NS) + NU)
                passes(psum[:, PO, 0:QW], (v_hi[:, n, :], v_lo[:, n, :]), (a_hi[t % 2][:, :], a_lo[t % 2][:, :]),
                       FIRST[t % NS], LAST[t % NS]).then_inc(o_mm, 1)

            scores(0)
            scores(1)
            e.wait_ge(masks_set, 2)
            for h in range(HEADS):
                nfill = fillers(h)
                if h >= 1:
                    weigh(h * NS - 1)
                e.wait_ge(dve_freed, unit_att(h))
                for g, (i0, ni) in enumerate(GROUPS):
                    u = unit_att(h) + g
                    for i in range(i0, i0 + ni):
                        last = e.transpose(psum[:, unit_bank(u), (i - i0) * P:(i - i0 + 1) * P], vt[:, i * P:(i + 1) * P],
                                           ident[:, :])
                    last.then_inc(unit_done, 1)
                for idx in range(NS):
                    t = h * NS + idx
                    bank = psum[:, PU[(HEADS * h + TILES[idx][0]) % 2], 0:QW]
                    e.wait_ge(sp_split, t + 1)
                    e.matmul(bank, neg_tri[:, :], sp_hi[t % 2][:, :], start=FIRST[idx], stop=False,
                             skip_group_check=True)
                    e.matmul(bank, neg_tri[:, :], sp_lo[t % 2][:, :], start=False, stop=True,
                             skip_group_check=True).then_inc(u_done, 1)
                    f = (idx - FILL0) // 2
                    if idx >= FILL0 and f < nfill:
                        u = unit_att(h) + NU + f
                        half_unit(slot_att(h, f // NU), u, f % NU, (idx - FILL0) % 2, dve_freed, u - NU + 1)
                    if t + 2 < STEPS:
                        scores(t + 2)
                    if not LAST[idx]:
                        e.wait_ge(logit_done, t + 1)
                        e.matmul(bank, neg_rest[:, :], sp_hi[t % 2][:, :], start=False, stop=False,
                                 skip_group_check=True)
                        e.matmul(bank, neg_rest[:, :], sp_lo[t % 2][:, :], start=False, stop=True,
                                 skip_group_check=True)
                    if idx >= 1:
                        weigh(t - 1)
            weigh(STEPS - 1)

            def freed_in_mix(c, j):
                if j < NU or j >= 4 * NU:
                    e.wait_ge(dve_freed, c * (3 * NU) + (DVE_MIX + (j - NU + 1 if j < NU else j - 4 * NU + 1)))
                else:
                    e.wait_ge(act_freed, c * (3 * NU) + (j - NU + 1))

            def gate_unit(c, br, tt):
                n = c * 4 + (SLOT_MIX + br)
                j = NU * br + tt
                if tt == 0:
                    e.wait_ge(w_lo_done, n + 1)
                freed_in_mix(c, j)
                last = tiles(br % 2, range(KC), hn, tt, unit_bank(j))
                last.then_inc(unit_done, 1)

            def branch_units(c, first):
                n = c * 4 + (SLOT_MIX + 3)
                e.wait_ge(w_lo_done, n + 1)
                for tt, (t0, tw) in enumerate(THIRD):
                    j = 3 * NU + 3 * tt
                    ts = slice(t0, t0 + tw)
                    freed_in_mix(c, j)
                    for k in range(HEADS):
                        last = passes(psum[:, 0, 0:tw], (wh[1][:, k, :], wl[1][:, k, :]),
                                      (att_hi[:, k, ts], att_lo[:, k, ts]), k == 0, k == HEADS - 1)
                    last.then_inc(unit_done, 1)
                    freed_in_mix(c, j + 1)
                    pc = first
                    last = passes(psum[:, 1, 0:tw], (wh[1][:, HEADS + CC, :], wl[1][:, HEADS + CC, :]),
                                  (pooled_hi[:, pc, ts], pooled_lo[:, pc, ts]), True, True)
                    last.then_inc(unit_done, 1)
                    freed_in_mix(c, j + 2)
                    for k in range(CC):
                        last = passes(psum[:, 2, 0:tw], (wh[1][:, HEADS + k, :], wl[1][:, HEADS + k, :]),
                                      (s_hi[:, k, ts], s_lo[:, k, ts]), k == 0, k == CC - 1)
                    last.then_inc(unit_done, 1)

            e.wait_ge(conv_chain, TAPS * CC)
            for tt, (t0, tw) in enumerate(THIRD):
                for cc in range(CC):
                    last = e.matmul(psum[:, (PZ[0], PZ[1], PU[0])[tt], 0:tw], ones[:, :], cv[:, cc, t0:t0 + tw],
                                    start=cc == 0, stop=cc == CC - 1)
                last.then_inc(mu_done, 1)
            for tt, (t0, tw) in enumerate(THIRD):
                gate_unit(0, 0, tt)
                e.wait_ge(sqc_done, tt + 1)
                if tt == 1:
                    e.wait_ge(o_evac, HEADS * (T // QW))
                for cc in range(CC):
                    last = e.matmul(psum[:, (PU[1], PO, PZ[0])[tt], 0:tw], ones[:, :], sq_cv[:, cc, 0:tw],
                                    start=cc == 0, stop=cc == CC - 1)
                last.then_inc(var_done, 1)
            for br in (1, 2):
                for tt in range(NU):
                    gate_unit(0, br, tt)
            e.wait_ge(s_ready, CC)
            branch_units(0, 0)
            for pc in range(CC):
                with e.Fori(max(1, pc * KC // CC), (pc + 1) * KC // CC) as c:
                    for br in range(3):
                        for tt in range(NU):
                            gate_unit(c, br, tt)
                    branch_units(c, pc)

            def out_unit(i, m, tt):
                n = SLOT_OUT + m
                if i < 2 * NU:
                    for b_ in range(2):
                        e.wait_ge(mix_split, 2 * tt + b_ + 1)
                if i < NU:
                    e.wait_ge(dve_freed, DVE_FFN - NU + i + 1)
                else:
                    e.wait_ge(act_freed, ACT_OUT + i - NU + 1)
                e.wait_ge(w_lo_done, n + 1)
                last = tiles(m % 2, range(KC), (mix_hi, mix_lo), tt, unit_bank(i))
                last.then_inc(unit_done, 1)

            def x_transposes(m):
                for g, (i0, ni) in enumerate(GROUPS):
                    n = NU * m + g
                    if n >= 5:
                        e.wait_ge(res_done, n - 4)
                    for i in range(i0, i0 + ni):
                        if i < NT - 1:
                            last = e.transpose(psum[:, PZ[0] + n % 5, (i - i0) * P:(i - i0 + 1) * P],
                                               x_again[:, i, m * P:(m + 1) * P], ident[:, :])
                        else:
                            last = e.transpose(psum[:, PZ[0] + n % 5, 0:REST], x_last[0:REST, m * P:(m + 1) * P],
                                               ident[0:REST, 0:REST])
                    last.then_inc(xt2_done, 1)

            i = 0
            for tt in range(NU):
                for m in range(2):
                    out_unit(i, m, tt)
                    i += 1
            e.wait_ge(x_again_in, 64)
            x_transposes(0)
            x_transposes(1)
            for m in range(2, KC):
                for tt in range(NU):
                    out_unit(i, m, tt)
                    i += 1
                x_transposes(m)
            for q, (c0, cn) in enumerate(SPAN):
                e.wait_ge(ssum_done, KC - 2 + q + 1)
                e.wait_ge(res_done, NU * KC)
                e.matmul(psum[:, PZ[0] + q, 0:cn], ones[:, :], sq_sum[:, c0:c0 + cn], start=True, stop=True)\
                    .then_inc(ss2_done, 1)

            def up_tile(n, which, ups_before, downs_before, first):
                e.wait_ge(w_lo_done, n + 1)
                for tt in range(NU):
                    if first:
                        e.wait_ge(dve_freed, downs_before + (tt + 1 - NU))
                    e.wait_ge(act_freed, ups_before + (tt + 1 - NU))
                    last = tiles(which, range(KC), hn, tt, tt)
                    last.then_inc(unit_done, 1)

            def half_body(it, half, chunks):
                n0 = it * (2 * HALF_SLOTS) + (SLOT_FFN + 2 + half * HALF_SLOTS)
                ups = it * (2 * HALF_UP) + (ACT_FFN + 2 * NU + half * HALF_UP)
                dns = it * (2 * HALF_DOWN) + (DVE_FFN + half * HALF_DOWN)
                for i in range(chunks):
                    for which in range(2):
                        s = 2 * i + which
                        up_tile(n0 + s, which, ups + NU * s, dns, s == 0)
                e.wait_ge(g_done, it * 6 + (3 * half + 3))
                for m in range(KC):
                    s = (m // 2) % 2
                    if m % 2 == 0:
                        e.wait_ge(w_lo_done, n0 + (2 * chunks + m // 2 + 1))
                    for tt, (t0, tw) in enumerate(THIRD):
                        if m == 0:
                            e.wait_ge(act_freed, ups + (2 * NU * chunks - NU + tt + 1))
                        else:
                            e.wait_ge(dve_freed, dns + (NU * (m - 1) + tt + 1))
                        for k in range(3):
                            r = (3 * half + k) % RING
                            last = passes(psum[:, tt, 0:tw], (wh[s][:, 2 * k + m % 2, :], wl[s][:, 2 * k + m % 2, :]),
                                          (g_hi[:, r, t0:t0 + tw], g_lo[:, r, t0:t0 + tw]), k == 0, k == 2)
                        last.then_inc(unit_done, 1)

            for which in range(2):
                n = SLOT_FFN + which
                e.wait_ge(w_lo_done, n + 1)
                for tt in range(NU):
                    if which == 0:
                        e.wait_ge(hn2_done, KC * (tt + 1))
                    e.wait_ge(act_freed, ACT_FFN + NU * (which - 1) + tt + 1)
                    last = tiles(which, range(KC), hn, tt, tt)
                    last.then_inc(unit_done, 1)
            with e.Fori(0, FC // 6 - 1) as it:
                half_body(it, 0, 3)
                half_body(it, 1, 3)
            half_body(FC // 6 - 1, 0, 3)
            half_body(FC // 6 - 1, 1, 2)

            e.wait_ge(dve_freed, DVE_FFN + HALF_DOWN * (FC // 3))
            for i in range(SEQ // P):
                if i >= 4:
                    e.wait_ge(y_done, i - 3)
                for k in range(KC):
                    last = e.transpose(psum[:, 2 * (i % 4) + k // 4, (k % 4) * P:(k % 4 + 1) * P],
                                       h2[:, k, NMETA + i * P:NMETA + (i + 1) * P], ident[:, :])
                last.then_inc(ht_done, 1)


_INS = ["x", "meta", "norm1", "w_in", "conv_dw_w", "conv_dw_b", "conv_ln_g", "conv_ln_b", "w_conv_out", "b_conv_out",
        "w_pool_grp", "pool_scale", "w_attn_out", "w_o", "norm2", "w_up", "ffn_dw_w", "ffn_dw_b", "w_down",
        "final_norm"]


def kernel(**inputs):
    import numpy as _np
    import concourse.bacc as _bacc
    from concourse import mybir as _mybir
    from concourse.bass_utils import run_bass_kernel_spmd as _run

    nc = _bacc.Bacc("TRN2", target_bir_lowering=False, num_devices=1)
    arrays, args = {}, []
    for name in _INS:
        a = _np.ascontiguousarray(inputs[name])
        arrays[f"in_{name}_dram"] = a
        args.append(nc.dram_tensor(f"in_{name}_dram", a.shape, _mybir.dt.from_np(a.dtype), kind="ExternalInput").ap())
    shape = arrays["in_x_dram"].shape
    out = nc.dram_tensor("out_dram", shape, _mybir.dt.float32, kind="ExternalOutput").ap()
    hybrid_trunk_kernel(nc, *args, out)
    r = _run(nc, [arrays], core_ids=[0])
    return r.results[0]["out_dram"]
```

```python
import concourse.bass as bass
from concourse import mybir
from contextlib import ExitStack


def hybrid_trunk_kernel(nc, x, meta, norm1, w_in, conv_dw_w, conv_dw_b, conv_ln_g, conv_ln_b, w_conv_out,
                        b_conv_out, w_pool_grp, pool_scale, w_attn_out, w_o, norm2, w_up, ffn_dw_w,
                        ffn_dw_b, w_down, final_norm, out):
    f32, f32r = mybir.dt.float32, mybir.dt.float32r
    ALU, ACT = mybir.AluOpType, mybir.ActivationFunctionType
    COPY = ACT.Copy

    P = 128
    SEQ, DM = x.shape[1], x.shape[2]
    NMETA = meta.shape[0]
    T = NMETA + SEQ
    KC = DM // P
    NT = -(-T // P)
    TP = NT * P
    REST = T - (NT - 1) * P
    TAPS, CONV = conv_dw_w.shape[1], conv_dw_w.shape[2]
    CC = CONV // P
    GRPS, GC, GOUT = w_pool_grp.shape[1:]
    POOLC = GRPS * GC
    WINDOWS = (2, 4, 8, 16)
    ATTW = w_attn_out.shape[1]
    DH = P
    HEADS = ATTW // DH
    FF = w_down.shape[1]
    FC = FF // P
    FTAPS = ffn_dw_w.shape[1]
    EPS = 1e-6
    SCALE = float(DH) ** -0.5
    COL_POOL = 2 * CONV
    COL_Q = COL_POOL + POOLC
    COL_K, COL_V, COL_GATE = COL_Q + ATTW, COL_Q + 2 * ATTW, COL_Q + 3 * ATTW

    GROUPS = [(i, 3) for i in range(0, NT, 3)]
    THIRD = [(i * P, min(ni * P, T - i * P)) for i, ni in GROUPS]
    NU = len(THIRD)
    TW = THIRD[0][1]
    QW = T // 4
    TILES = [(i, n) for i in range(T // QW) for n in reversed(range((QW * (i + 1) - 2) // P + 1))]
    LAST = [n == 0 for _, n in TILES]
    FIRST = [k == 0 or TILES[k - 1][0] != TILES[k][0] for k in range(len(TILES))]
    MASKED = [P * n + P - 1 >= QW * i for i, n in TILES]
    NS = len(TILES)
    STEPS = NS * HEADS
    MASKED_Z = -1e30
    FILL_STEPS = NS - 3
    VGROUPS = [(i, 3) for i in reversed(range(0, NT, 3))]

    C_N1, C_N2, C_BC, C_PS = 0, KC, 2 * KC, 3 * KC
    C_CB = 4 * KC
    C_LG, C_LB = C_CB + CC, C_CB + 2 * CC
    C_CW = C_CB + 3 * CC
    C_FW = C_CW + TAPS * CC
    C_FB = C_FW + FTAPS * 2 * FC
    NCOL = C_FB + 2 * FC

    SLOT_Q0 = 2 * CC
    SLOT_ATT = SLOT_Q0 + 3
    SLOT_MIX = SLOT_ATT + 3 * (HEADS - 1) + POOLC // P
    SLOT_OUT = SLOT_MIX + 4 * KC
    SLOT_FFN = SLOT_OUT + KC
    HALF_SLOTS = 6 + KC // 2
    SLOT_END = SLOT_FFN + 2 * FC + FC // 3 * (KC // 2)
    UNIT_Q0 = NU * SLOT_Q0
    UNIT_ATT = UNIT_Q0 + 3 * NU
    UNIT_MIX = UNIT_ATT + NU * HEADS + NU * (SLOT_MIX - SLOT_ATT)
    UNIT_OUT = UNIT_MIX + 2 * NU * 3 * KC
    UNIT_FFN = UNIT_OUT + NU * KC
    HALF_UP, HALF_DOWN = 6 * NU, NU * KC
    HALF_UNITS = HALF_UP + HALF_DOWN
    DVE_MIX = UNIT_MIX
    DVE_FFN = DVE_MIX + 3 * NU * KC
    ACT_OUT = 3 * NU * KC
    ACT_FFN = ACT_OUT + NU * KC

    def slot_att(h, j):
        return SLOT_ATT + 3 * h + j

    def unit_att(h):
        return UNIT_ATT + (4 * NU) * h

    def slot_left(n):
        if n < SLOT_Q0:
            return 2 * NU * (n // 2 + 1) - 1 + n % 2
        if n < SLOT_ATT:
            return UNIT_Q0 + NU * (n - SLOT_Q0 + 1)
        if n < SLOT_MIX:
            h = min((n - SLOT_ATT) // 3, HEADS - 1)
            return unit_att(h) + NU + NU * (n - slot_att(h, 0) + 1)
        if n < SLOT_OUT:
            c, j = divmod(n - SLOT_MIX, 4)
            return UNIT_MIX + 6 * NU * c + (NU * (j + 1) if j < 3 else 6 * NU)
        if n < SLOT_FFN:
            return UNIT_OUT + (2 * NU - 1 + n - SLOT_OUT if n < SLOT_OUT + 2 else NU * (n - SLOT_OUT + 1))
        assert n < SLOT_FFN + 2
        return UNIT_FFN + NU * (n - SLOT_FFN + 1)

    def fillers(h):
        return 3 * NU if h < HEADS - 1 else NU * (POOLC // P)

    def fill_bound(h, idx):
        return KC * fillers(h) * min(idx, FILL_STEPS) // FILL_STEPS

    def fill_ended(h, idx):
        return range(fill_bound(h, idx - 1) // KC, fill_bound(h, idx) // KC) if idx >= 1 else range(0)

    def split_pieces(t, lag, parts):
        due = []
        for h in range(HEADS):
            for idx in range(NS):
                for f in fill_ended(h, idx):
                    piece = t - (h * NS + idx + lag)
                    if f % NU == NU - 1 and 0 <= piece < parts:
                        due.append((slot_att(h, f // NU) + 2, piece))
        return due

    B = 4
    ctx = ExitStack()
    with ctx:
        base = [-(-nc.sbuf_base // 32) * 32]

        def place(name, shape, dtype, at):
            return nc.alloc_sbuf_tensor_at(name, shape, dtype, offset=at)

        def take(name, shape, dtype=f32):
            n = B
            for s in shape[1:]:
                n *= s
            at = base[0]
            base[0] += -(-n // 32) * 32
            return place(name, shape, dtype, at)

        ident = take("ident", [P, P])
        ones = take("ones", [P, P])
        neg_tri = take("neg_tri", [P, P], f32r)
        neg_rest = take("neg_rest", [P, P], f32r)
        cols = take("cols", [P, NCOL])
        eps = take("eps", [P, 1])
        stat = take("stat", [P, 4 * NT])
        inv_cnt = take("inv_cnt", [P, CC, WINDOWS[-1]])
        raw = [take(f"raw{s}", [P, KC, P]) for s in range(2)]
        wh = [take(f"wh{s}", [P, KC, P], f32r) for s in range(2)]
        wl = [take(f"wl{s}", [P, KC, P], f32r) for s in range(2)]
        HN = base[0]
        hn_hi = take("hn_hi", [P, KC, T], f32r)
        hn_lo = take("hn_lo", [P, KC, T], f32r)
        ATT = base[0]
        att_hi = take("att_hi", [P, HEADS, T], f32r)
        att_lo = take("att_lo", [P, HEADS, T], f32r)
        R = base[0]
        U, UP = T * B, TP * B

        assert R + 20 * T * B <= nc.sbuf_usable_end, (R, nc.sbuf_usable_end)
        xn = place("xn", [P, NT, DM], f32, R)
        QK = 2 * U + 2 * UP
        q_hi = [place(f"q_hi{s}", [P, T], f32r, R + s * QK) for s in range(2)]
        q_lo = [place(f"q_lo{s}", [P, T], f32r, R + s * QK + U) for s in range(2)]
        k_hi = [place(f"k_hi{s}", [P, TP], f32r, R + s * QK + 2 * U) for s in range(2)]
        k_lo = [place(f"k_lo{s}", [P, TP], f32r, R + s * QK + 2 * U + UP) for s in range(2)]
        R_VT = R + 2 * QK
        vt = place("vt", [P, TP], f32, R_VT)
        R_V = R_VT + UP
        v_hi = place("v_hi", [P, NT, DH], f32r, R_V)
        v_lo = place("v_lo", [P, NT, DH], f32r, R_V + UP)
        R_TMP = R_V + 2 * UP
        W = -(-QW * B // 32) * 32
        zs = [place(f"zs{s}", [P, QW], f32, R_TMP + s * W) for s in range(3)]
        soft = [place(f"soft{s}", [P, QW], f32, R_TMP + (3 + s) * W) for s in range(2)]
        sp = place("sp", [P, QW], f32, R_TMP + 5 * W)
        sp_hi = [place(f"sp_hi{s}", [P, QW], f32r, R_TMP + (6 + s) * W) for s in range(2)]
        sp_lo = [place(f"sp_lo{s}", [P, QW], f32r, R_TMP + (8 + s) * W) for s in range(2)]
        att_w = [place(f"att_w{s}", [P, QW], f32, R_TMP + (10 + s) * W) for s in range(2)]
        a_hi = [place(f"a_hi{s}", [P, QW], f32r, R_TMP + (12 + s) * W) for s in range(2)]
        a_lo = [place(f"a_lo{s}", [P, QW], f32r, R_TMP + (14 + s) * W) for s in range(2)]
        sig = [place(f"sig{s}", [P, TW], f32, R_TMP + s * TW * B) for s in range(2)]
        rows = place("rows", [P, 3, P], f32, R_TMP + 3072)
        junk = [place(f"junk{s}", [P, DM], f32, R_TMP + 4608 + s * DM * B) for s in range(2)]
        mask32 = place("mask32", [P, 2, P], f32, R_TMP + 4608 + 2 * DM * B)
        R_CV = R_TMP + 16 * W
        cv = place("cv", [P, CC, T], f32, R_CV)
        R_PB = R_CV + CC * U
        LEFT = WINDOWS[-1]
        glu = place("glu", [P, CC, TAPS - 1 + T], f32, R_PB)
        assert R_PB + CC * (TAPS - 1 + T) * B <= nc.sbuf_usable_end
        pool_in = place("pool_in", [P, CC, LEFT + T], f32, R_PB)
        s_hi = place("s_hi", [P, CC, T], f32r, R)
        s_lo = place("s_lo", [P, CC, T], f32r, R + 2 * U)
        pooled_hi = place("pooled_hi", [P, CC, T], f32r, R + 4 * U)
        pooled_lo = place("pooled_lo", [P, CC, T], f32r, R + 6 * U)
        gate = place("gate", [P, 3, T], f32, R + 8 * U)
        pool_w = place("pool_w", [P, KC, P], f32, R + 11 * U)
        R_MIX = R + 11 * U + KC * P * B
        mixed = place("mixed", [P, KC, T], f32, R_MIX)
        win = [place(f"win{s}", [P, LEFT + T], f32, R_MIX + s * (LEFT + T) * B) for s in range(2)]
        sq_cv = place("sq_cv", [P, CC, TW], f32, R_MIX + 2 * (LEFT + T) * B)
        std_cv = place("std_cv", [P, T], f32, R_MIX + 2 * (LEFT + T) * B + CC * TW * B)
        assert R_MIX + 2 * (LEFT + T) * B + CC * TW * B + U <= R_CV
        mix_hi = place("mix_hi", [P, KC, T], f32r, HN)
        mix_lo = place("mix_lo", [P, KC, T], f32r, HN + KC * U)
        x_again = place("x_again", [P, NT - 1, DM], f32, ATT)
        h2 = place("h2", [P, KC, T], f32, R)
        x_last = place("x_last", [P, DM], f32, R + 8 * U)
        sq_h = place("sq_h", [P, T], f32, R + 9 * U)
        sq_sum = place("sq_sum", [P, T], f32, R + 10 * U)
        R_T4 = R_MIX
        rstd2 = place("rstd2", [P, T], f32, R_T4)
        scaled = [place(f"scaled{s}", [P, 512], f32, R_T4 + U + s * 2048) for s in range(2)]
        UW = -(-(FTAPS - 1 + T) // 8) * 8
        up = [place(f"up{s}", [P, UW], f32, ATT + s * UW * B) for s in range(2)]
        acc = [place(f"acc{s}", [P, T], f32, ATT + 2 * UW * B + s * U) for s in range(4)]
        final_g = place("final_g", [P, DM], f32, ATT + 2 * UW * B + 4 * U)
        assert 2 * UW * B + 4 * U + DM * B <= 8 * U
        RING = 6
        g_hi = place("g_hi", [P, RING, T], f32r, R + 8 * U)
        g_lo = place("g_lo", [P, RING, T], f32r, R + 14 * U)
        sq_out = [place(f"sq_out{s}", [P, DM], f32, HN + s * DM * B) for s in range(2)]
        y_out = [place(f"y_out{s}", [P, DM], f32, HN + (2 + s) * DM * B) for s in range(3)]

        psum = ctx.enter_context(nc.psum_tensor("psum", [P, 8, 512], f32))
        PZ, PU, PO = [3, 4], [5, 6], 7

        def sem(name):
            return ctx.enter_context(nc.semaphore(name))

        x_in = [sem(f"x_in{g}") for g in range(3)]
        params_in = sem("params_in")
        raw_in = [sem("raw_in0"), sem("raw_in1")]
        pool_w_in = sem("pool_w_in")
        x_again_in = sem("x_again_in")
        final_g_in = sem("final_g_in")
        stored = [sem(f"stored{s}") for s in range(3)]
        ident_set = sem("ident_set")
        masks32_set = sem("masks32_set")
        masks_set = sem("masks_set")
        cols_t = sem("cols_t")
        cols_set = sem("cols_set")
        glu_pad_set = sem("glu_pad_set")
        kv_pads_set = sem("kv_pads_set")
        pool_pad_set = sem("pool_pad_set")
        up_pads_set = sem("up_pads_set")
        pool_w_zeroed = sem("pool_w_zeroed")
        cnt_set = sem("cnt_set")
        x_ss = sem("x_ss")
        x_ms = sem("x_ms")
        x_std = sem("x_std")
        x_rstd = sem("x_rstd")
        xn_done = sem("xn_done")
        xt_done = sem("xt_done")
        hn_hi_done = sem("hn_hi_done")
        hn_done = sem("hn_done")
        w_hi_done = sem("w_hi_done")
        w_lo_done = sem("w_lo_done")
        unit_done = sem("unit_done")
        act_freed = sem("act_freed")
        dve_freed = sem("dve_freed")
        evac_hi = sem("evac_hi")
        sig_done = sem("sig_done")
        conv_chain = sem("conv_chain")
        z_done = sem("z_done")
        z_copied = sem("z_copied")
        z_masked = sem("z_masked")
        abs_done = sem("abs_done")
        exp_done = sem("exp_done")
        log_done = sem("log_done")
        sp_done = sem("sp_done")
        sp_hi_done = sem("sp_hi_done")
        sp_split = sem("sp_split")
        u_done = sem("u_done")
        logit_done = sem("logit_done")
        a_done = sem("a_done")
        a_hi_done = sem("a_hi_done")
        a_split = sem("a_split")
        o_mm = sem("o_mm")
        o_hi_done = sem("o_hi_done")
        o_evac = sem("o_evac")
        mu_done = sem("mu_done")
        xc_done = sem("xc_done")
        sqc_done = sem("sqc_done")
        var_done = sem("var_done")
        stdc_done = sem("stdc_done")
        rstdc_done = sem("rstdc_done")
        yc_done = sem("yc_done")
        silu_done = sem("silu_done")
        s_hi_done = sem("s_hi_done")
        s_ready = sem("s_ready")
        win_chain = sem("win_chain")
        pooled_ready = sem("pooled_ready")
        mix_chain = sem("mix_chain")
        mix_done = sem("mix_done")
        mix_hi_done = sem("mix_hi_done")
        mix_split = sem("mix_split")
        h2_copied = sem("h2_copied")
        xt2_done = sem("xt2_done")
        res_done = sem("res_done")
        sqh_done = sem("sqh_done")
        ssum_done = sem("ssum_done")
        ss2_done = sem("ss2_done")
        std2_done = sem("std2_done")
        rstd2_done = sem("rstd2_done")
        scaled_done = sem("scaled_done")
        hn2_hi_done = sem("hn2_hi_done")
        hn2_done = sem("hn2_done")
        up_evac = sem("up_evac")
        tap_chain = sem("tap_chain")
        conv_done = sem("conv_done")
        gelu_done = sem("gelu_done")
        prod_done = sem("prod_done")
        g_hi_done = sem("g_hi_done")
        g_done = sem("g_done")
        ht_done = sem("ht_done")
        sso_done = sem("sso_done")
        mso_done = sem("mso_done")
        stdo_done = sem("stdo_done")
        rstdo_done = sem("rstdo_done")
        y_done = sem("y_done")

        block = ctx.enter_context(nc.Block())

        def unit_bank(j):
            return j % NU

        @block.sync
        def _(sp_eng):
            e = sp_eng

            def load(n, src, dst, again=0):
                if not (isinstance(n, int) and n < 2):
                    e.wait_ge(w_lo_done, n - 1)
                e.dma_start(dst, src).then_inc(raw_in[again], 16)

            def at_col(value):
                if isinstance(value, int):
                    return value
                return e.snap(value)

            def w_tile(w, col, width=P):
                return w[0].rearrange("(k p) n -> p k n", p=P)[:, :, bass.ds(col, width)]

            def full(s):
                return raw[s][:, :, :]

            first = NMETA
            e.dma_start(xn[0:first, 0, :], meta).then_inc(x_in[0], 16)
            e.dma_start(xn[first:P, 0, :], x[0, 0:P - first, :]).then_inc(x_in[0], 16)
            a = P - first
            e.dma_start(xn[:, 1:3, :], x[0, a:a + 2 * P, :].rearrange("(i p) d -> p i d", p=P)).then_inc(x_in[0], 16)
            load(0, w_tile(w_in, 0), full(0), 0)
            load(1, w_tile(w_in, CONV), full(1), 1)
            for g in (1, 2):
                b, n_whole = a + (3 * g - 1) * P, min(3, NT - 1 - 3 * g)
                e.dma_start(xn[:, 3 * g:3 * g + n_whole, :],
                            x[0, b:b + n_whole * P, :].rearrange("(i p) d -> p i d", p=P)).then_inc(x_in[g], 16)
            e.dma_start(xn[0:REST, NT - 1, :], x[0, SEQ - REST:SEQ, :]).then_inc(x_in[2], 16)
            for c in range(1, CC):
                load(2 * c, w_tile(w_in, c * P), full(0), 0)
                load(2 * c + 1, w_tile(w_in, CONV + c * P), full(1), 1)
            for j, col in enumerate((COL_V, COL_K, COL_Q)):
                n = SLOT_Q0 + j
                load(n, w_tile(w_in, col), full(n % 2), n % 2)
            for h in range(HEADS):
                cs = [c + (h + 1) * DH for c in (COL_V, COL_K, COL_Q)] if h < HEADS - 1 else \
                     [COL_POOL + c * P for c in range(POOLC // P)]
                for j, col in enumerate(cs):
                    n = slot_att(h, j)
                    load(n, w_tile(w_in, col), full(n % 2), n % 2)
            def load_gate(c, br):
                col = at_col(c * P + (COL_GATE + br * DM))
                e.wait_ge(w_lo_done, c * 4 + (SLOT_MIX + br - 1))
                e.dma_start(full(br % 2), w_tile(w_in, col)).then_inc(raw_in[br % 2], 16)

            load_gate(0, 0)
            load_gate(0, 1)
            e.wait_ge(pool_w_zeroed, 1)
            for g in range(GRPS):
                half = GC * (g % 2)
                per = GOUT // P
                e.dma_start(pool_w[half:half + GC, per * g:per * (g + 1), :],
                            w_pool_grp[0, g, :, :].rearrange("k (c n) -> k c n", n=P)).then_inc(pool_w_in, 16)
            load_gate(0, 2)
            with e.Fori(1, KC) as c:
                for br in range(3):
                    load_gate(c, br)
            for m in range(2):
                load(SLOT_OUT + m, w_tile(w_o, m * P), full(m % 2), m % 2)
            e.wait_ge(unit_done, UNIT_OUT)
            e.wait_ge(mix_done, NU * KC)
            e.dma_start(x_again[0:first, 0, :], meta).then_inc(x_again_in, 16)
            e.dma_start(x_again[first:P, 0, :], x[0, 0:P - first, :]).then_inc(x_again_in, 16)
            e.dma_start(x_again[:, 1:NT - 1, :],
                        x[0, a:a + (NT - 2) * P, :].rearrange("(i p) d -> p i d", p=P)).then_inc(x_again_in, 16)
            e.dma_start(x_last[0:REST, :], x[0, SEQ - REST:SEQ, :]).then_inc(x_again_in, 16)
            for m in range(2, KC):
                load(SLOT_OUT + m, w_tile(w_o, m * P), full(m % 2), m % 2)

            def load_up(n, j):
                for s in range(2):
                    col = at_col(j * P + s * FF)
                    load(n + s, w_tile(w_up, col), full(s), s)

            def load_half(n, j0, chunks):
                for i in range(chunks):
                    load_up(n + 2 * i, j0 + (1 + i))
                row = at_col(j0 * P)
                for m in range(KC // 2):
                    load(n + (2 * chunks + m),
                         w_down[0, bass.ds(row, 3 * P), m * 2 * P:(m + 1) * 2 * P].rearrange("(k p) n -> p k n", p=P),
                         raw[m % 2][:, 0:6, :].rearrange("p (k m) n -> p k (m n)", k=3), m % 2)

            load_up(SLOT_FFN, 0)
            e.wait_ge(xt2_done, NU * KC)
            e.dma_start(final_g[:, :], final_norm.partition_broadcast(P)).then_inc(final_g_in, 16)
            with e.Fori(0, FC // 6 - 1) as it:
                for half in range(2):
                    load_half(it * (2 * HALF_SLOTS) + (SLOT_FFN + 2 + half * HALF_SLOTS), it * 6 + 3 * half, 3)
            it = FC // 6 - 1
            for half in range(2):
                load_half(it * (2 * HALF_SLOTS) + (SLOT_FFN + 2 + half * HALF_SLOTS), it * 6 + 3 * half, 3 - half)
            for i in range(SEQ // P):
                e.wait_ge(y_done, i + 1)
                e.dma_start(out[0, i * P:(i + 1) * P, :], y_out[i % 3][:, :]).then_inc(stored[i % 3], 16)
            for s in range(3):
                e.wait_ge(stored[s], 16 * len(range(s, SEQ // P, 3)))

        @block.gpsimd
        def _(e):
            def split_lo(n):
                s = n % 2
                e.wait_ge(w_hi_done, n + 1)
                e.tensor_tensor(wl[s][:, :, :], raw[s][:, :, :], wh[s][:, :, :].bitcast(f32), ALU.subtract)\
                    .then_inc(w_lo_done, 1)

            def split_lo_at(s, n, tiles=KC):
                e.wait_ge(w_hi_done, n + 1)
                e.tensor_tensor(wl[s][:, 0:tiles, :], raw[s][:, 0:tiles, :], wh[s][:, 0:tiles, :].bitcast(f32),
                                ALU.subtract).then_inc(w_lo_done, 1)

            e.memset(ident[:, :], 0.0).then_inc(ident_set, 1)
            e.memset(ones[:, :], 1.0).then_inc(ident_set, 1)
            e.memset(eps[:, :], EPS).then_inc(ident_set, 1)
            e.memset(stat[:, :], 1.0).then_inc(ident_set, 1)
            e.wait_ge(ident_set, 4)
            e.affine_select(out=ident[:, :], in_=ident[:, :], compare_op=ALU.not_equal, fill=1.0, base=0,
                            pattern=[[-1, P]], channel_multiplier=1).then_inc(ident_set, 1)
            e.memset(mask32[:, :, :], -1.0).then_inc(masks32_set, 1)
            e.wait_ge(masks32_set, 1)
            e.affine_select(out=mask32[:, 0, :], in_=mask32[:, 0, :], compare_op=ALU.is_ge, fill=0.0, base=0,
                            pattern=[[-1, P]], channel_multiplier=1).then_inc(masks32_set, 1)
            e.affine_select(out=mask32[:, 1, :], in_=mask32[:, 1, :], compare_op=ALU.is_gt, fill=0.0, base=0,
                            pattern=[[1, P]], channel_multiplier=-1).then_inc(masks32_set, 1)
            e.memset(glu[:, :, 0:TAPS - 1], 0.0).then_inc(glu_pad_set, 1)
            e.iota(inv_cnt[:, :, :], pattern=[[0, CC], [1, LEFT]], base=1, channel_multiplier=0,
                   allow_small_or_imprecise_dtypes=True).then_inc(cnt_set, 1)
            split_lo(0)
            split_lo(1)
            e.wait_ge(xt_done, KC * len(GROUPS))
            for s in range(2):
                e.memset(k_hi[s][:, T:TP].bitcast(f32), 0.0).then_inc(kv_pads_set, 1)
                e.memset(k_lo[s][:, T:TP].bitcast(f32), 0.0).then_inc(kv_pads_set, 1)
            e.memset(vt[:, T:TP], 0.0).then_inc(kv_pads_set, 1)
            for n in range(2, SLOT_ATT + 1):
                split_lo(n)

            def mask_z(t):
                i, n = TILES[t % NS]
                if MASKED[t % NS]:
                    e.wait_ge(z_copied, t + 1)
                    e.affine_select(out=zs[t % 3][:, :], in_=zs[t % 3][:, :], compare_op=ALU.is_gt, fill=MASKED_Z,
                                    base=QW * i - P * n, pattern=[[1, QW]], channel_multiplier=-1)\
                        .then_inc(z_masked, 1)

            PIECES = ((0, 3), (3, 6), (6, KC))

            def lo_pieces(t):
                for n, piece in split_pieces(t, 2, len(PIECES)):
                    s, (k0, k1) = n % 2, PIECES[piece]
                    e.wait_ge(w_hi_done, n + 1)
                    ins = e.tensor_tensor(wl[s][:, k0:k1, :], raw[s][:, k0:k1, :], wh[s][:, k0:k1, :].bitcast(f32),
                                          ALU.subtract)
                    if piece == len(PIECES) - 1:
                        ins.then_inc(w_lo_done, 1)

            mask_z(0)
            mask_z(1)
            split_lo(SLOT_ATT + 1)
            for h in range(HEADS):
                if h == HEADS - 1:
                    e.wait_ge(conv_chain, 2 * TAPS * CC)
                    e.memset(pool_in[:, :, 0:LEFT], 0.0).then_inc(pool_pad_set, 1)
                for idx in range(NS):
                    t = h * NS + idx
                    if t + 2 < STEPS:
                        mask_z(t + 2)
                    e.wait_ge(a_hi_done, t + 1)
                    if t >= 2:
                        e.wait_ge(o_mm, t - 1)
                    e.tensor_tensor(a_lo[t % 2][:, :], att_w[t % 2][:, :], a_hi[t % 2][:, :].bitcast(f32),
                                    ALU.subtract).then_inc(a_split, 1)
                    lo_pieces(t)
            for t in range(STEPS, STEPS + 5):
                lo_pieces(t)
            e.wait_ge(o_evac, HEADS * (T // QW))
            e.memset(pool_w[:, :, :], 0.0).then_inc(pool_w_zeroed, 1)

            with e.Fori(0, KC) as c:
                n = SLOT_MIX + c * 4
                split_lo_at(0, n + 2)
                split_lo_at(1, n + 3, HEADS + CC + 1)
                split_lo_at(0, n + 4)
                split_lo_at(1, n + 5)
            for m in range(KC):
                split_lo(SLOT_OUT + 2 + m)

            split_lo(SLOT_FFN + 2)
            split_lo(SLOT_FFN + 3)

            def split_half(n, chunks, tail=0):
                for i in range(2 * chunks - 2):
                    split_lo_at(i % 2, n + i)
                for m in range(KC // 2):
                    split_lo_at(m % 2, n + (2 * chunks - 2 + m), 6)
                for i in range(2 - tail):
                    split_lo_at(i % 2, n + (2 * chunks - 2 + KC // 2 + i))

            with e.Fori(0, FC // 6 - 1) as it:
                for half in range(2):
                    split_half(it * (2 * HALF_SLOTS) + (SLOT_FFN + 4 + half * HALF_SLOTS), 3)
            n = SLOT_FFN + 4 + (FC // 6 - 1) * 2 * HALF_SLOTS
            split_half(n, 3)
            split_half(n + HALF_SLOTS, 2, tail=2)

        @block.scalar
        def _(e):
            raw_count = [0, 0]

            def split_hi(n, tiles=KC, dmas=1):
                s = n % 2
                raw_count[s] += 16 * dmas
                e.wait_ge(raw_in[s], raw_count[s])
                if n >= 2:
                    e.wait_ge(unit_done, slot_left(n - 2))
                e.activation(wh[s][:, 0:tiles, :], raw[s][:, 0:tiles, :], COPY).then_inc(w_hi_done, 1)

            def split_hi_at(s, left, raw_value, tiles=KC):
                e.wait_ge(raw_in[s], raw_value)
                e.wait_ge(unit_done, left)
                e.activation(wh[s][:, 0:tiles, :], raw[s][:, 0:tiles, :], COPY).then_inc(w_hi_done, 1)

            def rows_in(slot, at, count, src):
                e.dma_start(rows[at:at + count, slot, :], src).then_inc(params_in, 16)

            n_params = 0
            for at, p in ((C_N1, norm1), (C_N2, norm2), (C_BC, b_conv_out), (C_PS, pool_scale)):
                rows_in(0, at, KC, p[0].rearrange("(k p) -> k p", p=P))
                n_params += 1
            for at, p in ((C_CB, conv_dw_b), (C_LG, conv_ln_g), (C_LB, conv_ln_b)):
                rows_in(0, at, CC, p[0].rearrange("(k p) -> k p", p=P))
                n_params += 1
            rows_in(0, C_CW, TAPS * CC, conv_dw_w[0].rearrange("t (k p) -> (t k) p", p=P))
            fw = ffn_dw_w[0].rearrange("t (k p) -> (t k) p", p=P)
            rows_in(1, 0, P, fw[0:P, :])
            rows_in(2, 0, FTAPS * 2 * FC - P, fw[P:FTAPS * 2 * FC, :])
            rows_in(2, FTAPS * 2 * FC - P, 2 * FC, ffn_dw_b[0].rearrange("(k p) -> k p", p=P))

            def hn_hi_group(g):
                c0, cn = THIRD[g]
                for k in range(KC):
                    n = g * KC + k
                    if n == 0:
                        e.wait_ge(cols_set, 1)
                    e.wait_ge(xt_done, n + 1)
                    e.activation(hn_hi[:, k, c0:c0 + cn], psum[:, 3 + n % 4, 0:cn], COPY,
                                 scale=cols[:, C_N1 + k:C_N1 + k + 1]).then_inc(hn_hi_done, 1)

            def token_stats(g):
                i0, ni = GROUPS[g]
                e.wait_ge(x_in[g], (48, 16, 32)[g])
                for i in range(i0, i0 + ni):
                    r = P if i < NT - 1 else REST
                    if i == 0:
                        e.wait_ge(ident_set, 4)
                    if i >= 2:
                        e.wait_ge(x_ss, i - 1)
                    e.activation(junk[i % 2][0:r, :], xn[0:r, i, :], ACT.Square, accum_out=stat[0:r, i:i + 1])\
                        .then_inc(x_ss, 1)
                e.wait_ge(x_ms, g + 1)
                e.activation(stat[:, NT + i0:NT + i0 + ni], stat[:, NT + i0:NT + i0 + ni], ACT.Sqrt)\
                    .then_inc(x_std, 1)

            token_stats(0)
            split_hi(0)
            split_hi(1)
            for g in range(3):
                if g < 2:
                    token_stats(g + 1)
                hn_hi_group(g)

            for c in range(CC):
                for tt, (t0, tw) in enumerate(THIRD):
                    n = NU * c + tt
                    if tt == NU - 1:
                        split_hi(2 * c + 2)
                    e.wait_ge(unit_done, 2 * n + 2)
                    if n >= 2:
                        e.wait_ge(dve_freed, 2 * (n - 1))
                    e.activation(sig[n % 2][:, 0:tw], psum[:, unit_bank(2 * n + 1), 0:tw], ACT.Sigmoid)\
                        .then_inc(sig_done, 1)
                split_hi(2 * c + 3)
            def qk_hi(u, dst, tt, scale):
                t0, tw = THIRD[tt]
                e.wait_ge(unit_done, u + 1)
                e.activation(dst[:, t0:t0 + tw], psum[:, unit_bank(u), 0:tw], COPY, scale=scale)\
                    .then_inc(evac_hi, 1)

            seen_masks = [0]

            def log_of(t):
                b_ = soft[t % 2]
                e.wait_ge(z_copied, t + 1)
                if MASKED[t % NS]:
                    seen_masks[0] += 1
                    e.wait_ge(z_masked, seen_masks[0])
                if t >= 2:
                    e.wait_ge(sp_done, t - 1)
                e.activation(b_[:, :], zs[t % 3][:, :], ACT.Abs).then_inc(abs_done, 1)
                e.wait_ge(abs_done, t + 1)
                e.activation(b_[:, :], b_[:, :], ACT.Exp, scale=-1.0).then_inc(exp_done, 1)
                e.wait_ge(exp_done, t + 1)
                e.activation(b_[:, :], b_[:, :], ACT.Ln, bias=1.0).then_inc(log_done, 1)

            def copy_z(t):
                e.wait_ge(z_done, t + 1)
                if t >= 3:
                    e.wait_ge(logit_done, t - 2)
                e.activation(zs[t % 3][:, :], psum[:, PZ[t % 2], 0:QW], COPY).then_inc(z_copied, 1)

            for j in range(2):
                for tt in range(NU):
                    if j == 1:
                        qk_hi(UNIT_Q0 + NU * j + tt, k_hi[0], tt, 1.0)
                split_hi(SLOT_Q0 + j + 2)
            e.preload_act_table_set("natural_log_exp_and_others")
            for tt in range(NU):
                qk_hi(UNIT_Q0 + 2 * NU + tt, q_hi[0], tt, SCALE)
                if tt >= 1:
                    copy_z(tt - 1)
                    log_of(tt - 1)

            def v_hi_group(h, g):
                u = unit_att(h) + g
                i0, ni = VGROUPS[g]
                e.wait_ge(unit_done, u + 1)
                e.activation(v_hi[:, i0:i0 + ni, :],
                             psum[:, unit_bank(u), 0:ni * P].rearrange("p (n d) -> p n d", d=DH), COPY)\
                    .then_inc(evac_hi, 1)

            def hi_pieces(t):
                for n, piece in split_pieces(t, 0, 2):
                    s, half = n % 2, KC // 2
                    if piece == 0:
                        raw_count[s] += 16
                        e.wait_ge(raw_in[s], raw_count[s])
                        e.wait_ge(unit_done, slot_left(n - 2))
                    ks = slice(piece * half, (piece + 1) * half)
                    ins = e.activation(wh[s][:, ks, :], raw[s][:, ks, :], COPY)
                    if piece == 1:
                        ins.then_inc(w_hi_done, 1)

            v_hi_group(0, 0)
            v_hi_group(0, 1)
            split_hi(SLOT_Q0 + 4)
            for h in range(HEADS):
                for idx in range(NS):
                    t = h * NS + idx
                    if t + 2 < STEPS:
                        copy_z(t + 2)
                    e.wait_ge(logit_done, t + 1)
                    e.activation(att_w[t % 2][:, :], att_w[t % 2][:, :], ACT.Exp).then_inc(a_done, 1)
                    if idx == 1:
                        v_hi_group(h, 2)
                    if t >= 1 and LAST[(t - 1) % NS]:
                        hh, i = (t - 1) // NS, TILES[(t - 1) % NS][0]
                        e.wait_ge(o_mm, t)
                        e.activation(att_hi[:, hh, QW * i:QW * (i + 1)], psum[:, PO, 0:QW], COPY)\
                            .then_inc(o_hi_done, 1)
                    for f in fill_ended(h, idx):
                        if h < HEADS - 1 and f >= NU:
                            qk_hi(unit_att(h) + NU + f, (k_hi, q_hi)[f // NU - 1][(h + 1) % 2], f % NU,
                                  (1.0, SCALE)[f // NU - 1])
                    if t + 2 < STEPS:
                        log_of(t + 2)
                    if h < HEADS - 1 and idx >= NS - 2:
                        v_hi_group(h + 1, idx - (NS - 2))
                    hi_pieces(t)
            e.wait_ge(o_mm, STEPS)
            e.activation(att_hi[:, HEADS - 1, T - QW:T], psum[:, PO, 0:QW], COPY).then_inc(o_hi_done, 1)

            RAW_MIX = list(raw_count)

            def gate_evac(c, j):
                t0, tw = THIRD[j % NU]
                u = c * (6 * NU) + (UNIT_MIX + j)
                e.wait_ge(unit_done, u + 1)
                e.activation(gate[:, j // NU, t0:t0 + tw], psum[:, unit_bank(j), 0:tw], ACT.Sigmoid)\
                    .then_inc(act_freed, 1)

            def splits_mix(c, which):
                left = c * (6 * NU) + (UNIT_MIX + (NU * (which + 1) if which < 3 else 6 * NU))
                if which == 0:
                    split_hi_at(0, left, c * 32 + (RAW_MIX[0] + 16))
                if which == 1:
                    e.wait_ge(raw_in[1], c * 48 + (RAW_MIX[1] + 32))
                    e.wait_ge(unit_done, left)
                    e.activation(wh[1][:, 0:HEADS + CC, :], raw[1][:, 0:HEADS + CC, :], COPY)
                    e.activation(raw[1][:, HEADS + CC, :], pool_w[:, bass.ds(c, 1), :].rearrange("p a n -> p (a n)"),
                                 COPY)
                    e.activation(wh[1][:, HEADS + CC, :], pool_w[:, bass.ds(c, 1), :].rearrange("p a n -> p (a n)"),
                                 COPY).then_inc(w_hi_done, 1)
                if which == 2:
                    split_hi_at(0, left, c * 32 + (RAW_MIX[0] + 32))
                if which == 3:
                    split_hi_at(1, left, c * 48 + (RAW_MIX[1] + 48))

            def load_branch_tiles(c):
                e.wait_ge(w_lo_done, c * 4 + (SLOT_MIX + 2))
                for k, kn, w in ((0, HEADS, w_attn_out), (HEADS, CC, w_conv_out)):
                    e.dma_start(raw[1][:, k:k + kn, :],
                                w[0].rearrange("(k p) n -> p k n", p=P)[:, :, bass.ds(c * P, P)])\
                        .then_inc(raw_in[1], 16)

            load_branch_tiles(0)
            for tt, (t0, tw) in enumerate(THIRD):
                e.wait_ge(xc_done, CC * (tt + 1))
                if tt >= 1:
                    e.wait_ge(var_done, tt)
                e.activation(sq_cv[:, :, 0:tw], cv[:, :, t0:t0 + tw], ACT.Square).then_inc(sqc_done, 1)
                gate_evac(0, tt)
            for tt, (t0, tw) in enumerate(THIRD):
                e.wait_ge(var_done, tt + 1)
                e.activation(std_cv[:, t0:t0 + tw], psum[:, (PU[1], PO, PZ[0])[tt], 0:tw], ACT.Sqrt,
                             scale=1.0 / CONV, bias=eps[:, :]).then_inc(stdc_done, 1)
            e.wait_ge(pool_w_in, 16 * GRPS)
            splits_mix(0, 0)
            for j in range(NU, 2 * NU):
                gate_evac(0, j)
            splits_mix(0, 1)
            for j in range(2 * NU, 3 * NU):
                gate_evac(0, j)
            splits_mix(0, 2)
            e.wait_ge(yc_done, CC)
            for cc in range(CC):
                e.activation(cv[:, cc, :], cv[:, cc, :], ACT.Silu, scale=cols[:, C_LG + cc:C_LG + cc + 1],
                             bias=cols[:, C_LB + cc:C_LB + cc + 1]).then_inc(silu_done, 1)
            for cc in range(CC):
                e.wait_ge(silu_done, cc + 1)
                e.activation(s_hi[:, cc, :], cv[:, cc, :], COPY).then_inc(s_hi_done, 1)
            splits_mix(0, 3)
            with e.Fori(1, KC) as c:
                load_branch_tiles(c)
                e.wait_ge(mix_done, c * NU)
                for j in range(3 * NU):
                    gate_evac(c, j)
                    if j % NU == NU - 1:
                        splits_mix(c, j // NU)
                splits_mix(c, 3)

            e.wait_ge(unit_done, UNIT_OUT)
            for tt, (t0, tw) in enumerate(THIRD):
                e.wait_ge(mix_done, NU * (KC - 1) + tt + 1)
                for k in range(0, KC, KC // 2):
                    e.activation(mix_hi[:, k:k + KC // 2, t0:t0 + tw], mixed[:, k:k + KC // 2, t0:t0 + tw], COPY)\
                        .then_inc(mix_hi_done, 1)
            raw_count[0] = RAW_MIX[0] + 32 * KC
            raw_count[1] = RAW_MIX[1] + 48 * KC
            order = [(m, tt) for tt in range(NU) for m in range(2)]

            def h2_copy(i, m, tt):
                t0, tw = THIRD[tt]
                e.wait_ge(unit_done, UNIT_OUT + i + 1)
                if i == 0:
                    e.wait_ge(mix_split, 2 * NU)
                e.activation(h2[:, m, t0:t0 + tw], psum[:, unit_bank(i), 0:tw], COPY).then_inc(act_freed, 1)

            def square_h(m):
                spans = [(0, T)] if m < KC - 1 else THIRD
                for q, (c0, cn) in enumerate(spans):
                    e.wait_ge(res_done, NU * m + (NU if m < KC - 1 else q + 1))
                    if m >= 2 and q == 0:
                        e.wait_ge(ssum_done, m - 1)
                    dst = sq_sum if m == 0 else sq_h
                    e.activation(dst[:, c0:c0 + cn], h2[:, m, c0:c0 + cn], ACT.Square).then_inc(sqh_done, 1)

            for i, (m, tt) in enumerate(order):
                h2_copy(i, m, tt)
            split_hi(SLOT_OUT + 2)
            split_hi(SLOT_OUT + 3)
            for m in range(2, KC):
                for tt in range(NU):
                    h2_copy(NU * m + tt, m, tt)
                split_hi(SLOT_OUT + m + 2)
                if m == 2:
                    square_h(0)
                square_h(m - 1)
            square_h(KC - 1)
            for q, (c0, cn) in enumerate(THIRD):
                e.wait_ge(ss2_done, q + 1)
                e.activation(rstd2[:, c0:c0 + cn], psum[:, PZ[0] + q, 0:cn], ACT.Sqrt, scale=1.0 / DM,
                             bias=eps[:, :]).then_inc(std2_done, 1)
                for k in range(KC):
                    n = q * KC + k
                    e.wait_ge(scaled_done, n + 1)
                    e.activation(hn_hi[:, k, c0:c0 + cn], scaled[n % 2][:, 0:cn], COPY,
                                 scale=cols[:, C_N2 + k:C_N2 + k + 1]).then_inc(hn2_hi_done, 1)

            RAW_FFN = list(raw_count)

            def up_tile(ch, e6, which, u):
                j = ch + which * FC
                tile_n = 2 * ch + which
                if not isinstance(ch, int) or tile_n >= 2:
                    e.wait_ge(conv_done, tile_n - 1)
                if (not isinstance(ch, int) or ch >= 2) and which == 0:
                    e.wait_ge(g_done, ch - 1)
                w2 = cols[:, bass.ds(j + (C_FW + (FTAPS - 1) * 2 * FC), 1)]
                bb = cols[:, bass.ds(j + C_FB, 1)]
                dst = acc[2 * (e6 % 2) + which]
                for tt, (t0, tw) in enumerate(THIRD):
                    e.wait_ge(unit_done, u + (tt + 1))
                    bank = psum[:, NU * which + tt, 0:tw]
                    e.activation(up[which][:, FTAPS - 1 + t0:FTAPS - 1 + t0 + tw], bank, COPY)
                    last = e.activation(dst[:, t0:t0 + tw], bank, ACT.Identity, scale=w2, bias=bb)
                    last.then_inc(act_freed, 1)

            def gelu_and_hi(ch, e6):
                g = acc[2 * (e6 % 2)]
                e.wait_ge(conv_done, 2 * ch + 1)
                e.activation(g[:, :], g[:, :], ACT.Gelu_apprx_tanh).then_inc(gelu_done, 1)
                e.wait_ge(prod_done, ch + 1)
                e.activation(g_hi[:, e6 % RING, :], acc[2 * (e6 % 2) + 1][:, :], COPY).then_inc(g_hi_done, 1)

            def half_body(it6, half, chunks, total_it, last=False):
                u0 = total_it * (2 * HALF_UNITS) + (UNIT_FFN + 2 * NU + half * HALF_UNITS)
                r0 = [total_it * (16 * HALF_SLOTS) + (RAW_FFN[s] + 16 + half * 8 * HALF_SLOTS) for s in range(2)]
                count = 2 * chunks + KC // 2
                for i in range(chunks):
                    e6 = 3 * half + 1 + i
                    for which in range(2):
                        up_tile(it6 + e6, e6, which, u0 + NU * (2 * i + which))
                        s = 2 * i + which
                        split_hi_at(which, u0 + NU * (s + 1), r0[which] + 16 * (s // 2 + 1), 
                                    KC if s + 2 < 2 * chunks else 6)
                    gelu_and_hi(it6 + e6, e6)
                for m in range(KC // 2):
                    s = 2 * chunks + m
                    if last and m >= KC // 2 - 2:
                        break
                    tiles = 6 if s + 2 < count else KC
                    split_hi_at(s % 2, u0 + (2 * NU * chunks + 2 * NU * (m + 1)), r0[s % 2] + 16 * (s // 2 + 1), tiles)

            for which in range(2):
                up_tile(0, 0, which, UNIT_FFN + NU * which)
                split_hi_at(which, slot_left(SLOT_FFN + which), RAW_FFN[which] + 16)
            gelu_and_hi(0, 0)
            with e.Fori(0, FC // 6 - 1) as it:
                for half in range(2):
                    half_body(it * 6, half, 3, it)
            it = FC // 6 - 1
            half_body(it * 6, 0, 3, it)
            half_body(it * 6, 1, 2, it, last=True)

            def std_out(i):
                e.wait_ge(mso_done, i + 1)
                e.activation(stat[:, NT + i:NT + i + 1], stat[:, NT + i:NT + i + 1], ACT.Sqrt).then_inc(stdo_done, 1)

            for i in range(SEQ // P):
                e.wait_ge(ht_done, i + 1)
                if i >= 2:
                    e.wait_ge(sso_done, i - 1)
                e.activation(sq_out[i % 2][:, :].rearrange("p (a n) -> p a n", a=2), psum[:, 2 * (i % 4):2 * (i % 4) + 2, :],
                             ACT.Square, accum_out=stat[:, i:i + 1]).then_inc(sso_done, 1)
                if i >= 1:
                    std_out(i - 1)
            std_out(SEQ // P - 1)

        @block.vector
        def _(e):
            e.wait_ge(masks32_set, 3)
            e.tensor_copy(neg_tri[:, :], mask32[:, 0, :]).then_inc(masks_set, 1)
            e.tensor_copy(neg_rest[:, :], mask32[:, 1, :]).then_inc(masks_set, 1)
            e.wait_ge(cols_t, 3)
            e.tensor_copy(cols[:, :], psum[:, PO, 0:NCOL]).then_inc(cols_set, 1)

            def norm_group(g):
                i0, ni = GROUPS[g]
                s_in, s_out = stat[:, i0:i0 + ni], stat[:, NT + i0:NT + i0 + ni]
                e.wait_ge(x_ss, i0 + ni)
                e.tensor_scalar(s_out, s_in, 1.0 / DM, EPS, ALU.mult, ALU.add).then_inc(x_ms, 1)
                e.wait_ge(x_std, g + 1)
                e.reciprocal(s_out, s_out).then_inc(x_rstd, 1)
                e.wait_ge(x_rstd, g + 1)
                for i in range(i0, i0 + ni):
                    r = P if i < NT - 1 else REST
                    e.tensor_scalar(xn[0:r, i, :], xn[0:r, i, :], stat[0:r, NT + i:NT + i + 1], None, ALU.mult)\
                        .then_inc(xn_done, 1)

            def hn_lo_group(g):
                c0, cn = THIRD[g]
                for k in range(KC):
                    n = g * KC + k
                    e.wait_ge(hn_hi_done, n + 1)
                    e.scalar_tensor_tensor(out=hn_lo[:, k, c0:c0 + cn], in0=psum[:, 3 + n % 4, 0:cn],
                                           scalar=cols[:, C_N1 + k:C_N1 + k + 1],
                                           in1=hn_hi[:, k, c0:c0 + cn].bitcast(f32),
                                           op0=ALU.mult, op1=ALU.subtract).then_inc(hn_done, 1)

            norm_group(0)
            for g in range(3):
                if g < 2:
                    norm_group(g + 1)
                hn_lo_group(g)

            def glu_third(c, tt):
                t0, tw = THIRD[tt]
                n = NU * c + tt
                e.wait_ge(sig_done, n + 1)
                e.tensor_tensor(glu[:, c, TAPS - 1 + t0:TAPS - 1 + t0 + tw], psum[:, unit_bank(2 * n), 0:tw],
                                sig[n % 2][:, 0:tw], ALU.mult).then_inc(dve_freed, 2)

            def conv_tap(i):
                c, tap, half = i // (2 * TAPS), i // 2 % TAPS, i % 2
                ts = slice(half * T // 2, (half + 1) * T // 2)
                w = cols[:, C_CW + tap * CC + c:C_CW + tap * CC + c + 1]
                src = glu[:, c, tap + half * T // 2:tap + (half + 1) * T // 2]
                if tap == 0:
                    e.wait_ge(dve_freed, 2 * NU * (c + 1))
                    if c == 0:
                        e.wait_ge(glu_pad_set, 1)
                    e.tensor_scalar(cv[:, c, ts], src, w, cols[:, C_CB + c:C_CB + c + 1], ALU.mult, ALU.add)\
                        .then_inc(conv_chain, 1)
                else:
                    e.wait_ge(conv_chain, i - 1)
                    e.scalar_tensor_tensor(out=cv[:, c, ts], in0=src, scalar=w, in1=cv[:, c, ts],
                                           op0=ALU.mult, op1=ALU.add).then_inc(conv_chain, 1)

            taps = [0]

            def conv_taps(n):
                until = min(taps[0] + n, 2 * TAPS * CC)
                for i in range(taps[0], until):
                    conv_tap(i)
                taps[0] = until

            for tt in range(NU):
                glu_third(0, tt)
            for c in range(1, CC):
                for tt in range(NU):
                    conv_taps(10)
                    glu_third(c, tt)
            hi_seen = [0]

            def qk_lo(u, dst, hi, tt, scale):
                t0, tw = THIRD[tt]
                hi_seen[0] += 1
                e.wait_ge(evac_hi, hi_seen[0])
                e.scalar_tensor_tensor(out=dst[:, t0:t0 + tw], in0=psum[:, unit_bank(u), 0:tw], scalar=scale,
                                       in1=hi[:, t0:t0 + tw].bitcast(f32), op0=ALU.mult, op1=ALU.subtract)\
                    .then_inc(dve_freed, 1)

            def copy_unit(u, dst):
                e.wait_ge(unit_done, u + 1)
                e.tensor_copy(dst, psum[:, unit_bank(u), 0:dst.shape[-1]]).then_inc(dve_freed, 1)

            def softplus(t):
                e.wait_ge(log_done, t + 1)
                if t >= 1:
                    e.wait_ge(sp_split, t)
                e.scalar_tensor_tensor(out=sp[:, :], in0=zs[t % 3][:, :], scalar=0.0, in1=soft[t % 2][:, :],
                                       op0=ALU.max, op1=ALU.add).then_inc(sp_done, 1)

            def softplus_split(t):
                e.wait_ge(sp_done, t + 1)
                e.tensor_copy(sp_hi[t % 2][:, :], sp[:, :]).then_inc(sp_hi_done, 1)
                e.wait_ge(sp_hi_done, t + 1)
                e.tensor_tensor(sp_lo[t % 2][:, :], sp[:, :], sp_hi[t % 2][:, :].bitcast(f32), ALU.subtract)\
                    .then_inc(sp_split, 1)

            for j in range(3):
                for tt, (t0, tw) in enumerate(THIRD):
                    u = UNIT_Q0 + NU * j + tt
                    if j == 0:
                        copy_unit(u, vt[:, t0:t0 + tw])
                    else:
                        qk_lo(u, (k_lo, q_lo)[j - 1][0], (k_hi, q_hi)[j - 1][0], tt, (1.0, SCALE)[j - 1])
                    if j < 2 or tt == 0:
                        conv_taps(5)
            softplus(0)
            softplus_split(0)

            def v_lo_group(h, g):
                u = unit_att(h) + g
                i0, ni = VGROUPS[g]
                hi_seen[0] += 1
                e.wait_ge(evac_hi, hi_seen[0])
                e.tensor_tensor(v_lo[:, i0:i0 + ni, :],
                                psum[:, unit_bank(u), 0:ni * P].rearrange("p (n d) -> p n d", d=DH),
                                v_hi[:, i0:i0 + ni, :].bitcast(f32), ALU.subtract).then_inc(dve_freed, 1)

            v_lo_group(0, 0)
            v_lo_group(0, 1)
            for h in range(HEADS):
                for idx in range(NS):
                    t = h * NS + idx
                    e.wait_ge(u_done, t + 1)
                    if t >= 2:
                        e.wait_ge(a_split, t - 1)
                    e.tensor_tensor(att_w[t % 2][:, :], psum[:, PU[(HEADS * h + TILES[idx][0]) % 2], 0:QW],
                                    zs[t % 3][:, :], ALU.add).then_inc(logit_done, 1)
                    if t + 1 < STEPS:
                        softplus(t + 1)
                        softplus_split(t + 1)
                    if idx == 1:
                        v_lo_group(h, 2)
                    for f in fill_ended(h, idx):
                        u = unit_att(h) + NU + f
                        t0, tw = THIRD[f % NU]
                        if h == HEADS - 1:
                            copy_unit(u, pool_in[:, f // NU, LEFT + t0:LEFT + t0 + tw])
                        elif f < NU:
                            copy_unit(u, vt[:, t0:t0 + tw])
                        else:
                            p_, j = (h + 1) % 2, f // NU - 1
                            qk_lo(u, (k_lo, q_lo)[j][p_], (k_hi, q_hi)[j][p_], f % NU, (1.0, SCALE)[j])
                    if h < HEADS - 1 and idx >= NS - 2:
                        v_lo_group(h + 1, idx - (NS - 2))
                    conv_taps(1)
                    e.wait_ge(a_done, t + 1)
                    if t >= 2:
                        e.wait_ge(o_mm, t - 1)
                    e.tensor_copy(a_hi[t % 2][:, :], att_w[t % 2][:, :]).then_inc(a_hi_done, 1)
                    if t >= 1 and LAST[(t - 1) % NS]:
                        hh, i = (t - 1) // NS, TILES[(t - 1) % NS][0]
                        n_o = hh * (T // QW) + i
                        e.wait_ge(o_hi_done, n_o + 1)
                        e.tensor_tensor(att_lo[:, hh, QW * i:QW * (i + 1)], psum[:, PO, 0:QW],
                                        att_hi[:, hh, QW * i:QW * (i + 1)].bitcast(f32), ALU.subtract)\
                            .then_inc(o_evac, 1)
            n_o = HEADS * (T // QW)
            e.wait_ge(o_hi_done, n_o)
            e.tensor_tensor(att_lo[:, HEADS - 1, T - QW:T], psum[:, PO, 0:QW],
                            att_hi[:, HEADS - 1, T - QW:T].bitcast(f32), ALU.subtract).then_inc(o_evac, 1)

            for tt, (t0, tw) in enumerate(THIRD):
                e.wait_ge(mu_done, tt + 1)
                for cc in range(CC):
                    e.scalar_tensor_tensor(out=cv[:, cc, t0:t0 + tw], in0=psum[:, (PZ[0], PZ[1], PU[0])[tt], 0:tw],
                                           scalar=-1.0 / CONV, in1=cv[:, cc, t0:t0 + tw],
                                           op0=ALU.mult, op1=ALU.add).then_inc(xc_done, 1)
            chained = [0]

            def link(ins):
                ins.then_inc(win_chain, 1)
                chained[0] += 1
                e.wait_ge(win_chain, chained[0])

            link(e.memset(win[0][:, 0:LEFT], 0.0))
            link(e.memset(win[1][:, 0:LEFT], 0.0))
            e.wait_ge(cnt_set, 1)
            for g in range(GRPS):
                part = inv_cnt[GC * (g % 2):GC * (g % 2) + GC, g // 2, :]
                link(e.tensor_scalar(part, part, float(WINDOWS[g]), None, ALU.min))
            link(e.reciprocal(inv_cnt[:, :, :], inv_cnt[:, :, :]))
            e.wait_ge(pool_pad_set, 1)
            for c in range(CC):
                lo_w, hi_w = WINDOWS[2 * c], WINDOWS[2 * c + 1]
                cur, w_ = pool_in[:, c, :], 1
                flip = 0
                while w_ < lo_w:
                    dst = win[flip]
                    link(e.tensor_tensor(dst[:, LEFT:LEFT + T], cur[:, LEFT:LEFT + T], cur[:, LEFT - w_:LEFT - w_ + T],
                                         ALU.add))
                    cur, flip, w_ = dst, 1 - flip, 2 * w_
                dst = win[flip]
                link(e.tensor_tensor(dst[GC:P, LEFT:LEFT + T], cur[GC:P, LEFT:LEFT + T],
                                     cur[GC:P, LEFT - w_:LEFT - w_ + T], ALU.add))
                link(e.tensor_copy(dst[0:GC, LEFT:LEFT + T], cur[0:GC, LEFT:LEFT + T]))
                link(e.tensor_tensor(dst[:, LEFT:2 * LEFT], dst[:, LEFT:2 * LEFT], inv_cnt[:, c, :], ALU.mult))
                link(e.tensor_tensor(dst[:, LEFT:2 * LEFT], dst[:, LEFT:2 * LEFT], pool_in[:, c, LEFT:2 * LEFT],
                                     ALU.subtract))
                link(e.scalar_tensor_tensor(out=dst[:, 2 * LEFT:LEFT + T], in0=dst[:, 2 * LEFT:LEFT + T],
                                            scalar=inv_cnt[:, c, LEFT - 1:LEFT], in1=pool_in[:, c, 2 * LEFT:LEFT + T],
                                            op0=ALU.mult, op1=ALU.subtract))
                link(e.tensor_copy(pooled_hi[:, c, :], dst[:, LEFT:LEFT + T]))
                ins = e.tensor_tensor(pooled_lo[:, c, :], dst[:, LEFT:LEFT + T], pooled_hi[:, c, :].bitcast(f32),
                                      ALU.subtract)
                link(ins)
            for tt, (t0, tw) in enumerate(THIRD):
                e.wait_ge(stdc_done, tt + 1)
                e.reciprocal(std_cv[:, t0:t0 + tw], std_cv[:, t0:t0 + tw]).then_inc(rstdc_done, 1)
            e.wait_ge(rstdc_done, NU)
            for cc in range(CC):
                e.tensor_tensor(cv[:, cc, :], cv[:, cc, :], std_cv[:, :], ALU.mult).then_inc(yc_done, 1)
            for cc in range(CC):
                e.wait_ge(s_hi_done, cc + 1)
                e.tensor_tensor(s_lo[:, cc, :], cv[:, cc, :], s_hi[:, cc, :].bitcast(f32), ALU.subtract)\
                    .then_inc(s_ready, 1)

            def mix_chunk(c):
                bc = cols[:, bass.ds(c + C_BC, 1)]
                ps = cols[:, bass.ds(c + C_PS, 1)]
                for tt, (t0, tw) in enumerate(THIRD):
                    g0, g1, g2 = (gate[:, br, t0:t0 + tw] for br in range(3))
                    u = c * (6 * NU) + (UNIT_MIX + 3 * NU + 3 * tt)
                    if tt == 0:
                        e.wait_ge(act_freed, c * (3 * NU) + 3 * NU)
                    e.wait_ge(unit_done, u + 1)
                    e.tensor_tensor(g2, psum[:, 0, 0:tw], g2, ALU.mult).then_inc(dve_freed, 1)
                    e.wait_ge(unit_done, u + 2)
                    e.scalar_tensor_tensor(out=g1, in0=psum[:, 1, 0:tw], scalar=ps, in1=g1,
                                           op0=ALU.mult, op1=ALU.mult).then_inc(dve_freed, 1)
                    e.wait_ge(dve_freed, c * (3 * NU) + (DVE_MIX + 3 * tt + 2))
                    e.tensor_tensor(g1, g1, g2, ALU.add).then_inc(mix_chain, 1)
                    e.wait_ge(unit_done, u + 3)
                    e.scalar_tensor_tensor(out=g0, in0=psum[:, 2, 0:tw], scalar=bc, in1=g0,
                                           op0=ALU.add, op1=ALU.mult).then_inc(dve_freed, 1)
                    e.wait_ge(dve_freed, c * (3 * NU) + (DVE_MIX + 3 * tt + 3))
                    e.wait_ge(mix_chain, c * NU + (tt + 1))
                    e.tensor_tensor(mixed[:, bass.ds(c, 1), t0:t0 + tw].rearrange("p a n -> p (a n)"), g0, g1, ALU.add)\
                        .then_inc(mix_done, 1)

            with e.Fori(0, KC) as c:
                mix_chunk(c)

            for tt, (t0, tw) in enumerate(THIRD):
                for b_, k in enumerate(range(0, KC, KC // 2)):
                    e.wait_ge(mix_hi_done, 2 * tt + b_ + 1)
                    e.tensor_tensor(mix_lo[:, k:k + KC // 2, t0:t0 + tw], mixed[:, k:k + KC // 2, t0:t0 + tw],
                                    mix_hi[:, k:k + KC // 2, t0:t0 + tw].bitcast(f32), ALU.subtract)\
                        .then_inc(mix_split, 1)

            for m in range(KC):
                for g, (c0, cn) in enumerate(THIRD):
                    n = NU * m + g
                    e.wait_ge(xt2_done, n + 1)
                    e.wait_ge(act_freed, ACT_OUT + (2 * NU if m < 2 else NU * (m + 1)))
                    e.tensor_tensor(h2[:, m, c0:c0 + cn], h2[:, m, c0:c0 + cn], psum[:, PZ[0] + n % 5, 0:cn], ALU.add)\
                        .then_inc(res_done, 1)
                if m >= 2:
                    mm = m - 1
                    e.wait_ge(sqh_done, mm + 1)
                    if mm >= 2:
                        e.wait_ge(ssum_done, mm - 1)
                    e.tensor_tensor(sq_sum[:, :], sq_sum[:, :], sq_h[:, :], ALU.add).then_inc(ssum_done, 1)
            for q, (c0, cn) in enumerate(THIRD):
                e.wait_ge(sqh_done, KC - 1 + q + 1)
                if q == 0:
                    e.wait_ge(ssum_done, KC - 2)
                e.tensor_tensor(sq_sum[:, c0:c0 + cn], sq_sum[:, c0:c0 + cn], sq_h[:, c0:c0 + cn], ALU.add)\
                    .then_inc(ssum_done, 1)
            for q, (c0, cn) in enumerate(THIRD):
                e.wait_ge(std2_done, q + 1)
                e.reciprocal(rstd2[:, c0:c0 + cn], rstd2[:, c0:c0 + cn]).then_inc(rstd2_done, 1)
                e.wait_ge(rstd2_done, q + 1)

                def lo_of(n):
                    k = n % KC
                    e.wait_ge(hn2_hi_done, n + 1)
                    e.scalar_tensor_tensor(out=hn_lo[:, k, c0:c0 + cn], in0=scaled[n % 2][:, 0:cn],
                                           scalar=cols[:, C_N2 + k:C_N2 + k + 1],
                                           in1=hn_hi[:, k, c0:c0 + cn].bitcast(f32),
                                           op0=ALU.mult, op1=ALU.subtract).then_inc(hn2_done, 1)

                for k in range(KC):
                    n = q * KC + k
                    if n >= 2:
                        e.wait_ge(hn2_done, n - 1)
                    e.tensor_tensor(scaled[n % 2][:, 0:cn], h2[:, k, c0:c0 + cn], rstd2[:, c0:c0 + cn], ALU.mult)\
                        .then_inc(scaled_done, 1)
                    if k >= 1:
                        lo_of(n - 1)
                lo_of(q * KC + KC - 1)

            for s in range(2):
                e.memset(up[s][:, 0:FTAPS - 1], 0.0).then_inc(up_pads_set, 1)
            e.wait_ge(up_pads_set, 2)

            def conv3(ch, e6, which):
                j = ch + which * FC
                tile_n = 2 * ch + which
                a_ = acc[2 * (e6 % 2) + which]
                e.wait_ge(act_freed, tile_n * NU + (ACT_FFN + NU))
                w1 = cols[:, bass.ds(j + (C_FW + 2 * FC), 1)]
                w0 = cols[:, bass.ds(j + C_FW, 1)]
                e.scalar_tensor_tensor(out=a_[:, :], in0=up[which][:, 1:1 + T], scalar=w1, in1=a_[:, :],
                                       op0=ALU.mult, op1=ALU.add).then_inc(tap_chain, 1)
                e.wait_ge(tap_chain, tile_n + 1)
                e.scalar_tensor_tensor(out=a_[:, :], in0=up[which][:, 0:T], scalar=w0, in1=a_[:, :],
                                       op0=ALU.mult, op1=ALU.add).then_inc(conv_done, 1)

            def product(ch, e6):
                g, v = acc[2 * (e6 % 2)], acc[2 * (e6 % 2) + 1]
                e.wait_ge(gelu_done, ch + 1)
                e.wait_ge(conv_done, 2 * ch + 2)
                e.tensor_tensor(v[:, :], g[:, :], v[:, :], ALU.mult).then_inc(prod_done, 1)

            def product_lo(ch, e6):
                v = acc[2 * (e6 % 2) + 1]
                e.wait_ge(g_hi_done, ch + 1)
                e.tensor_tensor(g_lo[:, e6 % RING, :], v[:, :], g_hi[:, e6 % RING, :].bitcast(f32), ALU.subtract)\
                    .then_inc(g_done, 1)

            def down(u, m):
                for tt, (t0, tw) in enumerate(THIRD):
                    e.wait_ge(unit_done, u + (NU * m + tt + 1))
                    e.tensor_tensor(h2[:, m, t0:t0 + tw], h2[:, m, t0:t0 + tw], psum[:, NU * (m % 2) + tt, 0:tw],
                                    ALU.add).then_inc(dve_freed, 1)

            def half_body(it, half, chunks):
                u = it * (2 * HALF_UNITS) + (UNIT_FFN + 2 * NU + half * HALF_UNITS + 2 * NU * chunks)
                for i in range(chunks):
                    e6 = 3 * half + 1 + i
                    ch = it * 6 + e6
                    conv3(ch, e6, 0)
                    conv3(ch, e6, 1)
                    spread = i == chunks - 1 and chunks == 3
                    if spread:
                        down(u, 0)
                    product(ch, e6)
                    if spread:
                        down(u, 1)
                    product_lo(ch, e6)
                for m in range(2 if chunks == 3 else 0, KC):
                    down(u, m)

            conv3(0, 0, 0)
            conv3(0, 0, 1)
            product(0, 0)
            product_lo(0, 0)
            with e.Fori(0, FC // 6 - 1) as it:
                half_body(it, 0, 3)
                half_body(it, 1, 3)
            half_body(FC // 6 - 1, 0, 3)
            half_body(FC // 6 - 1, 1, 2)

            def finish(i):
                e.wait_ge(stdo_done, i + 1)
                e.reciprocal(stat[:, NT + i:NT + i + 1], stat[:, NT + i:NT + i + 1]).then_inc(rstdo_done, 1)
                e.wait_ge(rstdo_done, i + 1)
                if i == 0:
                    e.wait_ge(final_g_in, 16)
                if i >= 3:
                    e.wait_ge(stored[i % 3], 16 * (i // 3))
                e.scalar_tensor_tensor(out=y_out[i % 3][:, :].rearrange("p (a n) -> p a n", a=2),
                                       in0=psum[:, 2 * (i % 4):2 * (i % 4) + 2, :], scalar=stat[:, NT + i:NT + i + 1],
                                       in1=final_g[:, :].rearrange("p (a n) -> p a n", a=2),
                                       op0=ALU.mult, op1=ALU.mult).then_inc(y_done, 1)

            for i in range(SEQ // P):
                e.wait_ge(sso_done, i + 1)
                e.tensor_scalar(stat[:, NT + i:NT + i + 1], stat[:, i:i + 1], 1.0 / DM, EPS, ALU.mult, ALU.add)\
                    .then_inc(mso_done, 1)
                if i >= 1:
                    finish(i - 1)
            finish(SEQ // P - 1)

        @block.tensor
        def _(e):
            def passes(dst, w_pair, r_pair, start, stop):
                (a_h, a_l), (r_h, r_l) = w_pair, r_pair
                e.matmul(dst, a_h, r_h, start=start, stop=False)
                e.matmul(dst, a_h, r_l, start=False, stop=False)
                return e.matmul(dst, a_l, r_h, start=False, stop=stop)

            def tiles(s, ks, rhs, tt, bank, j0=0, ks_rhs=None):
                t0, tw = THIRD[tt]
                for k in ks:
                    last = passes(psum[:, bank, 0:tw], (wh[s][:, k, :], wl[s][:, k, :]),
                                  (rhs[0][:, k, t0:t0 + tw], rhs[1][:, k, t0:t0 + tw]),
                                  start=k == 0, stop=k == KC - 1)
                return last

            hn = (hn_hi, hn_lo)

            e.wait_ge(params_in, 16 * 11)
            e.wait_ge(ident_set, 5)
            at = 0
            for slot, count in ((0, C_FW), (1, P), (2, NCOL - C_FW - P)):
                e.transpose(psum[:, PO, at:at + count], rows[0:count, slot, :], ident[0:count, 0:count])\
                    .then_inc(cols_t, 1)
                at += count

            def xn_transposes(g):
                i0, ni = GROUPS[g]
                e.wait_ge(xn_done, i0 + ni)
                for k in range(KC):
                    n = g * KC + k
                    if n >= 4:
                        e.wait_ge(hn_done, n - 3)
                    for i in range(i0, i0 + ni):
                        r = P if i < NT - 1 else REST
                        last = e.transpose(psum[:, 3 + n % 4, (i - i0) * P:(i - i0) * P + r],
                                           xn[0:r, i, k * P:(k + 1) * P], ident[0:r, 0:r])
                    last.then_inc(xt_done, 1)

            def conv_units(c, tt):
                if c == 0:
                    e.wait_ge(hn_done, KC * (tt + 1))
                for s in range(2):
                    u = 2 * NU * c + 2 * tt + s
                    if tt == 0:
                        e.wait_ge(w_lo_done, 2 * c + s + 1)
                    if u >= NU:
                        e.wait_ge(dve_freed, u - NU + 1)
                    last = tiles(s, range(KC), hn, tt, unit_bank(u))
                    last.then_inc(unit_done, 1)

            xn_transposes(0)
            xn_transposes(1)
            conv_units(0, 0)
            xn_transposes(2)
            for tt in range(1, NU):
                conv_units(0, tt)
            for c in range(1, CC):
                for tt in range(NU):
                    conv_units(c, tt)

            def head0_unit(j, tt):
                u = UNIT_Q0 + NU * j + tt
                if tt == 0:
                    e.wait_ge(w_lo_done, SLOT_Q0 + j + 1)
                e.wait_ge(dve_freed, u - NU + 1)
                last = tiles((SLOT_Q0 + j) % 2, range(KC), hn, tt, unit_bank(u))
                last.then_inc(unit_done, 1)

            for j in range(2):
                for tt in range(NU):
                    head0_unit(j, tt)

            def scores(t):
                h, (i, n) = t // NS, TILES[t % NS]
                p_ = h % 2
                if t >= 2:
                    e.wait_ge(z_copied, t - 1)
                if t % NS == 0:
                    e.wait_ge(dve_freed, UNIT_Q0 + 2 * NU + 1 if h == 0 else unit_att(h))
                    e.wait_ge(kv_pads_set, 5)
                ks, qs = slice(n * P, (n + 1) * P), slice(i * QW, (i + 1) * QW)
                passes(psum[:, PZ[t % 2], 0:QW], (k_hi[p_][:, ks], k_lo[p_][:, ks]), (q_hi[p_][:, qs], q_lo[p_][:, qs]),
                       True, True).then_inc(z_done, 1)

            def weigh(t):
                i, n = TILES[t % NS]
                e.wait_ge(a_split, t + 1)
                if FIRST[t % NS]:
                    n_o = (t // NS) * (T // QW) + i
                    if n_o >= 1:
                        e.wait_ge(o_evac, n_o)
                if t % NS == 0:
                    e.wait_ge(dve_freed, unit_att(t // NS) + NU)
                passes(psum[:, PO, 0:QW], (v_hi[:, n, :], v_lo[:, n, :]), (a_hi[t % 2][:, :], a_lo[t % 2][:, :]),
                       FIRST[t % NS], LAST[t % NS]).then_inc(o_mm, 1)

            def v_transposes(h, g):
                u = unit_att(h) + g
                i0, ni = VGROUPS[g]
                e.wait_ge(dve_freed, u - NU + 1)
                for i in range(i0, i0 + ni):
                    last = e.transpose(psum[:, unit_bank(u), (i - i0) * P:(i - i0 + 1) * P], vt[:, i * P:(i + 1) * P],
                                       ident[:, :])
                last.then_inc(unit_done, 1)

            def filler(h, idx):
                for n in range(fill_bound(h, idx), fill_bound(h, idx + 1)):
                    f, k = divmod(n, KC)
                    u, slot = unit_att(h) + NU + f, slot_att(h, f // NU)
                    if k == 0:
                        if f % NU == 0:
                            e.wait_ge(w_lo_done, slot + 1)
                        e.wait_ge(dve_freed, u - NU + 1)
                    last = tiles(slot % 2, [k], hn, f % NU, unit_bank(u))
                    if k == KC - 1:
                        last.then_inc(unit_done, 1)

            head0_unit(2, 0)
            head0_unit(2, 1)
            scores(0)
            head0_unit(2, 2)
            scores(1)
            v_transposes(0, 0)
            v_transposes(0, 1)
            e.wait_ge(masks_set, 2)
            for h in range(HEADS):
                for idx in range(NS):
                    t = h * NS + idx
                    bank = psum[:, PU[(HEADS * h + TILES[idx][0]) % 2], 0:QW]
                    e.wait_ge(sp_split, t + 1)
                    e.matmul(bank, neg_tri[:, :], sp_hi[t % 2][:, :], start=FIRST[idx], stop=False,
                             skip_group_check=True)
                    e.matmul(bank, neg_tri[:, :], sp_lo[t % 2][:, :], start=False, stop=True,
                             skip_group_check=True).then_inc(u_done, 1)
                    if t + 2 < STEPS:
                        scores(t + 2)
                    filler(h, idx)
                    if not LAST[idx]:
                        e.wait_ge(logit_done, t + 1)
                        e.matmul(bank, neg_rest[:, :], sp_hi[t % 2][:, :], start=False, stop=False,
                                 skip_group_check=True)
                        e.matmul(bank, neg_rest[:, :], sp_lo[t % 2][:, :], start=False, stop=True,
                                 skip_group_check=True)
                    if t >= 1:
                        weigh(t - 1)
                    if idx == 0:
                        v_transposes(h, 2)
                    if h < HEADS - 1 and idx in (NS - 3, NS - 2):
                        v_transposes(h + 1, idx - (NS - 3))
            weigh(STEPS - 1)

            def freed_in_mix(c, j):
                if j < NU or j >= 4 * NU:
                    e.wait_ge(dve_freed, c * (3 * NU) + (DVE_MIX + (j - NU + 1 if j < NU else j - 4 * NU + 1)))
                else:
                    e.wait_ge(act_freed, c * (3 * NU) + (j - NU + 1))

            def gate_unit(c, br, tt):
                n = c * 4 + (SLOT_MIX + br)
                j = NU * br + tt
                if tt == 0:
                    e.wait_ge(w_lo_done, n + 1)
                freed_in_mix(c, j)
                last = tiles(br % 2, range(KC), hn, tt, unit_bank(j))
                last.then_inc(unit_done, 1)

            def branch_units(c, first):
                n = c * 4 + (SLOT_MIX + 3)
                e.wait_ge(w_lo_done, n + 1)
                for tt, (t0, tw) in enumerate(THIRD):
                    j = 3 * NU + 3 * tt
                    ts = slice(t0, t0 + tw)
                    freed_in_mix(c, j)
                    for k in range(HEADS):
                        last = passes(psum[:, 0, 0:tw], (wh[1][:, k, :], wl[1][:, k, :]),
                                      (att_hi[:, k, ts], att_lo[:, k, ts]), k == 0, k == HEADS - 1)
                    last.then_inc(unit_done, 1)
                    freed_in_mix(c, j + 1)
                    pc = first
                    last = passes(psum[:, 1, 0:tw], (wh[1][:, HEADS + CC, :], wl[1][:, HEADS + CC, :]),
                                  (pooled_hi[:, pc, ts], pooled_lo[:, pc, ts]), True, True)
                    last.then_inc(unit_done, 1)
                    freed_in_mix(c, j + 2)
                    for k in range(CC):
                        last = passes(psum[:, 2, 0:tw], (wh[1][:, HEADS + k, :], wl[1][:, HEADS + k, :]),
                                      (s_hi[:, k, ts], s_lo[:, k, ts]), k == 0, k == CC - 1)
                    last.then_inc(unit_done, 1)

            e.wait_ge(conv_chain, 2 * TAPS * CC)
            for tt, (t0, tw) in enumerate(THIRD):
                for cc in range(CC):
                    last = e.matmul(psum[:, (PZ[0], PZ[1], PU[0])[tt], 0:tw], ones[:, :], cv[:, cc, t0:t0 + tw],
                                    start=cc == 0, stop=cc == CC - 1)
                last.then_inc(mu_done, 1)
            for tt, (t0, tw) in enumerate(THIRD):
                gate_unit(0, 0, tt)
                e.wait_ge(sqc_done, tt + 1)
                if tt == 1:
                    e.wait_ge(o_evac, HEADS * (T // QW))
                for cc in range(CC):
                    last = e.matmul(psum[:, (PU[1], PO, PZ[0])[tt], 0:tw], ones[:, :], sq_cv[:, cc, 0:tw],
                                    start=cc == 0, stop=cc == CC - 1)
                last.then_inc(var_done, 1)
            for br in (1, 2):
                for tt in range(NU):
                    gate_unit(0, br, tt)
            e.wait_ge(s_ready, CC)
            branch_units(0, 0)
            for pc in range(CC):
                with e.Fori(max(1, pc * KC // CC), (pc + 1) * KC // CC) as c:
                    for br in range(3):
                        for tt in range(NU):
                            gate_unit(c, br, tt)
                    branch_units(c, pc)

            def out_unit(i, m, tt):
                n = SLOT_OUT + m
                if i < 2 * NU:
                    for b_ in range(2):
                        e.wait_ge(mix_split, 2 * tt + b_ + 1)
                if i < NU:
                    e.wait_ge(dve_freed, DVE_FFN - NU + i + 1)
                else:
                    e.wait_ge(act_freed, ACT_OUT + i - NU + 1)
                e.wait_ge(w_lo_done, n + 1)
                last = tiles(m % 2, range(KC), (mix_hi, mix_lo), tt, unit_bank(i))
                last.then_inc(unit_done, 1)

            def x_transposes(m):
                for g, (i0, ni) in enumerate(GROUPS):
                    n = NU * m + g
                    if n >= 5:
                        e.wait_ge(res_done, n - 4)
                    for i in range(i0, i0 + ni):
                        if i < NT - 1:
                            last = e.transpose(psum[:, PZ[0] + n % 5, (i - i0) * P:(i - i0 + 1) * P],
                                               x_again[:, i, m * P:(m + 1) * P], ident[:, :])
                        else:
                            last = e.transpose(psum[:, PZ[0] + n % 5, (i - i0) * P:(i - i0) * P + REST], x_last[0:REST, m * P:(m + 1) * P],
                                               ident[0:REST, 0:REST])
                    last.then_inc(xt2_done, 1)

            i = 0
            for tt in range(NU):
                for m in range(2):
                    out_unit(i, m, tt)
                    i += 1
            e.wait_ge(x_again_in, 64)
            x_transposes(0)
            x_transposes(1)
            for m in range(2, KC):
                for tt in range(NU):
                    out_unit(i, m, tt)
                    i += 1
                x_transposes(m)
            for q, (c0, cn) in enumerate(THIRD):
                e.wait_ge(ssum_done, KC - 2 + q + 1)
                e.wait_ge(res_done, NU * KC)
                e.matmul(psum[:, PZ[0] + q, 0:cn], ones[:, :], sq_sum[:, c0:c0 + cn], start=True, stop=True)\
                    .then_inc(ss2_done, 1)

            def up_tile(n, s, ups, downs):
                e.wait_ge(w_lo_done, n + s + 1)
                for tt in range(NU):
                    if s < 2:
                        e.wait_ge(dve_freed, downs + (NU * (s - 2) + tt + 1))
                    else:
                        e.wait_ge(act_freed, ups + (NU * (s - 2) + tt + 1))
                    last = tiles(s % 2, range(KC), hn, tt, NU * (s % 2) + tt)
                    last.then_inc(unit_done, 1)

            def half_body(it, half, chunks):
                n0 = it * (2 * HALF_SLOTS) + (SLOT_FFN + 2 + half * HALF_SLOTS)
                ups = it * (2 * HALF_UP) + (ACT_FFN + 2 * NU + half * HALF_UP)
                dns = it * (2 * HALF_DOWN) + (DVE_FFN + half * HALF_DOWN)
                for s in range(2 * chunks):
                    up_tile(n0, s, ups, dns)
                e.wait_ge(g_done, it * 6 + (3 * half + 3))
                for m in range(KC):
                    s = (m // 2) % 2
                    if m % 2 == 0:
                        e.wait_ge(w_lo_done, n0 + (2 * chunks + m // 2 + 1))
                    for tt, (t0, tw) in enumerate(THIRD):
                        if m < 2:
                            e.wait_ge(act_freed, ups + (NU * (2 * chunks - 2 + m) + tt + 1))
                        else:
                            e.wait_ge(dve_freed, dns + (NU * (m - 2) + tt + 1))
                        for k in range(3):
                            r = (3 * half + k) % RING
                            last = passes(psum[:, NU * (m % 2) + tt, 0:tw],
                                          (wh[s][:, 2 * k + m % 2, :], wl[s][:, 2 * k + m % 2, :]),
                                          (g_hi[:, r, t0:t0 + tw], g_lo[:, r, t0:t0 + tw]), k == 0, k == 2)
                        last.then_inc(unit_done, 1)

            for which in range(2):
                n = SLOT_FFN + which
                e.wait_ge(w_lo_done, n + 1)
                for tt in range(NU):
                    if which == 0:
                        e.wait_ge(hn2_done, KC * (tt + 1))
                    if which == 0:
                        e.wait_ge(act_freed, ACT_FFN + NU * (which - 1) + tt + 1)
                    last = tiles(which, range(KC), hn, tt, NU * which + tt)
                    last.then_inc(unit_done, 1)
            with e.Fori(0, FC // 6 - 1) as it:
                half_body(it, 0, 3)
                half_body(it, 1, 3)
            half_body(FC // 6 - 1, 0, 3)
            half_body(FC // 6 - 1, 1, 2)

            e.wait_ge(dve_freed, DVE_FFN + HALF_DOWN * (FC // 3))
            for i in range(SEQ // P):
                if i >= 4:
                    e.wait_ge(y_done, i - 3)
                for k in range(KC):
                    last = e.transpose(psum[:, 2 * (i % 4) + k // 4, (k % 4) * P:(k % 4 + 1) * P],
                                       h2[:, k, NMETA + i * P:NMETA + (i + 1) * P], ident[:, :])
                last.then_inc(ht_done, 1)


_INS = ["x", "meta", "norm1", "w_in", "conv_dw_w", "conv_dw_b", "conv_ln_g", "conv_ln_b", "w_conv_out", "b_conv_out",
        "w_pool_grp", "pool_scale", "w_attn_out", "w_o", "norm2", "w_up", "ffn_dw_w", "ffn_dw_b", "w_down",
        "final_norm"]


def kernel(**inputs):
    import numpy as _np
    import concourse.bacc as _bacc
    from concourse import mybir as _mybir
    from concourse.bass_utils import run_bass_kernel_spmd as _run

    nc = _bacc.Bacc("TRN2", target_bir_lowering=False, num_devices=1)
    arrays, args = {}, []
    for name in _INS:
        a = _np.ascontiguousarray(inputs[name])
        arrays[f"in_{name}_dram"] = a
        args.append(nc.dram_tensor(f"in_{name}_dram", a.shape, _mybir.dt.from_np(a.dtype), kind="ExternalInput").ap())
    shape = arrays["in_x_dram"].shape
    out = nc.dram_tensor("out_dram", shape, _mybir.dt.float32, kind="ExternalOutput").ap()
    hybrid_trunk_kernel(nc, *args, out)
    r = _run(nc, [arrays], core_ids=[0])
    return r.results[0]["out_dram"]
```

```python
import concourse.bass as bass
from concourse import mybir
from contextlib import ExitStack


def hybrid_trunk_kernel(nc, x, meta, norm1, w_in, conv_dw_w, conv_dw_b, conv_ln_g, conv_ln_b, w_conv_out,
                        b_conv_out, w_pool_grp, pool_scale, w_attn_out, w_o, norm2, w_up, ffn_dw_w,
                        ffn_dw_b, w_down, final_norm, out):
    f32, f32r = mybir.dt.float32, mybir.dt.float32r
    ALU, ACT = mybir.AluOpType, mybir.ActivationFunctionType
    COPY = ACT.Copy

    P = 128
    SEQ, DM = x.shape[1], x.shape[2]
    NMETA = meta.shape[0]
    T = NMETA + SEQ
    KC = DM // P
    NT = -(-T // P)
    TP = NT * P
    REST = T - (NT - 1) * P
    TAPS, CONV = conv_dw_w.shape[1], conv_dw_w.shape[2]
    CC = CONV // P
    GRPS, GC, GOUT = w_pool_grp.shape[1:]
    POOLC = GRPS * GC
    WINDOWS = (2, 4, 8, 16)
    ATTW = w_attn_out.shape[1]
    DH = P
    HEADS = ATTW // DH
    FF = w_down.shape[1]
    FC = FF // P
    FTAPS = ffn_dw_w.shape[1]
    EPS = 1e-6
    SCALE = float(DH) ** -0.5
    COL_POOL = 2 * CONV
    COL_Q = COL_POOL + POOLC
    COL_K, COL_V, COL_GATE = COL_Q + ATTW, COL_Q + 2 * ATTW, COL_Q + 3 * ATTW

    GROUPS = [(i, 3) for i in range(0, NT, 3)]
    THIRD = [(i * P, min(ni * P, T - i * P)) for i, ni in GROUPS]
    NU = len(THIRD)
    TW = THIRD[0][1]
    QW = T // 4
    TILES = [(i, n) for i in range(T // QW) for n in reversed(range((QW * (i + 1) - 2) // P + 1))]
    LAST = [n == 0 for _, n in TILES]
    FIRST = [k == 0 or TILES[k - 1][0] != TILES[k][0] for k in range(len(TILES))]
    MASKED = [P * n + P - 1 >= QW * i for i, n in TILES]
    NS = len(TILES)
    STEPS = NS * HEADS
    MASKED_Z = -1e30
    FILL_STEPS = NS - 3
    VGROUPS = [(i, 3) for i in reversed(range(0, NT, 3))]

    C_N1, C_N2, C_BC, C_PS = 0, KC, 2 * KC, 3 * KC
    C_CB = 4 * KC
    C_LG, C_LB = C_CB + CC, C_CB + 2 * CC
    C_CW = C_CB + 3 * CC
    C_FW = C_CW + TAPS * CC
    C_FB = C_FW + FTAPS * 2 * FC
    NCOL = C_FB + 2 * FC

    SLOT_Q0 = 2 * CC
    SLOT_ATT = SLOT_Q0 + 3
    SLOT_MIX = SLOT_ATT + 3 * (HEADS - 1) + POOLC // P
    SLOT_OUT = SLOT_MIX + 4 * KC
    SLOT_FFN = SLOT_OUT + KC
    HALF_SLOTS = 6 + KC // 2
    SLOT_END = SLOT_FFN + 2 * FC + FC // 3 * (KC // 2)
    UNIT_Q0 = NU * SLOT_Q0
    UNIT_ATT = UNIT_Q0 + 3 * NU
    UNIT_MIX = UNIT_ATT + NU * HEADS + NU * (SLOT_MIX - SLOT_ATT)
    UNIT_OUT = UNIT_MIX + 2 * NU * 3 * KC
    UNIT_FFN = UNIT_OUT + NU * KC
    HALF_UP, HALF_DOWN = 6 * NU, NU * KC
    HALF_UNITS = HALF_UP + HALF_DOWN
    DVE_MIX = UNIT_MIX
    DVE_FFN = DVE_MIX + 3 * NU * KC
    ACT_OUT = 3 * NU * KC
    ACT_FFN = ACT_OUT + NU * KC

    OUT_ORDER = [(m, tt) for tt in range(NU) for m in (0, 1)] + \
                [(m, tt) for m in range(2, KC - 2) for tt in range(NU)] + \
                [(m, tt) for tt in range(NU) for m in (KC - 2, KC - 1)]
    TAIL = NU * (KC - 2)
    EARLY = KC // 2
    MIX_HI = [(1, 2, 4), (3, 5, 8), (6, 7, 9)]

    def slot_att(h, j):
        return SLOT_ATT + 3 * h + j

    def unit_att(h):
        return UNIT_ATT + (4 * NU) * h

    def slot_left(n):
        if n < SLOT_Q0:
            return 2 * NU * (n // 2 + 1) - 1 + n % 2
        if n < SLOT_ATT:
            return UNIT_Q0 + NU * (n - SLOT_Q0 + 1)
        if n < SLOT_MIX:
            h = min((n - SLOT_ATT) // 3, HEADS - 1)
            return unit_att(h) + NU + NU * (n - slot_att(h, 0) + 1)
        if n < SLOT_OUT:
            c, j = divmod(n - SLOT_MIX, 4)
            return UNIT_MIX + 6 * NU * c + (NU * (j + 1) if j < 3 else 6 * NU)
        if n < SLOT_FFN:
            return UNIT_OUT + OUT_ORDER.index((n - SLOT_OUT, NU - 1)) + 1
        assert n < SLOT_FFN + 2
        return UNIT_FFN + 2 * NU - 1 + n - SLOT_FFN

    def fillers(h):
        return 3 * NU if h < HEADS - 1 else NU * (POOLC // P)

    def fill_bound(h, idx):
        return -(-KC * fillers(h) * min(idx, FILL_STEPS) // FILL_STEPS)

    def fill_ended(h, idx):
        return range(fill_bound(h, idx - 1) // KC, fill_bound(h, idx) // KC) if idx >= 1 else range(0)

    def split_pieces(t, lag, parts):
        due = []
        for h in range(HEADS):
            for idx in range(NS):
                for f in fill_ended(h, idx):
                    piece = t - (h * NS + idx + lag)
                    if f % NU == NU - 1 and 0 <= piece < parts:
                        due.append((slot_att(h, f // NU) + 2, piece))
        return due

    B = 4
    ctx = ExitStack()
    with ctx:
        base = [-(-nc.sbuf_base // 32) * 32]

        def place(name, shape, dtype, at):
            return nc.alloc_sbuf_tensor_at(name, shape, dtype, offset=at)

        def take(name, shape, dtype=f32):
            n = B
            for s in shape[1:]:
                n *= s
            at = base[0]
            base[0] += -(-n // 32) * 32
            return place(name, shape, dtype, at)

        ident = take("ident", [P, P])
        ones = take("ones", [P, P])
        neg_tri = take("neg_tri", [P, P], f32r)
        neg_rest = take("neg_rest", [P, P], f32r)
        cols = take("cols", [P, NCOL])
        eps = take("eps", [P, 1])
        stat = take("stat", [P, 4 * NT])
        inv_cnt = take("inv_cnt", [P, CC, WINDOWS[-1]])
        raw = [take(f"raw{s}", [P, KC, P]) for s in range(2)]
        wh = [take(f"wh{s}", [P, KC, P], f32r) for s in range(2)]
        wl = [take(f"wl{s}", [P, KC, P], f32r) for s in range(2)]
        HN = base[0]
        hn_hi = take("hn_hi", [P, KC, T], f32r)
        hn_lo = take("hn_lo", [P, KC, T], f32r)
        ATT = base[0]
        att_hi = take("att_hi", [P, HEADS, T], f32r)
        att_lo = take("att_lo", [P, HEADS, T], f32r)
        R = base[0]
        U, UP = T * B, TP * B

        assert R + 20 * T * B <= nc.sbuf_usable_end, (R, nc.sbuf_usable_end)
        xn = place("xn", [P, NT, DM], f32, R)
        QK = 2 * U + 2 * UP
        q_hi = [place(f"q_hi{s}", [P, T], f32r, R + s * QK) for s in range(2)]
        q_lo = [place(f"q_lo{s}", [P, T], f32r, R + s * QK + U) for s in range(2)]
        k_hi = [place(f"k_hi{s}", [P, TP], f32r, R + s * QK + 2 * U) for s in range(2)]
        k_lo = [place(f"k_lo{s}", [P, TP], f32r, R + s * QK + 2 * U + UP) for s in range(2)]
        R_VT = R + 2 * QK
        vt = place("vt", [P, TP], f32, R_VT)
        R_V = R_VT + UP
        v_hi = place("v_hi", [P, NT, DH], f32r, R_V)
        v_lo = place("v_lo", [P, NT, DH], f32r, R_V + UP)
        R_TMP = R_V + 2 * UP
        W = -(-QW * B // 32) * 32
        zs = [place(f"zs{s}", [P, QW], f32, R_TMP + s * W) for s in range(3)]
        soft = [place(f"soft{s}", [P, QW], f32, R_TMP + (3 + s) * W) for s in range(2)]
        sp = place("sp", [P, QW], f32, R_TMP + 5 * W)
        sp_hi = [place(f"sp_hi{s}", [P, QW], f32r, R_TMP + (6 + s) * W) for s in range(2)]
        sp_lo = [place(f"sp_lo{s}", [P, QW], f32r, R_TMP + (8 + s) * W) for s in range(2)]
        att_w = [place(f"att_w{s}", [P, QW], f32, R_TMP + (10 + s) * W) for s in range(2)]
        a_hi = [place(f"a_hi{s}", [P, QW], f32r, R_TMP + (12 + s) * W) for s in range(2)]
        a_lo = [place(f"a_lo{s}", [P, QW], f32r, R_TMP + (14 + s) * W) for s in range(2)]
        sig = [place(f"sig{s}", [P, TW], f32, R_TMP + s * TW * B) for s in range(2)]
        rows = place("rows", [P, 3, P], f32, R_TMP + 3072)
        junk = [place(f"junk{s}", [P, DM], f32, R_TMP + 4608 + s * DM * B) for s in range(2)]
        mask32 = place("mask32", [P, 2, P], f32, R_TMP + 4608 + 2 * DM * B)
        R_CV = R_TMP + 16 * W
        cv = place("cv", [P, CC, T], f32, R_CV)
        R_PB = R_CV + CC * U
        LEFT = WINDOWS[-1]
        glu = place("glu", [P, CC, TAPS - 1 + T], f32, R_PB)
        assert R_PB + CC * (TAPS - 1 + T) * B <= nc.sbuf_usable_end
        pool_in = place("pool_in", [P, CC, LEFT + T], f32, R_PB)
        s_hi = place("s_hi", [P, CC, T], f32r, R)
        s_lo = place("s_lo", [P, CC, T], f32r, R + 2 * U)
        pooled_hi = place("pooled_hi", [P, CC, T], f32r, R + 4 * U)
        pooled_lo = place("pooled_lo", [P, CC, T], f32r, R + 6 * U)
        gate = place("gate", [P, 3, T], f32, R + 8 * U)
        pool_w = place("pool_w", [P, KC, P], f32, R + 11 * U)
        R_MIX = R + 11 * U + KC * P * B
        mixed = place("mixed", [P, KC, T], f32, R_MIX)
        win = [place(f"win{s}", [P, LEFT + T], f32, R_MIX + s * (LEFT + T) * B) for s in range(2)]
        sq_cv = place("sq_cv", [P, CC, TW], f32, R_MIX + 2 * (LEFT + T) * B)
        std_cv = place("std_cv", [P, T], f32, R_MIX + 2 * (LEFT + T) * B + CC * TW * B)
        assert R_MIX + 2 * (LEFT + T) * B + CC * TW * B + U <= R_CV
        mix_hi = place("mix_hi", [P, KC, T], f32r, HN)
        mix_lo = place("mix_lo", [P, KC, T], f32r, HN + KC * U)
        x_again = place("x_again", [P, NT - 1, DM], f32, ATT)
        h2 = place("h2", [P, KC, T], f32, R)
        x_last = place("x_last", [P, DM], f32, R + 8 * U)
        sq_h = place("sq_h", [P, T], f32, R + 9 * U)
        sq_sum = place("sq_sum", [P, T], f32, R + 10 * U)
        R_T4 = R_MIX
        rstd2 = place("rstd2", [P, T], f32, R_T4)
        scaled = [place(f"scaled{s}", [P, TW], f32, R_T4 + U + s * TW * B) for s in range(5)]
        sq_last = place("sq_last", [P, T], f32, R_T4 + U + 5 * TW * B)
        UW = -(-(FTAPS - 1 + T) // 8) * 8
        up = [place(f"up{s}", [P, UW], f32, ATT + s * UW * B) for s in range(2)]
        acc = [place(f"acc{s}", [P, T], f32, ATT + 2 * UW * B + s * U) for s in range(4)]
        final_g = place("final_g", [P, DM], f32, ATT + 2 * UW * B + 4 * U)
        assert 2 * UW * B + 4 * U + DM * B <= 8 * U
        RING = 6
        g_hi = place("g_hi", [P, RING, T], f32r, R + 8 * U)
        g_lo = place("g_lo", [P, RING, T], f32r, R + 14 * U)
        sq_out = [place(f"sq_out{s}", [P, DM], f32, HN + s * DM * B) for s in range(2)]
        y_out = [place(f"y_out{s}", [P, DM], f32, HN + (2 + s) * DM * B) for s in range(3)]

        psum = ctx.enter_context(nc.psum_tensor("psum", [P, 8, 512], f32))
        PZ, PU, PO = [3, 4], [5, 6], 7

        def sem(name):
            return ctx.enter_context(nc.semaphore(name))

        x_in = [sem(f"x_in{g}") for g in range(3)]
        params_in = sem("params_in")
        raw_in = [sem("raw_in0"), sem("raw_in1")]
        pool_w_in = sem("pool_w_in")
        x_again_in = sem("x_again_in")
        final_g_in = sem("final_g_in")
        stored = [sem(f"stored{s}") for s in range(3)]
        ident_set = sem("ident_set")
        masks32_set = sem("masks32_set")
        masks_set = sem("masks_set")
        cols_t = sem("cols_t")
        cols_set = sem("cols_set")
        glu_pad_set = sem("glu_pad_set")
        kv_pads_set = sem("kv_pads_set")
        pool_pad_set = sem("pool_pad_set")
        up_pads_set = sem("up_pads_set")
        pool_w_zeroed = sem("pool_w_zeroed")
        cnt_set = sem("cnt_set")
        x_ss = sem("x_ss")
        x_ms = sem("x_ms")
        x_std = sem("x_std")
        x_rstd = sem("x_rstd")
        xn_done = sem("xn_done")
        xt_done = sem("xt_done")
        hn_hi_done = sem("hn_hi_done")
        hn_done = sem("hn_done")
        w_hi_done = sem("w_hi_done")
        w_lo_done = sem("w_lo_done")
        unit_done = sem("unit_done")
        act_freed = sem("act_freed")
        dve_freed = sem("dve_freed")
        evac_hi = sem("evac_hi")
        sig_done = sem("sig_done")
        conv_chain = sem("conv_chain")
        z_done = sem("z_done")
        z_copied = sem("z_copied")
        z_masked = sem("z_masked")
        abs_done = sem("abs_done")
        exp_done = sem("exp_done")
        log_done = sem("log_done")
        sp_done = sem("sp_done")
        sp_hi_done = sem("sp_hi_done")
        sp_split = sem("sp_split")
        u_done = sem("u_done")
        logit_done = sem("logit_done")
        a_done = sem("a_done")
        a_hi_done = sem("a_hi_done")
        a_split = sem("a_split")
        o_mm = sem("o_mm")
        o_hi_done = sem("o_hi_done")
        o_evac = sem("o_evac")
        mu_done = sem("mu_done")
        xc_done = sem("xc_done")
        sqc_done = sem("sqc_done")
        var_done = sem("var_done")
        stdc_done = sem("stdc_done")
        rstdc_done = sem("rstdc_done")
        yc_done = sem("yc_done")
        silu_done = sem("silu_done")
        s_hi_done = sem("s_hi_done")
        s_ready = sem("s_ready")
        win_chain = sem("win_chain")
        pooled_ready = sem("pooled_ready")
        mix_chain = sem("mix_chain")
        mix_done = sem("mix_done")
        mix_hi_done = sem("mix_hi_done")
        mix_split = sem("mix_split")
        mix_lo_early = sem("mix_lo_early")
        xt2_done = sem("xt2_done")
        res_done = sem("res_done")
        sqh_done = sem("sqh_done")
        ssum_done = sem("ssum_done")
        ss2_done = sem("ss2_done")
        std2_done = sem("std2_done")
        rstd2_done = sem("rstd2_done")
        scaled_done = sem("scaled_done")
        scaled_pool = sem("scaled_pool")
        hn2_hi_done = sem("hn2_hi_done")
        hn2_done = sem("hn2_done")
        up_evac = sem("up_evac")
        tap_chain = sem("tap_chain")
        conv_done = sem("conv_done")
        gelu_done = sem("gelu_done")
        prod_done = sem("prod_done")
        g_hi_done = sem("g_hi_done")
        g_done = sem("g_done")
        ht_done = sem("ht_done")
        sso_done = sem("sso_done")
        mso_done = sem("mso_done")
        stdo_done = sem("stdo_done")
        rstdo_done = sem("rstdo_done")
        y_done = sem("y_done")

        block = ctx.enter_context(nc.Block())

        def unit_bank(j):
            return j % NU

        @block.sync
        def _(sp_eng):
            e = sp_eng

            def load(n, src, dst, again=0):
                if not (isinstance(n, int) and n < 2):
                    e.wait_ge(w_lo_done, n - 1)
                e.dma_start(dst, src).then_inc(raw_in[again], 16)

            def at_col(value):
                if isinstance(value, int):
                    return value
                return e.snap(value)

            def w_tile(w, col, width=P):
                return w[0].rearrange("(k p) n -> p k n", p=P)[:, :, bass.ds(col, width)]

            def full(s):
                return raw[s][:, :, :]

            first = NMETA
            e.dma_start(xn[0:first, 0, :], meta).then_inc(x_in[0], 16)
            e.dma_start(xn[first:P, 0, :], x[0, 0:P - first, :]).then_inc(x_in[0], 16)
            a = P - first
            e.dma_start(xn[:, 1:3, :], x[0, a:a + 2 * P, :].rearrange("(i p) d -> p i d", p=P)).then_inc(x_in[0], 16)
            load(0, w_tile(w_in, 0), full(0), 0)
            load(1, w_tile(w_in, CONV), full(1), 1)
            e.wait_ge(params_in, 16 * 11)
            for g in (1, 2):
                b, n_whole = a + (3 * g - 1) * P, min(3, NT - 1 - 3 * g)
                e.dma_start(xn[:, 3 * g:3 * g + n_whole, :],
                            x[0, b:b + n_whole * P, :].rearrange("(i p) d -> p i d", p=P)).then_inc(x_in[g], 16)
            e.dma_start(xn[0:REST, NT - 1, :], x[0, SEQ - REST:SEQ, :]).then_inc(x_in[2], 16)
            for c in range(1, CC):
                load(2 * c, w_tile(w_in, c * P), full(0), 0)
                load(2 * c + 1, w_tile(w_in, CONV + c * P), full(1), 1)
            for j, col in enumerate((COL_V, COL_K, COL_Q)):
                n = SLOT_Q0 + j
                load(n, w_tile(w_in, col), full(n % 2), n % 2)
            for h in range(HEADS):
                cs = [c + (h + 1) * DH for c in (COL_V, COL_K, COL_Q)] if h < HEADS - 1 else \
                     [COL_POOL + c * P for c in range(POOLC // P)]
                for j, col in enumerate(cs):
                    n = slot_att(h, j)
                    load(n, w_tile(w_in, col), full(n % 2), n % 2)
            def load_gate(c, br):
                col = at_col(c * P + (COL_GATE + br * DM))
                e.wait_ge(w_lo_done, c * 4 + (SLOT_MIX + br - 1))
                e.dma_start(full(br % 2), w_tile(w_in, col)).then_inc(raw_in[br % 2], 16)

            load_gate(0, 0)
            load_gate(0, 1)
            e.wait_ge(pool_w_zeroed, 1)
            for g in range(GRPS):
                half = GC * (g % 2)
                per = GOUT // P
                e.dma_start(pool_w[half:half + GC, per * g:per * (g + 1), :],
                            w_pool_grp[0, g, :, :].rearrange("k (c n) -> k c n", n=P)).then_inc(pool_w_in, 16)
            load_gate(0, 2)
            with e.Fori(1, KC) as c:
                for br in range(3):
                    load_gate(c, br)
            for m in range(2):
                load(SLOT_OUT + m, w_tile(w_o, m * P), full(m % 2), m % 2)
            e.wait_ge(unit_done, UNIT_OUT)
            e.wait_ge(mix_done, NU * KC)
            e.dma_start(x_again[0:first, 0, :], meta).then_inc(x_again_in, 16)
            e.dma_start(x_again[first:P, 0, :], x[0, 0:P - first, :]).then_inc(x_again_in, 16)
            e.dma_start(x_again[:, 1:NT - 1, :],
                        x[0, a:a + (NT - 2) * P, :].rearrange("(i p) d -> p i d", p=P)).then_inc(x_again_in, 16)
            e.dma_start(x_last[0:REST, :], x[0, SEQ - REST:SEQ, :]).then_inc(x_again_in, 16)
            for m in range(2, KC):
                load(SLOT_OUT + m, w_tile(w_o, m * P), full(m % 2), m % 2)

            def load_up(n, j):
                for s in range(2):
                    col = at_col(j * P + s * FF)
                    load(n + s, w_tile(w_up, col), full(s), s)

            def load_half(n, j0, chunks):
                for i in range(chunks):
                    load_up(n + 2 * i, j0 + (1 + i))
                row = at_col(j0 * P)
                for m in range(KC // 2):
                    load(n + (2 * chunks + m),
                         w_down[0, bass.ds(row, 3 * P), m * 2 * P:(m + 1) * 2 * P].rearrange("(k p) n -> p k n", p=P),
                         raw[m % 2][:, 0:6, :].rearrange("p (k m) n -> p k (m n)", k=3), m % 2)

            load_up(SLOT_FFN, 0)
            e.wait_ge(xt2_done, NU * KC)
            e.dma_start(final_g[:, :], final_norm.partition_broadcast(P)).then_inc(final_g_in, 16)
            with e.Fori(0, FC // 6 - 1) as it:
                for half in range(2):
                    load_half(it * (2 * HALF_SLOTS) + (SLOT_FFN + 2 + half * HALF_SLOTS), it * 6 + 3 * half, 3)
            it = FC // 6 - 1
            for half in range(2):
                load_half(it * (2 * HALF_SLOTS) + (SLOT_FFN + 2 + half * HALF_SLOTS), it * 6 + 3 * half, 3 - half)
            for i in range(SEQ // P):
                e.wait_ge(y_done, i + 1)
                e.dma_start(out[0, i * P:(i + 1) * P, :], y_out[i % 3][:, :]).then_inc(stored[i % 3], 16)
            for s in range(3):
                e.wait_ge(stored[s], 16 * len(range(s, SEQ // P, 3)))

        @block.gpsimd
        def _(e):
            def split_lo(n):
                s = n % 2
                e.wait_ge(w_hi_done, n + 1)
                e.tensor_tensor(wl[s][:, :, :], raw[s][:, :, :], wh[s][:, :, :].bitcast(f32), ALU.subtract)\
                    .then_inc(w_lo_done, 1)

            def split_lo_at(s, n, tiles=KC):
                e.wait_ge(w_hi_done, n + 1)
                e.tensor_tensor(wl[s][:, 0:tiles, :], raw[s][:, 0:tiles, :], wh[s][:, 0:tiles, :].bitcast(f32),
                                ALU.subtract).then_inc(w_lo_done, 1)

            e.memset(ident[:, :], 0.0).then_inc(ident_set, 1)
            e.memset(ones[:, :], 1.0).then_inc(ident_set, 1)
            e.memset(eps[:, :], EPS).then_inc(ident_set, 1)
            e.memset(stat[:, :], 1.0).then_inc(ident_set, 1)
            e.wait_ge(ident_set, 4)
            e.affine_select(out=ident[:, :], in_=ident[:, :], compare_op=ALU.not_equal, fill=1.0, base=0,
                            pattern=[[-1, P]], channel_multiplier=1).then_inc(ident_set, 1)
            e.memset(mask32[:, :, :], -1.0).then_inc(masks32_set, 1)
            e.wait_ge(masks32_set, 1)
            e.affine_select(out=mask32[:, 0, :], in_=mask32[:, 0, :], compare_op=ALU.is_ge, fill=0.0, base=0,
                            pattern=[[-1, P]], channel_multiplier=1).then_inc(masks32_set, 1)
            e.affine_select(out=mask32[:, 1, :], in_=mask32[:, 1, :], compare_op=ALU.is_gt, fill=0.0, base=0,
                            pattern=[[1, P]], channel_multiplier=-1).then_inc(masks32_set, 1)
            e.memset(glu[:, :, 0:TAPS - 1], 0.0).then_inc(glu_pad_set, 1)
            e.iota(inv_cnt[:, :, :], pattern=[[0, CC], [1, LEFT]], base=1, channel_multiplier=0,
                   allow_small_or_imprecise_dtypes=True).then_inc(cnt_set, 1)
            split_lo(0)
            split_lo(1)
            e.wait_ge(xt_done, KC * len(GROUPS))
            for s in range(2):
                e.memset(k_hi[s][:, T:TP].bitcast(f32), 0.0).then_inc(kv_pads_set, 1)
                e.memset(k_lo[s][:, T:TP].bitcast(f32), 0.0).then_inc(kv_pads_set, 1)
            e.memset(vt[:, T:TP], 0.0).then_inc(kv_pads_set, 1)
            for n in range(2, SLOT_ATT + 1):
                split_lo(n)

            def mask_z(t):
                i, n = TILES[t % NS]
                if MASKED[t % NS]:
                    e.wait_ge(z_copied, t + 1)
                    e.affine_select(out=zs[t % 3][:, :], in_=zs[t % 3][:, :], compare_op=ALU.is_gt, fill=MASKED_Z,
                                    base=QW * i - P * n, pattern=[[1, QW]], channel_multiplier=-1)\
                        .then_inc(z_masked, 1)

            PIECES = ((0, 3), (3, 6), (6, KC))

            def lo_pieces(t):
                for n, piece in split_pieces(t, 2, len(PIECES)):
                    s, (k0, k1) = n % 2, PIECES[piece]
                    e.wait_ge(w_hi_done, n + 1)
                    ins = e.tensor_tensor(wl[s][:, k0:k1, :], raw[s][:, k0:k1, :], wh[s][:, k0:k1, :].bitcast(f32),
                                          ALU.subtract)
                    if piece == len(PIECES) - 1:
                        ins.then_inc(w_lo_done, 1)

            mask_z(0)
            mask_z(1)
            split_lo(SLOT_ATT + 1)
            for h in range(HEADS):
                if h == HEADS - 1:
                    e.wait_ge(conv_chain, 2 * TAPS * CC)
                    e.memset(pool_in[:, :, 0:LEFT], 0.0).then_inc(pool_pad_set, 1)
                for idx in range(NS):
                    t = h * NS + idx
                    if t + 2 < STEPS:
                        mask_z(t + 2)
                    e.wait_ge(a_hi_done, t + 1)
                    if t >= 2:
                        e.wait_ge(o_mm, t - 1)
                    e.tensor_tensor(a_lo[t % 2][:, :], att_w[t % 2][:, :], a_hi[t % 2][:, :].bitcast(f32),
                                    ALU.subtract).then_inc(a_split, 1)
                    lo_pieces(t)
            for t in range(STEPS, STEPS + 5):
                lo_pieces(t)
            e.wait_ge(o_evac, HEADS * (T // QW))
            e.memset(pool_w[:, :, :], 0.0).then_inc(pool_w_zeroed, 1)

            def splits_of_chunk(c):
                n = SLOT_MIX + c * 4
                split_lo_at(0, n + 2)
                split_lo_at(1, n + 3, HEADS + CC + 1)
                split_lo_at(0, n + 4)

            with e.Fori(0, KC - 1) as c:
                splits_of_chunk(c)
                split_lo_at(1, SLOT_MIX + c * 4 + 5)
            splits_of_chunk(KC - 1)
            for tt, (t0, tw) in enumerate(THIRD):
                e.wait_ge(mix_hi_done, MIX_HI[tt][0])
                e.tensor_tensor(mix_lo[:, 0:EARLY, t0:t0 + tw], mixed[:, 0:EARLY, t0:t0 + tw],
                                mix_hi[:, 0:EARLY, t0:t0 + tw].bitcast(f32), ALU.subtract).then_inc(mix_lo_early, 1)
                if tt == 0:
                    split_lo(SLOT_OUT + 1)
            for m in range(2, KC):
                split_lo(SLOT_OUT + m)
            for q, (c0, cn) in enumerate(THIRD):
                for k in range(2, KC):
                    p_ = (KC - 2) * q + k - 2
                    e.wait_ge(rstd2_done, q + 1)
                    if p_ >= 3:
                        e.wait_ge(hn2_done, (p_ - 3) // (KC - 2) * KC + 2 + (p_ - 3) % (KC - 2) + 1)
                    e.tensor_tensor(scaled[2 + p_ % 3][:, 0:cn], h2[:, k, c0:c0 + cn], rstd2[:, c0:c0 + cn], ALU.mult)\
                        .then_inc(scaled_pool, 1)
                if q == 0:
                    split_lo(SLOT_FFN)
                    split_lo(SLOT_FFN + 1)

            split_lo(SLOT_FFN + 2)
            split_lo(SLOT_FFN + 3)

            def split_half(n, chunks, tail=0):
                for i in range(2 * chunks - 2):
                    split_lo_at(i % 2, n + i)
                for m in range(KC // 2):
                    split_lo_at(m % 2, n + (2 * chunks - 2 + m), 6)
                for i in range(2 - tail):
                    split_lo_at(i % 2, n + (2 * chunks - 2 + KC // 2 + i))

            with e.Fori(0, FC // 6 - 1) as it:
                for half in range(2):
                    split_half(it * (2 * HALF_SLOTS) + (SLOT_FFN + 4 + half * HALF_SLOTS), 3)
            n = SLOT_FFN + 4 + (FC // 6 - 1) * 2 * HALF_SLOTS
            split_half(n, 3)
            split_half(n + HALF_SLOTS, 2, tail=2)

        @block.scalar
        def _(e):
            raw_count = [0, 0]

            def split_hi(n, tiles=KC, dmas=1):
                s = n % 2
                raw_count[s] += 16 * dmas
                e.wait_ge(raw_in[s], raw_count[s])
                if n >= 2:
                    e.wait_ge(unit_done, slot_left(n - 2))
                e.activation(wh[s][:, 0:tiles, :], raw[s][:, 0:tiles, :], COPY).then_inc(w_hi_done, 1)

            def split_hi_at(s, left, raw_value, tiles=KC):
                e.wait_ge(raw_in[s], raw_value)
                e.wait_ge(unit_done, left)
                e.activation(wh[s][:, 0:tiles, :], raw[s][:, 0:tiles, :], COPY).then_inc(w_hi_done, 1)

            e.preload_act_table_set("sqrt_and_others")
            def rows_in(slot, at, count, src):
                e.dma_start(rows[at:at + count, slot, :], src).then_inc(params_in, 16)

            n_params = 0
            for at, p in ((C_N1, norm1), (C_N2, norm2), (C_BC, b_conv_out), (C_PS, pool_scale)):
                rows_in(0, at, KC, p[0].rearrange("(k p) -> k p", p=P))
                n_params += 1
            for at, p in ((C_CB, conv_dw_b), (C_LG, conv_ln_g), (C_LB, conv_ln_b)):
                rows_in(0, at, CC, p[0].rearrange("(k p) -> k p", p=P))
                n_params += 1
            rows_in(0, C_CW, TAPS * CC, conv_dw_w[0].rearrange("t (k p) -> (t k) p", p=P))
            fw = ffn_dw_w[0].rearrange("t (k p) -> (t k) p", p=P)
            rows_in(1, 0, P, fw[0:P, :])
            rows_in(2, 0, FTAPS * 2 * FC - P, fw[P:FTAPS * 2 * FC, :])
            rows_in(2, FTAPS * 2 * FC - P, 2 * FC, ffn_dw_b[0].rearrange("(k p) -> k p", p=P))

            def hn_hi_group(g, ks=range(KC)):
                c0, cn = THIRD[g]
                for k in ks:
                    n = g * KC + k
                    if n == 0:
                        e.wait_ge(cols_set, 1)
                    e.wait_ge(xt_done, n + 1)
                    e.activation(hn_hi[:, k, c0:c0 + cn], psum[:, 3 + n % 4, 0:cn], COPY,
                                 scale=cols[:, C_N1 + k:C_N1 + k + 1]).then_inc(hn_hi_done, 1)

            def token_squares(g):
                i0, ni = GROUPS[g]
                e.wait_ge(x_in[g], (48, 16, 32)[g])
                for i in range(i0, i0 + ni):
                    r = P if i < NT - 1 else REST
                    if i == 0:
                        e.wait_ge(ident_set, 4)
                    if i >= 2:
                        e.wait_ge(x_ss, i - 1)
                    e.activation(junk[i % 2][0:r, :], xn[0:r, i, :], ACT.Square, accum_out=stat[0:r, i:i + 1])\
                        .then_inc(x_ss, 1)

            def token_std(g):
                i0, ni = GROUPS[g]
                e.wait_ge(x_ms, g + 1)
                e.activation(stat[:, NT + i0:NT + i0 + ni], stat[:, NT + i0:NT + i0 + ni], ACT.Sqrt)\
                    .then_inc(x_std, 1)

            token_squares(0)
            token_std(0)
            split_hi(0)
            split_hi(1)
            hn_hi_group(0)
            token_squares(1)
            token_std(1)
            hn_hi_group(1, range(0, KC // 2))
            token_squares(2)
            hn_hi_group(1, range(KC // 2, KC))
            token_std(2)

            def conv_gate(c, tt):
                t0, tw = THIRD[tt]
                n = NU * c + tt
                e.wait_ge(unit_done, 2 * n + 2)
                if n >= 2:
                    e.wait_ge(dve_freed, 2 * (n - 1))
                e.activation(sig[n % 2][:, 0:tw], psum[:, unit_bank(2 * n + 1), 0:tw], ACT.Sigmoid)\
                    .then_inc(sig_done, 1)

            conv_gate(0, 0)
            hn_hi_group(2)
            for c in range(CC):
                for tt in range(0 if c else 1, NU):
                    if tt == NU - 1:
                        split_hi(2 * c + 2)
                    conv_gate(c, tt)
                split_hi(2 * c + 3)

            def qk_hi(u, dst, tt, scale):
                t0, tw = THIRD[tt]
                e.wait_ge(unit_done, u + 1)
                e.activation(dst[:, t0:t0 + tw], psum[:, unit_bank(u), 0:tw], COPY, scale=scale)\
                    .then_inc(evac_hi, 1)

            seen_masks = [0]

            def log_of(t):
                b_ = soft[t % 2]
                e.wait_ge(z_copied, t + 1)
                if MASKED[t % NS]:
                    seen_masks[0] += 1
                    e.wait_ge(z_masked, seen_masks[0])
                if t >= 2:
                    e.wait_ge(sp_done, t - 1)
                e.activation(b_[:, :], zs[t % 3][:, :], ACT.Abs).then_inc(abs_done, 1)
                e.wait_ge(abs_done, t + 1)
                e.activation(b_[:, :], b_[:, :], ACT.Exp, scale=-1.0).then_inc(exp_done, 1)
                e.wait_ge(exp_done, t + 1)
                e.activation(b_[:, :], b_[:, :], ACT.Ln, bias=1.0).then_inc(log_done, 1)

            def copy_z(t):
                e.wait_ge(z_done, t + 1)
                if t >= 3:
                    e.wait_ge(logit_done, t - 2)
                e.activation(zs[t % 3][:, :], psum[:, PZ[t % 2], 0:QW], COPY).then_inc(z_copied, 1)

            for j in range(2):
                for tt in range(NU):
                    if j == 1:
                        qk_hi(UNIT_Q0 + NU * j + tt, k_hi[0], tt, 1.0)
                split_hi(SLOT_Q0 + j + 2)
            e.preload_act_table_set("natural_log_exp_and_others")
            for tt in range(NU):
                qk_hi(UNIT_Q0 + 2 * NU + tt, q_hi[0], tt, SCALE)
                if tt >= 1:
                    copy_z(tt - 1)
                    log_of(tt - 1)

            def v_hi_group(h, g):
                u = unit_att(h) + g
                i0, ni = VGROUPS[g]
                e.wait_ge(unit_done, u + 1)
                e.activation(v_hi[:, i0:i0 + ni, :],
                             psum[:, unit_bank(u), 0:ni * P].rearrange("p (n d) -> p n d", d=DH), COPY)\
                    .then_inc(evac_hi, 1)

            def hi_pieces(t):
                for n, piece in split_pieces(t, 0, 2):
                    s, half = n % 2, KC // 2
                    if piece == 0:
                        raw_count[s] += 16
                        e.wait_ge(raw_in[s], raw_count[s])
                        e.wait_ge(unit_done, slot_left(n - 2))
                    ks = slice(piece * half, (piece + 1) * half)
                    ins = e.activation(wh[s][:, ks, :], raw[s][:, ks, :], COPY)
                    if piece == 1:
                        ins.then_inc(w_hi_done, 1)

            v_hi_group(0, 0)
            v_hi_group(0, 1)
            split_hi(SLOT_Q0 + 4)
            for h in range(HEADS):
                for idx in range(NS):
                    t = h * NS + idx
                    if t + 2 < STEPS:
                        copy_z(t + 2)
                    e.wait_ge(logit_done, t + 1)
                    e.activation(att_w[t % 2][:, :], att_w[t % 2][:, :], ACT.Exp).then_inc(a_done, 1)
                    if t >= 1 and LAST[(t - 1) % NS]:
                        hh, i = (t - 1) // NS, TILES[(t - 1) % NS][0]
                        e.wait_ge(o_mm, t)
                        e.activation(att_hi[:, hh, QW * i:QW * (i + 1)], psum[:, PO, 0:QW], COPY)\
                            .then_inc(o_hi_done, 1)
                    for f in fill_ended(h, idx):
                        if h < HEADS - 1 and f >= NU:
                            qk_hi(unit_att(h) + NU + f, (k_hi, q_hi)[f // NU - 1][(h + 1) % 2], f % NU,
                                  (1.0, SCALE)[f // NU - 1])
                    if h < HEADS - 1 and idx >= NS - 2:
                        v_hi_group(h + 1, idx - (NS - 2))
                    if t + 2 < STEPS:
                        log_of(t + 2)
                    if idx == 0:
                        v_hi_group(h, 2)
                    hi_pieces(t)
            e.wait_ge(o_mm, STEPS)
            e.activation(att_hi[:, HEADS - 1, T - QW:T], psum[:, PO, 0:QW], COPY).then_inc(o_hi_done, 1)

            RAW_MIX = list(raw_count)

            def gate_evac(c, j):
                t0, tw = THIRD[j % NU]
                u = c * (6 * NU) + (UNIT_MIX + j)
                e.wait_ge(unit_done, u + 1)
                e.activation(gate[:, j // NU, t0:t0 + tw], psum[:, unit_bank(j), 0:tw], ACT.Sigmoid)\
                    .then_inc(act_freed, 1)

            def splits_mix(c, which):
                left = c * (6 * NU) + (UNIT_MIX + (NU * (which + 1) if which < 3 else 6 * NU))
                if which == 0:
                    split_hi_at(0, left, c * 32 + (RAW_MIX[0] + 16))
                if which == 1:
                    e.wait_ge(raw_in[1], c * 48 + (RAW_MIX[1] + 32))
                    e.wait_ge(unit_done, left)
                    e.activation(wh[1][:, 0:HEADS + CC, :], raw[1][:, 0:HEADS + CC, :], COPY)
                    e.activation(raw[1][:, HEADS + CC, :], pool_w[:, bass.ds(c, 1), :].rearrange("p a n -> p (a n)"),
                                 COPY)
                    e.activation(wh[1][:, HEADS + CC, :], pool_w[:, bass.ds(c, 1), :].rearrange("p a n -> p (a n)"),
                                 COPY).then_inc(w_hi_done, 1)
                if which == 2:
                    split_hi_at(0, left, c * 32 + (RAW_MIX[0] + 32))
                if which == 3:
                    split_hi_at(1, left, c * 48 + (RAW_MIX[1] + 48))

            def load_branch_tiles(c):
                e.wait_ge(w_lo_done, c * 4 + (SLOT_MIX + 2))
                for k, kn, w in ((0, HEADS, w_attn_out), (HEADS, CC, w_conv_out)):
                    e.dma_start(raw[1][:, k:k + kn, :],
                                w[0].rearrange("(k p) n -> p k n", p=P)[:, :, bass.ds(c * P, P)])\
                        .then_inc(raw_in[1], 16)

            load_branch_tiles(0)
            for tt, (t0, tw) in enumerate(THIRD):
                e.wait_ge(xc_done, CC * (tt + 1))
                if tt >= 1:
                    e.wait_ge(var_done, tt)
                e.activation(sq_cv[:, :, 0:tw], cv[:, :, t0:t0 + tw], ACT.Square).then_inc(sqc_done, 1)
                gate_evac(0, tt)
            for tt, (t0, tw) in enumerate(THIRD):
                e.wait_ge(var_done, tt + 1)
                e.activation(std_cv[:, t0:t0 + tw], psum[:, (PU[1], PO, PZ[0])[tt], 0:tw], ACT.Sqrt,
                             scale=1.0 / CONV, bias=eps[:, :]).then_inc(stdc_done, 1)
            e.wait_ge(pool_w_in, 16 * GRPS)
            splits_mix(0, 0)
            for j in range(NU, 2 * NU):
                gate_evac(0, j)
            splits_mix(0, 1)
            gate_evac(0, 2 * NU)
            e.wait_ge(yc_done, CC)
            for cc in range(CC):
                e.activation(cv[:, cc, :], cv[:, cc, :], ACT.Silu, scale=cols[:, C_LG + cc:C_LG + cc + 1],
                             bias=cols[:, C_LB + cc:C_LB + cc + 1]).then_inc(silu_done, 1)
            for cc in range(CC):
                e.wait_ge(silu_done, cc + 1)
                e.activation(s_hi[:, cc, :], cv[:, cc, :], COPY).then_inc(s_hi_done, 1)
            for j in range(2 * NU + 1, 3 * NU):
                gate_evac(0, j)
            splits_mix(0, 2)
            splits_mix(0, 3)
            def mix_gates(c):
                load_branch_tiles(c)
                e.wait_ge(mix_done, c * NU)
                for j in range(3 * NU):
                    gate_evac(c, j)
                    if j % NU == NU - 1:
                        splits_mix(c, j // NU)

            with e.Fori(1, KC - 1) as c:
                mix_gates(c)
                splits_mix(c, 3)
            mix_gates(KC - 1)
            e.wait_ge(unit_done, UNIT_OUT - 3 * NU)
            def mix_hi_part(k0, k1, tt):
                t0, tw = THIRD[tt]
                e.activation(mix_hi[:, k0:k1, t0:t0 + tw], mixed[:, k0:k1, t0:t0 + tw], COPY).then_inc(mix_hi_done, 1)

            def mix_hi_last(tt):
                e.wait_ge(mix_done, NU * (KC - 1) + tt + 1)
                mix_hi_part(KC - 1, KC, tt)

            mix_hi_part(0, EARLY, 0)
            mix_hi_part(EARLY, KC - 1, 0)
            mix_hi_part(0, EARLY, 1)
            mix_hi_last(0)
            mix_hi_part(EARLY, KC - 1, 1)
            mix_hi_part(0, EARLY, 2)
            mix_hi_part(EARLY, KC - 1, 2)
            mix_hi_last(1)
            splits_mix(KC - 1, 3)
            mix_hi_last(2)

            raw_count[0] = RAW_MIX[0] + 32 * KC
            raw_count[1] = RAW_MIX[1] + 48 * KC

            def h2_copy(i):
                m, (t0, tw) = OUT_ORDER[i][0], THIRD[OUT_ORDER[i][1]]
                e.wait_ge(unit_done, UNIT_OUT + i + 1)
                e.activation(h2[:, m, t0:t0 + tw], psum[:, unit_bank(i), 0:tw], COPY).then_inc(act_freed, 1)

            def square_h(m):
                e.wait_ge(res_done, OUT_ORDER.index((m, NU - 1)) + 1)
                if m >= 2:
                    e.wait_ge(ssum_done, m - 1)
                e.activation((sq_sum if m == 0 else sq_h)[:, :], h2[:, m, :], ACT.Square).then_inc(sqh_done, 1)

            def square_tail(tt):
                t0, tw = THIRD[tt]
                for b_ in range(2):
                    e.wait_ge(res_done, TAIL + 2 * tt + b_ + 1)
                    if tt == 0 and b_ == 0:
                        e.wait_ge(ssum_done, KC - 3)
                    e.activation((sq_h, sq_last)[b_][:, t0:t0 + tw], h2[:, KC - 2 + b_, t0:t0 + tw], ACT.Square)\
                        .then_inc(sqh_done, 1)

            def std2(q):
                c0, cn = THIRD[q]
                e.wait_ge(ss2_done, q + 1)
                e.activation(rstd2[:, c0:c0 + cn], psum[:, PO, 0:cn], ACT.Sqrt, scale=1.0 / DM, bias=eps[:, :])\
                    .then_inc(std2_done, 1)

            def hn2_hi(q, ks):
                c0, cn = THIRD[q]
                for k in ks:
                    if k < 2:
                        e.wait_ge(scaled_done, 2 * q + k + 1)
                        src = scaled[k]
                    else:
                        p_ = (KC - 2) * q + k - 2
                        e.wait_ge(scaled_pool, p_ + 1)
                        src = scaled[2 + p_ % 3]
                    e.activation(hn_hi[:, k, c0:c0 + cn], src[:, 0:cn], COPY,
                                 scale=cols[:, C_N2 + k:C_N2 + k + 1]).then_inc(hn2_hi_done, 1)

            for i in range(2 * NU):
                if i == 2 * NU - 1:
                    split_hi(SLOT_OUT + 2)
                h2_copy(i)
            split_hi(SLOT_OUT + 3)
            for m in range(2, KC - 2):
                for tt in range(NU):
                    h2_copy(NU * m + tt)
                split_hi(SLOT_OUT + m + 2)
                if m == 2:
                    square_h(0)
                square_h(m - 1)
            h2_copy(TAIL)
            h2_copy(TAIL + 1)
            square_h(KC - 3)
            e.preload_act_table_set("sqrt_and_others")
            square_tail(0)
            h2_copy(TAIL + 2)
            std2(0)
            hn2_hi(0, range(0, 4))
            h2_copy(TAIL + 3)
            square_tail(1)
            split_hi(SLOT_OUT + KC)
            h2_copy(TAIL + 4)
            hn2_hi(0, range(4, KC))
            split_hi(SLOT_OUT + KC + 1)
            h2_copy(TAIL + 5)
            square_tail(2)
            for q in (1, 2):
                std2(q)
                hn2_hi(q, range(KC))
            e.preload_act_table_set("gelu_and_others")

            RAW_FFN = list(raw_count)

            def up_third(e6, which, tt, w2, bb):
                t0, tw = THIRD[tt]
                bank = psum[:, NU * which + tt, 0:tw]
                e.activation(up[which][:, FTAPS - 1 + t0:FTAPS - 1 + t0 + tw], bank, COPY)
                e.activation(acc[2 * (e6 % 2) + which][:, t0:t0 + tw], bank, ACT.Identity, scale=w2, bias=bb)\
                    .then_inc(act_freed, 1)

            def up_tile(ch, e6, which, u):
                j = ch + which * FC
                tile_n = 2 * ch + which
                if not isinstance(ch, int) or tile_n >= 2:
                    e.wait_ge(conv_done, tile_n - 1)
                if (not isinstance(ch, int) or ch >= 2) and which == 0:
                    e.wait_ge(g_done, ch - 1)
                w2 = cols[:, bass.ds(j + (C_FW + (FTAPS - 1) * 2 * FC), 1)]
                bb = cols[:, bass.ds(j + C_FB, 1)]
                for tt in range(NU):
                    e.wait_ge(unit_done, u + (tt + 1))
                    up_third(e6, which, tt, w2, bb)

            def gelu_and_hi(ch, e6):
                g = acc[2 * (e6 % 2)]
                e.wait_ge(conv_done, 2 * ch + 1)
                e.activation(g[:, :], g[:, :], ACT.Gelu_apprx_tanh).then_inc(gelu_done, 1)
                e.wait_ge(prod_done, ch + 1)
                e.activation(g_hi[:, e6 % RING, :], acc[2 * (e6 % 2) + 1][:, :], COPY).then_inc(g_hi_done, 1)

            def half_body(it6, half, chunks, total_it, last=False):
                u0 = total_it * (2 * HALF_UNITS) + (UNIT_FFN + 2 * NU + half * HALF_UNITS)
                r0 = [total_it * (16 * HALF_SLOTS) + (RAW_FFN[s] + 16 + half * 8 * HALF_SLOTS) for s in range(2)]
                count = 2 * chunks + KC // 2
                for i in range(chunks):
                    e6 = 3 * half + 1 + i
                    for which in range(2):
                        up_tile(it6 + e6, e6, which, u0 + NU * (2 * i + which))
                        s = 2 * i + which
                        split_hi_at(which, u0 + NU * (s + 1), r0[which] + 16 * (s // 2 + 1), 
                                    KC if s + 2 < 2 * chunks else 6)
                    gelu_and_hi(it6 + e6, e6)
                for m in range(KC // 2):
                    s = 2 * chunks + m
                    if last and m >= KC // 2 - 2:
                        break
                    tiles = 6 if s + 2 < count else KC
                    split_hi_at(s % 2, u0 + (2 * NU * chunks + 2 * NU * (m + 1)), r0[s % 2] + 16 * (s // 2 + 1), tiles)

            for u in range(2 * NU):
                which, j = u % 2, (u % 2) * FC
                if u == 2 * NU - 1:
                    split_hi_at(0, slot_left(SLOT_FFN), RAW_FFN[0] + 16)
                e.wait_ge(unit_done, UNIT_FFN + u + 1)
                at = j + C_FW + (FTAPS - 1) * 2 * FC
                up_third(0, which, u // 2, cols[:, at:at + 1], cols[:, C_FB + j:C_FB + j + 1])
            split_hi_at(1, slot_left(SLOT_FFN + 1), RAW_FFN[1] + 16)
            gelu_and_hi(0, 0)
            with e.Fori(0, FC // 6 - 1) as it:
                for half in range(2):
                    half_body(it * 6, half, 3, it)
            it = FC // 6 - 1
            half_body(it * 6, 0, 3, it)
            half_body(it * 6, 1, 2, it, last=True)

            e.preload_act_table_set("sqrt_and_others")
            def std_out(i):
                e.wait_ge(mso_done, i + 1)
                e.activation(stat[:, NT + i:NT + i + 1], stat[:, NT + i:NT + i + 1], ACT.Sqrt).then_inc(stdo_done, 1)

            for i in range(SEQ // P):
                e.wait_ge(ht_done, i + 1)
                if i >= 2:
                    e.wait_ge(sso_done, i - 1)
                e.activation(sq_out[i % 2][:, :].rearrange("p (a n) -> p a n", a=2), psum[:, 2 * (i % 4):2 * (i % 4) + 2, :],
                             ACT.Square, accum_out=stat[:, i:i + 1]).then_inc(sso_done, 1)
                if i >= 1:
                    std_out(i - 1)
            std_out(SEQ // P - 1)

        @block.vector
        def _(e):
            e.wait_ge(masks32_set, 3)
            e.tensor_copy(neg_tri[:, :], mask32[:, 0, :]).then_inc(masks_set, 1)
            e.tensor_copy(neg_rest[:, :], mask32[:, 1, :]).then_inc(masks_set, 1)

            def norm_group(g):
                i0, ni = GROUPS[g]
                s_in, s_out = stat[:, i0:i0 + ni], stat[:, NT + i0:NT + i0 + ni]
                e.wait_ge(x_ss, i0 + ni)
                e.tensor_scalar(s_out, s_in, 1.0 / DM, EPS, ALU.mult, ALU.add).then_inc(x_ms, 1)
                e.wait_ge(x_std, g + 1)
                e.reciprocal(s_out, s_out).then_inc(x_rstd, 1)
                e.wait_ge(x_rstd, g + 1)
                for i in range(i0, i0 + ni):
                    r = P if i < NT - 1 else REST
                    e.tensor_scalar(xn[0:r, i, :], xn[0:r, i, :], stat[0:r, NT + i:NT + i + 1], None, ALU.mult)\
                        .then_inc(xn_done, 1)

            def hn_lo_group(g):
                c0, cn = THIRD[g]
                for k in range(KC):
                    n = g * KC + k
                    e.wait_ge(hn_hi_done, n + 1)
                    e.scalar_tensor_tensor(out=hn_lo[:, k, c0:c0 + cn], in0=psum[:, 3 + n % 4, 0:cn],
                                           scalar=cols[:, C_N1 + k:C_N1 + k + 1],
                                           in1=hn_hi[:, k, c0:c0 + cn].bitcast(f32),
                                           op0=ALU.mult, op1=ALU.subtract).then_inc(hn_done, 1)

            e.wait_ge(cols_t, 3)
            e.tensor_copy(cols[:, :], psum[:, PO, 0:NCOL]).then_inc(cols_set, 1)
            norm_group(0)
            e.wait_ge(cols_set, 1)
            hn_lo_group(0)
            norm_group(1)
            hn_lo_group(1)
            norm_group(2)

            def glu_third(c, tt):
                t0, tw = THIRD[tt]
                n = NU * c + tt
                e.wait_ge(sig_done, n + 1)
                e.tensor_tensor(glu[:, c, TAPS - 1 + t0:TAPS - 1 + t0 + tw], psum[:, unit_bank(2 * n), 0:tw],
                                sig[n % 2][:, 0:tw], ALU.mult).then_inc(dve_freed, 2)

            def conv_tap(i):
                c, tap, half = i // (2 * TAPS), i // 2 % TAPS, i % 2
                ts = slice(half * T // 2, (half + 1) * T // 2)
                w = cols[:, C_CW + tap * CC + c:C_CW + tap * CC + c + 1]
                src = glu[:, c, tap + half * T // 2:tap + (half + 1) * T // 2]
                if tap == 0:
                    e.wait_ge(dve_freed, 2 * NU * (c + 1))
                    if c == 0:
                        e.wait_ge(glu_pad_set, 1)
                    e.tensor_scalar(cv[:, c, ts], src, w, cols[:, C_CB + c:C_CB + c + 1], ALU.mult, ALU.add)\
                        .then_inc(conv_chain, 1)
                else:
                    e.wait_ge(conv_chain, i - 1)
                    e.scalar_tensor_tensor(out=cv[:, c, ts], in0=src, scalar=w, in1=cv[:, c, ts],
                                           op0=ALU.mult, op1=ALU.add).then_inc(conv_chain, 1)

            taps = [0]

            def conv_taps(n):
                until = min(taps[0] + n, 2 * TAPS * CC)
                for i in range(taps[0], until):
                    conv_tap(i)
                taps[0] = until

            glu_third(0, 0)
            hn_lo_group(2)
            for tt in range(1, NU):
                glu_third(0, tt)
            for c in range(1, CC):
                for tt in range(NU):
                    conv_taps(10)
                    glu_third(c, tt)
            hi_seen = [0]

            def qk_lo(u, dst, hi, tt, scale):
                t0, tw = THIRD[tt]
                hi_seen[0] += 1
                e.wait_ge(evac_hi, hi_seen[0])
                e.scalar_tensor_tensor(out=dst[:, t0:t0 + tw], in0=psum[:, unit_bank(u), 0:tw], scalar=scale,
                                       in1=hi[:, t0:t0 + tw].bitcast(f32), op0=ALU.mult, op1=ALU.subtract)\
                    .then_inc(dve_freed, 1)

            def copy_unit(u, dst):
                e.wait_ge(unit_done, u + 1)
                e.tensor_copy(dst, psum[:, unit_bank(u), 0:dst.shape[-1]]).then_inc(dve_freed, 1)

            def softplus(t):
                e.wait_ge(log_done, t + 1)
                if t >= 1:
                    e.wait_ge(sp_split, t)
                e.scalar_tensor_tensor(out=sp[:, :], in0=zs[t % 3][:, :], scalar=0.0, in1=soft[t % 2][:, :],
                                       op0=ALU.max, op1=ALU.add).then_inc(sp_done, 1)

            def softplus_split(t):
                e.wait_ge(sp_done, t + 1)
                e.tensor_copy(sp_hi[t % 2][:, :], sp[:, :]).then_inc(sp_hi_done, 1)
                e.wait_ge(sp_hi_done, t + 1)
                e.tensor_tensor(sp_lo[t % 2][:, :], sp[:, :], sp_hi[t % 2][:, :].bitcast(f32), ALU.subtract)\
                    .then_inc(sp_split, 1)

            for j in range(3):
                for tt, (t0, tw) in enumerate(THIRD):
                    u = UNIT_Q0 + NU * j + tt
                    if j == 0:
                        copy_unit(u, vt[:, t0:t0 + tw])
                    else:
                        qk_lo(u, (k_lo, q_lo)[j - 1][0], (k_hi, q_hi)[j - 1][0], tt, (1.0, SCALE)[j - 1])
                    if j < 2 or tt == 0:
                        conv_taps(5)
            softplus(0)
            softplus_split(0)

            def v_lo_group(h, g):
                u = unit_att(h) + g
                i0, ni = VGROUPS[g]
                hi_seen[0] += 1
                e.wait_ge(evac_hi, hi_seen[0])
                e.tensor_tensor(v_lo[:, i0:i0 + ni, :],
                                psum[:, unit_bank(u), 0:ni * P].rearrange("p (n d) -> p n d", d=DH),
                                v_hi[:, i0:i0 + ni, :].bitcast(f32), ALU.subtract).then_inc(dve_freed, 1)

            v_lo_group(0, 0)
            v_lo_group(0, 1)
            for h in range(HEADS):
                for idx in range(NS):
                    t = h * NS + idx
                    e.wait_ge(u_done, t + 1)
                    if t >= 2:
                        e.wait_ge(a_split, t - 1)
                    e.tensor_tensor(att_w[t % 2][:, :], psum[:, PU[(HEADS * h + TILES[idx][0]) % 2], 0:QW],
                                    zs[t % 3][:, :], ALU.add).then_inc(logit_done, 1)
                    if idx == 1:
                        v_lo_group(h, 2)
                    if t + 1 < STEPS:
                        softplus(t + 1)
                        softplus_split(t + 1)
                    for f in fill_ended(h, idx):
                        u = unit_att(h) + NU + f
                        t0, tw = THIRD[f % NU]
                        if h == HEADS - 1:
                            copy_unit(u, pool_in[:, f // NU, LEFT + t0:LEFT + t0 + tw])
                        elif f < NU:
                            copy_unit(u, vt[:, t0:t0 + tw])
                        else:
                            p_, j = (h + 1) % 2, f // NU - 1
                            qk_lo(u, (k_lo, q_lo)[j][p_], (k_hi, q_hi)[j][p_], f % NU, (1.0, SCALE)[j])
                    if h < HEADS - 1 and idx >= NS - 2:
                        v_lo_group(h + 1, idx - (NS - 2))
                    conv_taps(1)
                    e.wait_ge(a_done, t + 1)
                    if t >= 2:
                        e.wait_ge(o_mm, t - 1)
                    e.tensor_copy(a_hi[t % 2][:, :], att_w[t % 2][:, :]).then_inc(a_hi_done, 1)
                    if t >= 1 and LAST[(t - 1) % NS]:
                        hh, i = (t - 1) // NS, TILES[(t - 1) % NS][0]
                        n_o = hh * (T // QW) + i
                        e.wait_ge(o_hi_done, n_o + 1)
                        e.tensor_tensor(att_lo[:, hh, QW * i:QW * (i + 1)], psum[:, PO, 0:QW],
                                        att_hi[:, hh, QW * i:QW * (i + 1)].bitcast(f32), ALU.subtract)\
                            .then_inc(o_evac, 1)
            n_o = HEADS * (T // QW)
            e.wait_ge(o_hi_done, n_o)
            e.tensor_tensor(att_lo[:, HEADS - 1, T - QW:T], psum[:, PO, 0:QW],
                            att_hi[:, HEADS - 1, T - QW:T].bitcast(f32), ALU.subtract).then_inc(o_evac, 1)

            for tt, (t0, tw) in enumerate(THIRD):
                e.wait_ge(mu_done, tt + 1)
                for cc in range(CC):
                    e.scalar_tensor_tensor(out=cv[:, cc, t0:t0 + tw], in0=psum[:, (PZ[0], PZ[1], PU[0])[tt], 0:tw],
                                           scalar=-1.0 / CONV, in1=cv[:, cc, t0:t0 + tw],
                                           op0=ALU.mult, op1=ALU.add).then_inc(xc_done, 1)
            chained = [0]

            def link(ins):
                ins.then_inc(win_chain, 1)
                chained[0] += 1
                e.wait_ge(win_chain, chained[0])

            link(e.memset(win[0][:, 0:LEFT], 0.0))
            link(e.memset(win[1][:, 0:LEFT], 0.0))
            e.wait_ge(cnt_set, 1)
            for g in range(GRPS):
                part = inv_cnt[GC * (g % 2):GC * (g % 2) + GC, g // 2, :]
                link(e.tensor_scalar(part, part, float(WINDOWS[g]), None, ALU.min))
            link(e.reciprocal(inv_cnt[:, :, :], inv_cnt[:, :, :]))
            e.wait_ge(pool_pad_set, 1)
            for c in range(CC):
                lo_w, hi_w = WINDOWS[2 * c], WINDOWS[2 * c + 1]
                cur, w_ = pool_in[:, c, :], 1
                flip = 0
                while w_ < lo_w:
                    dst = win[flip]
                    link(e.tensor_tensor(dst[:, LEFT:LEFT + T], cur[:, LEFT:LEFT + T], cur[:, LEFT - w_:LEFT - w_ + T],
                                         ALU.add))
                    cur, flip, w_ = dst, 1 - flip, 2 * w_
                dst = win[flip]
                link(e.tensor_tensor(dst[GC:P, LEFT:LEFT + T], cur[GC:P, LEFT:LEFT + T],
                                     cur[GC:P, LEFT - w_:LEFT - w_ + T], ALU.add))
                link(e.tensor_copy(dst[0:GC, LEFT:LEFT + T], cur[0:GC, LEFT:LEFT + T]))
                link(e.tensor_tensor(dst[:, LEFT:2 * LEFT], dst[:, LEFT:2 * LEFT], inv_cnt[:, c, :], ALU.mult))
                link(e.tensor_tensor(dst[:, LEFT:2 * LEFT], dst[:, LEFT:2 * LEFT], pool_in[:, c, LEFT:2 * LEFT],
                                     ALU.subtract))
                link(e.scalar_tensor_tensor(out=dst[:, 2 * LEFT:LEFT + T], in0=dst[:, 2 * LEFT:LEFT + T],
                                            scalar=inv_cnt[:, c, LEFT - 1:LEFT], in1=pool_in[:, c, 2 * LEFT:LEFT + T],
                                            op0=ALU.mult, op1=ALU.subtract))
                link(e.tensor_copy(pooled_hi[:, c, :], dst[:, LEFT:LEFT + T]))
                ins = e.tensor_tensor(pooled_lo[:, c, :], dst[:, LEFT:LEFT + T], pooled_hi[:, c, :].bitcast(f32),
                                      ALU.subtract)
                link(ins)
            for tt, (t0, tw) in enumerate(THIRD):
                e.wait_ge(stdc_done, tt + 1)
                e.reciprocal(std_cv[:, t0:t0 + tw], std_cv[:, t0:t0 + tw]).then_inc(rstdc_done, 1)
            e.wait_ge(rstdc_done, NU)
            for cc in range(CC):
                e.tensor_tensor(cv[:, cc, :], cv[:, cc, :], std_cv[:, :], ALU.mult).then_inc(yc_done, 1)
            for cc in range(CC):
                e.wait_ge(s_hi_done, cc + 1)
                e.tensor_tensor(s_lo[:, cc, :], cv[:, cc, :], s_hi[:, cc, :].bitcast(f32), ALU.subtract)\
                    .then_inc(s_ready, 1)

            def mix_chunk(c, thirds=range(NU)):
                bc = cols[:, bass.ds(c + C_BC, 1)]
                ps = cols[:, bass.ds(c + C_PS, 1)]
                for tt in thirds:
                    t0, tw = THIRD[tt]
                    g0, g1, g2 = (gate[:, br, t0:t0 + tw] for br in range(3))
                    u = c * (6 * NU) + (UNIT_MIX + 3 * NU + 3 * tt)
                    if tt == 0:
                        e.wait_ge(act_freed, c * (3 * NU) + 3 * NU)
                    e.wait_ge(unit_done, u + 1)
                    e.tensor_tensor(g2, psum[:, 0, 0:tw], g2, ALU.mult).then_inc(dve_freed, 1)
                    e.wait_ge(unit_done, u + 2)
                    e.scalar_tensor_tensor(out=g1, in0=psum[:, 1, 0:tw], scalar=ps, in1=g1,
                                           op0=ALU.mult, op1=ALU.mult).then_inc(dve_freed, 1)
                    e.wait_ge(dve_freed, c * (3 * NU) + (DVE_MIX + 3 * tt + 2))
                    e.tensor_tensor(g1, g1, g2, ALU.add).then_inc(mix_chain, 1)
                    e.wait_ge(unit_done, u + 3)
                    e.scalar_tensor_tensor(out=g0, in0=psum[:, 2, 0:tw], scalar=bc, in1=g0,
                                           op0=ALU.add, op1=ALU.mult).then_inc(dve_freed, 1)
                    e.wait_ge(dve_freed, c * (3 * NU) + (DVE_MIX + 3 * tt + 3))
                    e.wait_ge(mix_chain, c * NU + (tt + 1))
                    e.tensor_tensor(mixed[:, bass.ds(c, 1), t0:t0 + tw].rearrange("p a n -> p (a n)"), g0, g1, ALU.add)\
                        .then_inc(mix_done, 1)

            with e.Fori(0, KC - 1) as c:
                mix_chunk(c)

            def mix_lo_part(k0, k1, tt, hi_count):
                t0, tw = THIRD[tt]
                e.wait_ge(mix_hi_done, hi_count)
                e.tensor_tensor(mix_lo[:, k0:k1, t0:t0 + tw], mixed[:, k0:k1, t0:t0 + tw],
                                mix_hi[:, k0:k1, t0:t0 + tw].bitcast(f32), ALU.subtract).then_inc(mix_split, 1)

            mix_chunk(KC - 1, [0])
            mix_lo_part(EARLY, KC - 1, 0, MIX_HI[0][1])
            mix_chunk(KC - 1, [1])
            mix_lo_part(KC - 1, KC, 0, MIX_HI[0][2])
            mix_chunk(KC - 1, [2])
            for tt in (1, 2):
                mix_lo_part(EARLY, KC - 1, tt, MIX_HI[tt][1])
                mix_lo_part(KC - 1, KC, tt, MIX_HI[tt][2])

            def residual(i):
                m, (t0, tw) = OUT_ORDER[i][0], THIRD[OUT_ORDER[i][1]]
                e.wait_ge(xt2_done, i + 1)
                e.wait_ge(act_freed, ACT_OUT + i + 1)
                e.tensor_tensor(h2[:, m, t0:t0 + tw], h2[:, m, t0:t0 + tw], psum[:, PZ[0] + i % 5, 0:tw], ALU.add)\
                    .then_inc(res_done, 1)

            def sum_tail(tt):
                t0, tw = THIRD[tt]
                for b_ in range(2):
                    e.wait_ge(sqh_done, KC - 2 + 2 * tt + b_ + 1)
                    if b_ == 1:
                        e.wait_ge(ssum_done, KC - 3 + 2 * tt + 1)
                    elif tt == 0:
                        e.wait_ge(ssum_done, KC - 3)
                    e.tensor_tensor(sq_sum[:, t0:t0 + tw], sq_sum[:, t0:t0 + tw], (sq_h, sq_last)[b_][:, t0:t0 + tw],
                                    ALU.add).then_inc(ssum_done, 1)

            def rstd2_of(q):
                c0, cn = THIRD[q]
                e.wait_ge(std2_done, q + 1)
                e.reciprocal(rstd2[:, c0:c0 + cn], rstd2[:, c0:c0 + cn]).then_inc(rstd2_done, 1)
                e.wait_ge(rstd2_done, q + 1)
                for k in range(2):
                    if q >= 1:
                        e.wait_ge(hn2_done, KC * (q - 1) + k + 1)
                    e.tensor_tensor(scaled[k][:, 0:cn], h2[:, k, c0:c0 + cn], rstd2[:, c0:c0 + cn], ALU.mult)\
                        .then_inc(scaled_done, 1)

            def hn2_lo(q, ks):
                c0, cn = THIRD[q]
                for k in ks:
                    src = scaled[k] if k < 2 else scaled[2 + ((KC - 2) * q + k - 2) % 3]
                    e.wait_ge(hn2_hi_done, KC * q + k + 1)
                    e.scalar_tensor_tensor(out=hn_lo[:, k, c0:c0 + cn], in0=src[:, 0:cn],
                                           scalar=cols[:, C_N2 + k:C_N2 + k + 1],
                                           in1=hn_hi[:, k, c0:c0 + cn].bitcast(f32),
                                           op0=ALU.mult, op1=ALU.subtract).then_inc(hn2_done, 1)

            for m in range(KC - 2):
                for j in range(NU):
                    residual(NU * m + j)
                if m >= 2:
                    mm = m - 1
                    e.wait_ge(sqh_done, mm + 1)
                    if mm >= 2:
                        e.wait_ge(ssum_done, mm - 1)
                    e.tensor_tensor(sq_sum[:, :], sq_sum[:, :], sq_h[:, :], ALU.add).then_inc(ssum_done, 1)
            residual(TAIL)
            residual(TAIL + 1)
            e.wait_ge(sqh_done, KC - 2)
            e.wait_ge(ssum_done, KC - 4)
            e.tensor_tensor(sq_sum[:, :], sq_sum[:, :], sq_h[:, :], ALU.add).then_inc(ssum_done, 1)
            sum_tail(0)
            residual(TAIL + 2)
            rstd2_of(0)
            hn2_lo(0, range(0, 4))
            residual(TAIL + 3)
            sum_tail(1)
            hn2_lo(0, range(4, KC))
            residual(TAIL + 4)
            residual(TAIL + 5)
            sum_tail(2)
            for q in (1, 2):
                rstd2_of(q)
                hn2_lo(q, range(KC))

            for s in range(2):
                e.memset(up[s][:, 0:FTAPS - 1], 0.0).then_inc(up_pads_set, 1)
            e.wait_ge(up_pads_set, 2)

            def conv3(ch, e6, which, evacuated=None):
                j = ch + which * FC
                tile_n = 2 * ch + which
                a_ = acc[2 * (e6 % 2) + which]
                e.wait_ge(act_freed, evacuated or tile_n * NU + (ACT_FFN + NU))
                w1 = cols[:, bass.ds(j + (C_FW + 2 * FC), 1)]
                w0 = cols[:, bass.ds(j + C_FW, 1)]
                e.scalar_tensor_tensor(out=a_[:, :], in0=up[which][:, 1:1 + T], scalar=w1, in1=a_[:, :],
                                       op0=ALU.mult, op1=ALU.add).then_inc(tap_chain, 1)
                e.wait_ge(tap_chain, tile_n + 1)
                e.scalar_tensor_tensor(out=a_[:, :], in0=up[which][:, 0:T], scalar=w0, in1=a_[:, :],
                                       op0=ALU.mult, op1=ALU.add).then_inc(conv_done, 1)

            def product(ch, e6):
                g, v = acc[2 * (e6 % 2)], acc[2 * (e6 % 2) + 1]
                e.wait_ge(gelu_done, ch + 1)
                e.wait_ge(conv_done, 2 * ch + 2)
                e.tensor_tensor(v[:, :], g[:, :], v[:, :], ALU.mult).then_inc(prod_done, 1)

            def product_lo(ch, e6):
                v = acc[2 * (e6 % 2) + 1]
                e.wait_ge(g_hi_done, ch + 1)
                e.tensor_tensor(g_lo[:, e6 % RING, :], v[:, :], g_hi[:, e6 % RING, :].bitcast(f32), ALU.subtract)\
                    .then_inc(g_done, 1)

            def down(u, m):
                for tt, (t0, tw) in enumerate(THIRD):
                    e.wait_ge(unit_done, u + (NU * m + tt + 1))
                    e.tensor_tensor(h2[:, m, t0:t0 + tw], h2[:, m, t0:t0 + tw], psum[:, NU * (m % 2) + tt, 0:tw],
                                    ALU.add).then_inc(dve_freed, 1)

            def half_body(it, half, chunks):
                u = it * (2 * HALF_UNITS) + (UNIT_FFN + 2 * NU + half * HALF_UNITS + 2 * NU * chunks)
                for i in range(chunks):
                    e6 = 3 * half + 1 + i
                    ch = it * 6 + e6
                    conv3(ch, e6, 0)
                    conv3(ch, e6, 1)
                    spread = i == chunks - 1 and chunks == 3
                    if spread:
                        down(u, 0)
                    product(ch, e6)
                    if spread:
                        down(u, 1)
                    product_lo(ch, e6)
                for m in range(2 if chunks == 3 else 0, KC):
                    down(u, m)

            conv3(0, 0, 0, ACT_FFN + 2 * NU - 1)
            conv3(0, 0, 1, ACT_FFN + 2 * NU)
            product(0, 0)
            product_lo(0, 0)
            with e.Fori(0, FC // 6 - 1) as it:
                half_body(it, 0, 3)
                half_body(it, 1, 3)
            half_body(FC // 6 - 1, 0, 3)
            half_body(FC // 6 - 1, 1, 2)

            def finish(i):
                e.wait_ge(stdo_done, i + 1)
                e.reciprocal(stat[:, NT + i:NT + i + 1], stat[:, NT + i:NT + i + 1]).then_inc(rstdo_done, 1)
                e.wait_ge(rstdo_done, i + 1)
                if i == 0:
                    e.wait_ge(final_g_in, 16)
                if i >= 3:
                    e.wait_ge(stored[i % 3], 16 * (i // 3))
                e.scalar_tensor_tensor(out=y_out[i % 3][:, :].rearrange("p (a n) -> p a n", a=2),
                                       in0=psum[:, 2 * (i % 4):2 * (i % 4) + 2, :], scalar=stat[:, NT + i:NT + i + 1],
                                       in1=final_g[:, :].rearrange("p (a n) -> p a n", a=2),
                                       op0=ALU.mult, op1=ALU.mult).then_inc(y_done, 1)

            for i in range(SEQ // P):
                e.wait_ge(sso_done, i + 1)
                e.tensor_scalar(stat[:, NT + i:NT + i + 1], stat[:, i:i + 1], 1.0 / DM, EPS, ALU.mult, ALU.add)\
                    .then_inc(mso_done, 1)
                if i >= 1:
                    finish(i - 1)
            finish(SEQ // P - 1)

        @block.tensor
        def _(e):
            def passes(dst, w_pair, r_pair, start, stop):
                (a_h, a_l), (r_h, r_l) = w_pair, r_pair
                e.matmul(dst, a_h, r_h, start=start, stop=False)
                e.matmul(dst, a_h, r_l, start=False, stop=False)
                return e.matmul(dst, a_l, r_h, start=False, stop=stop)

            def tiles(s, ks, rhs, tt, bank, j0=0, ks_rhs=None):
                t0, tw = THIRD[tt]
                for k in ks:
                    last = passes(psum[:, bank, 0:tw], (wh[s][:, k, :], wl[s][:, k, :]),
                                  (rhs[0][:, k, t0:t0 + tw], rhs[1][:, k, t0:t0 + tw]),
                                  start=k == 0, stop=k == KC - 1)
                return last

            hn = (hn_hi, hn_lo)

            def xn_transposes(g, part):
                i0, ni = GROUPS[g]
                e.wait_ge(xn_done, i0 + ni)
                for k in range(part * KC // 2, (part + 1) * KC // 2):
                    n = g * KC + k
                    if n >= 4:
                        e.wait_ge(hn_done, n - 3)
                    for i in range(i0, i0 + ni):
                        r = P if i < NT - 1 else REST
                        last = e.transpose(psum[:, 3 + n % 4, (i - i0) * P:(i - i0) * P + r],
                                           xn[0:r, i, k * P:(k + 1) * P], ident[0:r, 0:r])
                    last.then_inc(xt_done, 1)

            def conv_unit(c, tt, s):
                if c == 0 and s == 0:
                    e.wait_ge(hn_done, KC * (tt + 1))
                u = 2 * NU * c + 2 * tt + s
                if tt == 0:
                    e.wait_ge(w_lo_done, 2 * c + s + 1)
                if u >= NU:
                    e.wait_ge(dve_freed, u - NU + 1)
                last = tiles(s, range(KC), hn, tt, unit_bank(u))
                last.then_inc(unit_done, 1)

            e.wait_ge(ident_set, 5)
            e.wait_ge(params_in, 16 * 11)
            at = 0
            for slot, count in ((0, C_FW), (1, P), (2, NCOL - C_FW - P)):
                e.transpose(psum[:, PO, at:at + count], rows[0:count, slot, :], ident[0:count, 0:count])\
                    .then_inc(cols_t, 1)
                at += count
            xn_transposes(0, 0)
            xn_transposes(0, 1)
            for tt in range(NU):
                for s in range(2):
                    conv_unit(0, tt, s)
                    if tt < NU - 1:
                        xn_transposes(tt + 1, s)
            for c in range(1, CC):
                for tt in range(NU):
                    for s in range(2):
                        conv_unit(c, tt, s)

            def head0_unit(j, tt):
                u = UNIT_Q0 + NU * j + tt
                if tt == 0:
                    e.wait_ge(w_lo_done, SLOT_Q0 + j + 1)
                e.wait_ge(dve_freed, u - NU + 1)
                last = tiles((SLOT_Q0 + j) % 2, range(KC), hn, tt, unit_bank(u))
                last.then_inc(unit_done, 1)

            for j in range(2):
                for tt in range(NU):
                    head0_unit(j, tt)

            def scores(t):
                h, (i, n) = t // NS, TILES[t % NS]
                p_ = h % 2
                if t >= 2:
                    e.wait_ge(z_copied, t - 1)
                if t % NS == 0:
                    e.wait_ge(dve_freed, UNIT_Q0 + 2 * NU + 1 if h == 0 else unit_att(h))
                    e.wait_ge(kv_pads_set, 5)
                if t % NS == 1 and h >= 1:
                    e.wait_ge(dve_freed, unit_att(h))
                ks, qs = slice(n * P, (n + 1) * P), slice(i * QW, (i + 1) * QW)
                passes(psum[:, PZ[t % 2], 0:QW], (k_hi[p_][:, ks], k_lo[p_][:, ks]), (q_hi[p_][:, qs], q_lo[p_][:, qs]),
                       True, True).then_inc(z_done, 1)

            def weigh(t):
                i, n = TILES[t % NS]
                e.wait_ge(a_split, t + 1)
                if FIRST[t % NS]:
                    n_o = (t // NS) * (T // QW) + i
                    if n_o >= 1:
                        e.wait_ge(o_evac, n_o)
                if t % NS == 0:
                    e.wait_ge(dve_freed, unit_att(t // NS) + NU)
                passes(psum[:, PO, 0:QW], (v_hi[:, n, :], v_lo[:, n, :]), (a_hi[t % 2][:, :], a_lo[t % 2][:, :]),
                       FIRST[t % NS], LAST[t % NS]).then_inc(o_mm, 1)

            def v_transposes(h, g):
                u = unit_att(h) + g
                i0, ni = VGROUPS[g]
                e.wait_ge(dve_freed, u - NU + 1)
                for i in range(i0, i0 + ni):
                    last = e.transpose(psum[:, unit_bank(u), (i - i0) * P:(i - i0 + 1) * P], vt[:, i * P:(i + 1) * P],
                                       ident[:, :])
                last.then_inc(unit_done, 1)

            def filler(h, idx, part):
                n0, n1 = fill_bound(h, idx), fill_bound(h, idx + 1)
                cut = n0 + 2 if idx == 0 else n1
                for n in (range(n0, cut), range(cut, n1))[part]:
                    f, k = divmod(n, KC)
                    u, slot = unit_att(h) + NU + f, slot_att(h, f // NU)
                    if k == 0:
                        if f % NU == 0:
                            e.wait_ge(w_lo_done, slot + 1)
                        e.wait_ge(dve_freed, u - NU + 1)
                    last = tiles(slot % 2, [k], hn, f % NU, unit_bank(u))
                    if k == KC - 1:
                        last.then_inc(unit_done, 1)

            head0_unit(2, 0)
            head0_unit(2, 1)
            scores(0)
            head0_unit(2, 2)
            scores(1)
            v_transposes(0, 0)
            v_transposes(0, 1)
            e.wait_ge(masks_set, 2)
            for h in range(HEADS):
                for idx in range(NS):
                    t = h * NS + idx
                    bank = psum[:, PU[(HEADS * h + TILES[idx][0]) % 2], 0:QW]
                    e.wait_ge(sp_split, t + 1)
                    e.matmul(bank, neg_tri[:, :], sp_hi[t % 2][:, :], start=FIRST[idx], stop=False,
                             skip_group_check=True)
                    e.matmul(bank, neg_tri[:, :], sp_lo[t % 2][:, :], start=False, stop=True,
                             skip_group_check=True).then_inc(u_done, 1)
                    if t + 2 < STEPS:
                        scores(t + 2)
                    filler(h, idx, 0)
                    if not LAST[idx]:
                        e.wait_ge(logit_done, t + 1)
                        e.matmul(bank, neg_rest[:, :], sp_hi[t % 2][:, :], start=False, stop=False,
                                 skip_group_check=True)
                        e.matmul(bank, neg_rest[:, :], sp_lo[t % 2][:, :], start=False, stop=True,
                                 skip_group_check=True)
                    if t >= 1:
                        weigh(t - 1)
                    if idx == 0:
                        v_transposes(h, 2)
                        filler(h, idx, 1)
                    if h < HEADS - 1 and idx in (NS - 3, NS - 2):
                        v_transposes(h + 1, idx - (NS - 3))
            weigh(STEPS - 1)

            def freed_in_mix(c, j):
                if j < NU or j >= 4 * NU:
                    e.wait_ge(dve_freed, c * (3 * NU) + (DVE_MIX + (j - NU + 1 if j < NU else j - 4 * NU + 1)))
                else:
                    e.wait_ge(act_freed, c * (3 * NU) + (j - NU + 1))

            def gate_unit(c, br, tt):
                n = c * 4 + (SLOT_MIX + br)
                j = NU * br + tt
                if tt == 0:
                    e.wait_ge(w_lo_done, n + 1)
                freed_in_mix(c, j)
                last = tiles(br % 2, range(KC), hn, tt, unit_bank(j))
                last.then_inc(unit_done, 1)

            def branch_units(c, first):
                n = c * 4 + (SLOT_MIX + 3)
                e.wait_ge(w_lo_done, n + 1)
                for tt, (t0, tw) in enumerate(THIRD):
                    j = 3 * NU + 3 * tt
                    ts = slice(t0, t0 + tw)
                    freed_in_mix(c, j)
                    for k in range(HEADS):
                        last = passes(psum[:, 0, 0:tw], (wh[1][:, k, :], wl[1][:, k, :]),
                                      (att_hi[:, k, ts], att_lo[:, k, ts]), k == 0, k == HEADS - 1)
                    last.then_inc(unit_done, 1)
                    freed_in_mix(c, j + 1)
                    pc = first
                    last = passes(psum[:, 1, 0:tw], (wh[1][:, HEADS + CC, :], wl[1][:, HEADS + CC, :]),
                                  (pooled_hi[:, pc, ts], pooled_lo[:, pc, ts]), True, True)
                    last.then_inc(unit_done, 1)
                    freed_in_mix(c, j + 2)
                    if isinstance(c, int) and tt == 0:
                        e.wait_ge(s_ready, CC)
                    for k in range(CC):
                        last = passes(psum[:, 2, 0:tw], (wh[1][:, HEADS + k, :], wl[1][:, HEADS + k, :]),
                                      (s_hi[:, k, ts], s_lo[:, k, ts]), k == 0, k == CC - 1)
                    last.then_inc(unit_done, 1)

            e.wait_ge(conv_chain, 2 * TAPS * CC)
            for tt, (t0, tw) in enumerate(THIRD):
                for cc in range(CC):
                    last = e.matmul(psum[:, (PZ[0], PZ[1], PU[0])[tt], 0:tw], ones[:, :], cv[:, cc, t0:t0 + tw],
                                    start=cc == 0, stop=cc == CC - 1)
                last.then_inc(mu_done, 1)
            for tt, (t0, tw) in enumerate(THIRD):
                gate_unit(0, 0, tt)
                e.wait_ge(sqc_done, tt + 1)
                if tt == 1:
                    e.wait_ge(o_evac, HEADS * (T // QW))
                for cc in range(CC):
                    last = e.matmul(psum[:, (PU[1], PO, PZ[0])[tt], 0:tw], ones[:, :], sq_cv[:, cc, 0:tw],
                                    start=cc == 0, stop=cc == CC - 1)
                last.then_inc(var_done, 1)
            for br in (1, 2):
                for tt in range(NU):
                    gate_unit(0, br, tt)
            branch_units(0, 0)
            for pc in range(CC):
                with e.Fori(max(1, pc * KC // CC), (pc + 1) * KC // CC) as c:
                    for br in range(3):
                        for tt in range(NU):
                            gate_unit(c, br, tt)
                    branch_units(c, pc)

            def out_unit(i):
                m, tt = OUT_ORDER[i]
                if i < 2 * NU and m == 0:
                    e.wait_ge(mix_lo_early, tt + 1)
                    e.wait_ge(mix_split, 2 * tt + 2)
                if i < NU:
                    e.wait_ge(dve_freed, DVE_FFN - NU + i + 1)
                else:
                    e.wait_ge(act_freed, ACT_OUT + i - NU + 1)
                e.wait_ge(w_lo_done, SLOT_OUT + m + 1)
                last = tiles(m % 2, range(KC), (mix_hi, mix_lo), tt, unit_bank(i))
                last.then_inc(unit_done, 1)

            def x_transposes(i):
                m, (i0, ni) = OUT_ORDER[i][0], GROUPS[OUT_ORDER[i][1]]
                if i >= 5:
                    e.wait_ge(res_done, i - 4)
                for tile in range(i0, i0 + ni):
                    r, src = (P, x_again[:, tile, :]) if tile < NT - 1 else (REST, x_last[0:REST, :])
                    at = (tile - i0) * P
                    last = e.transpose(psum[:, PZ[0] + i % 5, at:at + r], src[:, m * P:(m + 1) * P], ident[0:r, 0:r])
                last.then_inc(xt2_done, 1)

            def sum_of_squares(q):
                c0, cn = THIRD[q]
                e.wait_ge(ssum_done, KC - 3 + 2 * q + 2)
                if q >= 1:
                    e.wait_ge(std2_done, q)
                e.matmul(psum[:, PO, 0:cn], ones[:, :], sq_sum[:, c0:c0 + cn], start=True, stop=True)\
                    .then_inc(ss2_done, 1)

            for i in range(2 * NU):
                out_unit(i)
            e.wait_ge(x_again_in, 64)
            for i in range(2 * NU):
                x_transposes(i)
            for i in range(2 * NU, NU * KC):
                out_unit(i)
                x_transposes(i)
                if i == TAIL + 2:
                    sum_of_squares(0)
                if i == TAIL + 4:
                    sum_of_squares(1)

            def up_tile(n, s, ups, downs):
                e.wait_ge(w_lo_done, n + s + 1)
                for tt in range(NU):
                    if s < 2:
                        e.wait_ge(dve_freed, downs + (NU * (s - 2) + tt + 1))
                    else:
                        e.wait_ge(act_freed, ups + (NU * (s - 2) + tt + 1))
                    last = tiles(s % 2, range(KC), hn, tt, NU * (s % 2) + tt)
                    last.then_inc(unit_done, 1)

            def half_body(it, half, chunks):
                n0 = it * (2 * HALF_SLOTS) + (SLOT_FFN + 2 + half * HALF_SLOTS)
                ups = it * (2 * HALF_UP) + (ACT_FFN + 2 * NU + half * HALF_UP)
                dns = it * (2 * HALF_DOWN) + (DVE_FFN + half * HALF_DOWN)
                for s in range(2 * chunks):
                    up_tile(n0, s, ups, dns)
                def down_pass(m, tt, ks):
                    s, (t0, tw) = (m // 2) % 2, THIRD[tt]
                    for k in ks:
                        r = (3 * half + k) % RING
                        last = passes(psum[:, NU * (m % 2) + tt, 0:tw],
                                      (wh[s][:, 2 * k + m % 2, :], wl[s][:, 2 * k + m % 2, :]),
                                      (g_hi[:, r, t0:t0 + tw], g_lo[:, r, t0:t0 + tw]), k == 0, k == 2)
                    return last

                if chunks == 2:
                    e.wait_ge(g_done, FC - 1)
                    e.wait_ge(w_lo_done, n0 + (2 * chunks + 1))
                    for m in range(2):
                        for tt in range(NU):
                            e.wait_ge(act_freed, ups + (NU * (2 * chunks - 2 + m) + tt + 1))
                            down_pass(m, tt, range(2))
                e.wait_ge(g_done, it * 6 + (3 * half + 3))
                if chunks == 2:
                    for m in range(2):
                        for tt in range(NU):
                            down_pass(m, tt, [2]).then_inc(unit_done, 1)
                for m in range(2 if chunks == 2 else 0, KC):
                    if m % 2 == 0:
                        e.wait_ge(w_lo_done, n0 + (2 * chunks + m // 2 + 1))
                    for tt, (t0, tw) in enumerate(THIRD):
                        if m < 2:
                            e.wait_ge(act_freed, ups + (NU * (2 * chunks - 2 + m) + tt + 1))
                        else:
                            e.wait_ge(dve_freed, dns + (NU * (m - 2) + tt + 1))
                        down_pass(m, tt, range(3)).then_inc(unit_done, 1)

            for u in range(2 * NU):
                which, tt = u % 2, u // 2
                if tt == 0:
                    e.wait_ge(w_lo_done, SLOT_FFN + which + 1)
                if which == 0:
                    e.wait_ge(hn2_done, KC * (tt + 1))
                    e.wait_ge(act_freed, ACT_FFN - NU + tt + 1)
                last = tiles(which, range(KC), hn, tt, NU * which + tt)
                last.then_inc(unit_done, 1)
                if u == 0:
                    sum_of_squares(2)
            with e.Fori(0, FC // 6 - 1) as it:
                half_body(it, 0, 3)
                half_body(it, 1, 3)
            half_body(FC // 6 - 1, 0, 3)
            half_body(FC // 6 - 1, 1, 2)

            e.wait_ge(dve_freed, DVE_FFN + HALF_DOWN * (FC // 3))
            for i in range(SEQ // P):
                if i >= 4:
                    e.wait_ge(y_done, i - 3)
                for k in range(KC):
                    last = e.transpose(psum[:, 2 * (i % 4) + k // 4, (k % 4) * P:(k % 4 + 1) * P],
                                       h2[:, k, NMETA + i * P:NMETA + (i + 1) * P], ident[:, :])
                last.then_inc(ht_done, 1)


_INS = ["x", "meta", "norm1", "w_in", "conv_dw_w", "conv_dw_b", "conv_ln_g", "conv_ln_b", "w_conv_out", "b_conv_out",
        "w_pool_grp", "pool_scale", "w_attn_out", "w_o", "norm2", "w_up", "ffn_dw_w", "ffn_dw_b", "w_down",
        "final_norm"]


def kernel(**inputs):
    import numpy as _np
    import concourse.bacc as _bacc
    from concourse import mybir as _mybir
    from concourse.bass_utils import run_bass_kernel_spmd as _run

    nc = _bacc.Bacc("TRN2", target_bir_lowering=False, num_devices=1)
    arrays, args = {}, []
    for name in _INS:
        a = _np.ascontiguousarray(inputs[name])
        arrays[f"in_{name}_dram"] = a
        args.append(nc.dram_tensor(f"in_{name}_dram", a.shape, _mybir.dt.from_np(a.dtype), kind="ExternalInput").ap())
    shape = arrays["in_x_dram"].shape
    out = nc.dram_tensor("out_dram", shape, _mybir.dt.float32, kind="ExternalOutput").ap()
    hybrid_trunk_kernel(nc, *args, out)
    r = _run(nc, [arrays], core_ids=[0])
    return r.results[0]["out_dram"]
```
